# Optimizing a Trainium2 kernel written in Bass

```python
import jax
import jax.numpy as jnp
from jax import lax
import numpy as np
import math
import jax, jax.numpy as jnp

D_MODEL = 1024
BATCH = 1
SEQ = 256
DEPTH = 1

MEM_LEN = 256
EPS = 1e-6
FOX_HEADS = 8
FOX_HEAD_DIM = 64
FOX_WIDTH = FOX_HEADS * FOX_HEAD_DIM
FOX_BLOCK = 128
FORGET_BIAS_INIT = 3.0
GLA_HEADS = 4
GLA_KEY_DIM = 64
GLA_VAL_DIM = 128
GLA_QK_WIDTH = GLA_HEADS * GLA_KEY_DIM
GLA_V_WIDTH = GLA_HEADS * GLA_VAL_DIM
GLA_GATE_RANK = 16
GLA_GATE_TAU = 16.0
GLA_CHUNK = 64
MIX_WIDTH = FOX_WIDTH + GLA_V_WIDTH
IN_WIDTHS = (FOX_WIDTH, FOX_WIDTH, FOX_WIDTH, FOX_HEADS, GLA_QK_WIDTH, GLA_QK_WIDTH, GLA_V_WIDTH, GLA_V_WIDTH, GLA_GATE_RANK)
IN_PROJ_WIDTH = 3096
X_HEADS = 4
X_HEAD_DIM = 128
X_WIDTH = X_HEADS * X_HEAD_DIM
N_GROUPS = 4
EXPERTS_PER_GROUP = 4
N_EXPERTS = N_GROUPS * EXPERTS_PER_GROUP
TOP_K = 2
D_EXPERT = 512
MOE_BLOCK = 128
RESID_SCALE = 0.5


def rms_norm(x, gain):
    xf = x.astype(jnp.float32)
    y = xf * lax.rsqrt(jnp.mean(xf * xf, axis=-1, keepdims=True) + EPS)
    return (y * gain.astype(jnp.float32)).astype(x.dtype)

def forgetting_attention(q, k, v, f_logit):
    B, S, H, d = q.shape
    q = q.transpose(0, 2, 1, 3)
    k = k.transpose(0, 2, 1, 3)
    v = v.transpose(0, 2, 1, 3)
    log_f = jax.nn.log_sigmoid(f_logit.astype(jnp.float32)).transpose(0, 2, 1)
    c = jnp.cumsum(log_f, axis=-1)
    scale = d ** -0.5
    outs = []
    for blk in range(S // FOX_BLOCK):
        q0 = blk * FOX_BLOCK
        q1 = q0 + FOX_BLOCK
        s = jnp.einsum('bhqd,bhkd->bhqk', q[:, :, q0:q1], k[:, :, :q1], preferred_element_type=jnp.float32) * scale
        s = s + c[:, :, q0:q1, None] - c[:, :, None, :q1]
        causal = jnp.arange(q0, q1)[:, None] >= jnp.arange(q1)[None, :]
        p = jax.nn.softmax(jnp.where(causal, s, -jnp.inf), axis=-1)
        outs.append(jnp.einsum('bhqk,bhkd->bhqd', p.astype(v.dtype), v[:, :, :q1]))
    return jnp.concatenate(outs, axis=2).transpose(0, 2, 1, 3)

def gla_chunked(q, k, v, log_a):
    B, S, H, dk = q.shape
    dv = v.shape[-1]
    C = GLA_CHUNK
    nc = S // C

    def to_chunks(t):
        return t.astype(jnp.float32).reshape(B, nc, C, H, t.shape[-1]).transpose(1, 0, 3, 2, 4)

    qc = to_chunks(q) * (dk ** -0.5)
    kc = to_chunks(k)
    vc = to_chunks(v)
    gc = to_chunks(log_a)
    causal = jnp.tril(jnp.ones((C, C), dtype=bool))[:, :, None]

    def step(state, inp):
        qi, ki, vi, gi = inp
        b = jnp.cumsum(gi, axis=2)
        b_last = b[:, :, -1:, :]
        o_inter = jnp.einsum('bhtd,bhdv->bhtv', qi * jnp.exp(b), state)
        diff = b[:, :, :, None, :] - b[:, :, None, :, :]
        decay = jnp.exp(jnp.where(causal, diff, -jnp.inf))
        attn = jnp.einsum('bhtd,bhsd,bhtsd->bhts', qi, ki, decay)
        o_intra = jnp.einsum('bhts,bhsv->bhtv', attn, vi)
        new_state = jnp.exp(b_last[:, :, 0, :])[..., None] * state + jnp.einsum('bhsd,bhsv->bhdv', ki * jnp.exp(b_last - b), vi)
        return new_state, o_inter + o_intra

    state0 = jnp.zeros((B, H, dk, dv), jnp.float32)
    _, o = lax.scan(step, state0, (qc, kc, vc, gc))
    return o.transpose(1, 0, 3, 2, 4).reshape(B, S, H, dv).astype(v.dtype)

def hybrid_mixer(h, w_in, b_forget, w_alpha_up, b_alpha, fox_out_gain, gla_out_gain, w_out):
    B, S, _ = h.shape
    offsets = [int(o) for o in np.cumsum(IN_WIDTHS)[:-1]]
    fq, fk, fv, ff, gq, gk, gv, gg, ga = jnp.split(h @ w_in, offsets, axis=-1)
    fox = forgetting_attention(
        fq.reshape(B, S, FOX_HEADS, FOX_HEAD_DIM),
        fk.reshape(B, S, FOX_HEADS, FOX_HEAD_DIM),
        fv.reshape(B, S, FOX_HEADS, FOX_HEAD_DIM),
        ff + b_forget)
    fox = rms_norm(fox, fox_out_gain.reshape(FOX_HEADS, FOX_HEAD_DIM))
    log_a = jax.nn.log_sigmoid((ga @ w_alpha_up + b_alpha).astype(jnp.float32)) / GLA_GATE_TAU
    gla = gla_chunked(
        gq.reshape(B, S, GLA_HEADS, GLA_KEY_DIM),
        gk.reshape(B, S, GLA_HEADS, GLA_KEY_DIM),
        gv.reshape(B, S, GLA_HEADS, GLA_VAL_DIM),
        log_a.reshape(B, S, GLA_HEADS, GLA_KEY_DIM))
    gla = rms_norm(gla, gla_out_gain.reshape(GLA_HEADS, GLA_VAL_DIM)) * jax.nn.silu(gg.reshape(B, S, GLA_HEADS, GLA_VAL_DIM))
    y = jnp.concatenate([fox.reshape(B, S, FOX_WIDTH), gla.reshape(B, S, GLA_V_WIDTH)], axis=-1)
    return y @ w_out

def memory_cross_attention(h, mem_n, w_xq, w_xk, w_xv, w_xo):
    B, S, _ = h.shape
    M = mem_n.shape[1]
    q = (h @ w_xq).reshape(B, S, X_HEADS, X_HEAD_DIM)
    k = (mem_n @ w_xk).reshape(B, M, X_HEADS, X_HEAD_DIM)
    v = (mem_n @ w_xv).reshape(B, M, X_HEADS, X_HEAD_DIM)
    s = jnp.einsum('bqhd,bkhd->bhqk', q, k, preferred_element_type=jnp.float32) * (X_HEAD_DIM ** -0.5)
    p = jax.nn.softmax(s, axis=-1)
    o = jnp.einsum('bhqk,bkhd->bqhd', p.astype(v.dtype), v).reshape(B, S, X_WIDTH)
    return o @ w_xo

def hierarchical_moe(h, w_rg, b_rg, w_re, b_re, w_e_gate, w_e_up, w_e_down):
    B, S, D = h.shape
    N = B * S
    hf = h.reshape(N, D)
    g_prob = jax.nn.softmax((hf @ w_rg).astype(jnp.float32) + b_rg.astype(jnp.float32), axis=-1)
    grp = jnp.argmax(g_prob, axis=-1)
    p_grp = jnp.take_along_axis(g_prob, grp[:, None], axis=-1)
    e_logits = ((hf @ w_re).astype(jnp.float32) + b_re.astype(jnp.float32)).reshape(N, N_GROUPS, EXPERTS_PER_GROUP)
    e_logits = jnp.take_along_axis(e_logits, grp[:, None, None], axis=1)[:, 0]
    top_p, top_i = lax.top_k(jax.nn.softmax(e_logits, axis=-1), TOP_K)
    gate = p_grp * top_p / jnp.sum(top_p, axis=-1, keepdims=True)
    expert = grp[:, None].astype(jnp.int32) * EXPERTS_PER_GROUP + top_i.astype(jnp.int32)
    Mrows = N * TOP_K
    flat_e = expert.reshape(Mrows)
    flat_g = gate.reshape(Mrows)
    flat_tok = jnp.repeat(jnp.arange(N, dtype=jnp.int32), TOP_K)
    order = jnp.argsort(flat_e)
    sorted_e = flat_e[order]
    counts = jnp.bincount(flat_e, length=N_EXPERTS)
    padded = (counts + MOE_BLOCK - 1) // MOE_BLOCK * MOE_BLOCK
    starts = jnp.cumsum(counts) - counts
    pad_ends = jnp.cumsum(padded)
    pad_starts = pad_ends - padded
    dest = pad_starts[sorted_e] + jnp.arange(Mrows, dtype=jnp.int32) - starts[sorted_e]
    R = Mrows + N_EXPERTS * MOE_BLOCK
    n_blocks = R // MOE_BLOCK
    row_tok = jnp.full((R,), N, dtype=jnp.int32).at[dest].set(flat_tok[order])
    row_gate = jnp.zeros((R,), jnp.float32).at[dest].set(flat_g[order])
    block_e = jnp.minimum(jnp.searchsorted(pad_ends, jnp.arange(n_blocks) * MOE_BLOCK, side='right'), N_EXPERTS - 1)
    x_rows = jnp.concatenate([hf, jnp.zeros((1, D), hf.dtype)], axis=0)[row_tok].reshape(n_blocks, MOE_BLOCK, D)

    def expert_block(args):
        xb, e = args
        u = jax.nn.silu(xb @ w_e_gate[e]) * (xb @ w_e_up[e])
        return u @ w_e_down[e]

    y_rows = lax.map(expert_block, (x_rows, block_e)).reshape(R, D)
    y = jax.ops.segment_sum(y_rows.astype(jnp.float32) * row_gate[:, None], row_tok, num_segments=N + 1)[:N]
    return y.reshape(B, S, D).astype(h.dtype)

def first_inputs(seed: int = 0) -> dict:
    key = jax.random.key(seed)
    ks = jax.random.split(key, 26)
    f32 = jnp.float32
    L = DEPTH

    def w(k, shape, fan_in, scale=1.0):
        return jax.random.normal(k, shape, f32) * (scale * fan_in ** -0.5)

    def gain(k, shape):
        return 1.0 + 0.02 * jax.random.normal(k, shape, f32)

    def small(k, shape, scale):
        return scale * jax.random.normal(k, shape, f32)

    return {
        'x': jax.random.normal(ks[0], (BATCH, SEQ, D_MODEL), f32),
        'mem': jax.random.normal(ks[1], (BATCH, MEM_LEN, D_MODEL), f32),
        'mem_norm': gain(ks[2], (D_MODEL,)),
        'mix_norm': gain(ks[3], (L, D_MODEL)),
        'w_in': w(ks[4], (L, D_MODEL, IN_PROJ_WIDTH), D_MODEL),
        'b_forget': FORGET_BIAS_INIT + small(ks[5], (L, FOX_HEADS), 0.1),
        'w_alpha_up': w(ks[6], (L, GLA_GATE_RANK, GLA_QK_WIDTH), GLA_GATE_RANK),
        'b_alpha': small(ks[7], (L, GLA_QK_WIDTH), 0.1),
        'fox_out_gain': gain(ks[8], (L, FOX_WIDTH)),
        'gla_out_gain': gain(ks[9], (L, GLA_V_WIDTH)),
        'w_out': w(ks[10], (L, MIX_WIDTH, D_MODEL), MIX_WIDTH, RESID_SCALE),
        'cross_norm': gain(ks[11], (L, D_MODEL)),
        'w_xq': w(ks[12], (L, D_MODEL, X_WIDTH), D_MODEL),
        'w_xk': w(ks[13], (L, D_MODEL, X_WIDTH), D_MODEL),
        'w_xv': w(ks[14], (L, D_MODEL, X_WIDTH), D_MODEL),
        'w_xo': w(ks[15], (L, X_WIDTH, D_MODEL), X_WIDTH, RESID_SCALE),
        'moe_norm': gain(ks[16], (L, D_MODEL)),
        'w_router_group': w(ks[17], (L, D_MODEL, N_GROUPS), D_MODEL),
        'b_router_group': small(ks[18], (L, N_GROUPS), 0.01),
        'w_router_expert': w(ks[19], (L, D_MODEL, N_EXPERTS), D_MODEL),
        'b_router_expert': small(ks[20], (L, N_EXPERTS), 0.01),
        'w_expert_gate': w(ks[21], (L, N_EXPERTS, D_MODEL, D_EXPERT), D_MODEL),
        'w_expert_up': w(ks[22], (L, N_EXPERTS, D_MODEL, D_EXPERT), D_MODEL),
        'w_expert_down': w(ks[23], (L, N_EXPERTS, D_EXPERT, D_MODEL), D_EXPERT, RESID_SCALE),
        'final_norm': gain(ks[24], (D_MODEL,)),
    }

def first_block(x, mem, mem_norm, mix_norm, w_in, b_forget, w_alpha_up, b_alpha, fox_out_gain, gla_out_gain, w_out,
              cross_norm, w_xq, w_xk, w_xv, w_xo, moe_norm, w_router_group, b_router_group, w_router_expert,
              b_router_expert, w_expert_gate, w_expert_up, w_expert_down, final_norm):
    mem_n = rms_norm(mem, mem_norm)
    h = x
    for l in range(DEPTH):
        h = h + hybrid_mixer(rms_norm(h, mix_norm[l]), w_in[l], b_forget[l], w_alpha_up[l], b_alpha[l],
                             fox_out_gain[l], gla_out_gain[l], w_out[l])
        h = h + memory_cross_attention(rms_norm(h, cross_norm[l]), mem_n, w_xq[l], w_xk[l], w_xv[l], w_xo[l])
        h = h + hierarchical_moe(rms_norm(h, moe_norm[l]), w_router_group[l], b_router_group[l],
                                 w_router_expert[l], b_router_expert[l], w_expert_gate[l], w_expert_up[l],
                                 w_expert_down[l])
    return rms_norm(h, final_norm)


DEPTH_2 = 2

N_MIXERS = 3
GRID_W = 64
Q_BLOCK = 128
D_FF = 2816
FFN_RES = 0.5

DIFF_HEAD_DIM = 64
DIFF_HEADS = D_MODEL // (2 * DIFF_HEAD_DIM)
ROPE_THETA = 500000.0
ROPE_DIMS = DIFF_HEAD_DIM // 4

NA_HEAD_DIM = 64
NA_HEADS = D_MODEL // NA_HEAD_DIM
NA_WIN_H = 8
NA_WIN_W = 16

GQA_HEAD_DIM = 64
GQA_Q_HEADS = D_MODEL // GQA_HEAD_DIM
GQA_KV_HEADS = GQA_Q_HEADS // 4
AXIAL_THETA = 10000.0

N_A = len(range(0, DEPTH_2, N_MIXERS))
N_B = len(range(1, DEPTH_2, N_MIXERS))
N_C = len(range(2, DEPTH_2, N_MIXERS))


def _rmsnorm(x, g):
    xf = x.astype(jnp.float32)
    y = xf * lax.rsqrt(jnp.mean(xf * xf, axis=-1, keepdims=True) + EPS)
    return (y * g.astype(jnp.float32)).astype(x.dtype)

def _swiglu(x, wg, wu, wd):
    return (jax.nn.silu(x @ wg) * (x @ wu)) @ wd

def _rope_angles(pos, dims, theta):
    inv = theta ** (-jnp.arange(0, dims, 2, dtype=jnp.float32) / dims)
    return pos[:, None] * inv[None, :]

def _rotate(x, ang):
    m = ang.shape[1]
    ang = ang.reshape((1, ang.shape[0]) + (1,) * (x.ndim - 3) + (m,))
    cos = jnp.cos(ang).astype(x.dtype)
    sin = jnp.sin(ang).astype(x.dtype)
    x1, x2 = x[..., :m], x[..., m:]
    return jnp.concatenate([x1 * cos - x2 * sin, x2 * cos + x1 * sin], axis=-1)

def _to_blocks(q):
    b, s = q.shape[:2]
    return jnp.moveaxis(q.reshape((b, s // Q_BLOCK, Q_BLOCK) + q.shape[2:]), 1, 0)

def _from_blocks(o):
    o = jnp.moveaxis(o, 0, 1)
    return o.reshape((o.shape[0], o.shape[1] * o.shape[2]) + o.shape[3:])

def _diff_attention(h, w_in, w_out, lam_vecs, subln_g, layer_idx):
    b, s, _ = h.shape
    nh, dh = DIFF_HEADS, DIFF_HEAD_DIM
    q, k, v = jnp.split(h @ w_in, 3, axis=-1)
    q = q.reshape(b, s, nh, 2, dh)
    k = k.reshape(b, s, nh, 2, dh)
    v = v.reshape(b, s, nh, 2 * dh)
    ang = _rope_angles(jnp.arange(s, dtype=jnp.float32), ROPE_DIMS, ROPE_THETA)
    q = jnp.concatenate([_rotate(q[..., :ROPE_DIMS], ang), q[..., ROPE_DIMS:]], axis=-1)
    k = jnp.concatenate([_rotate(k[..., :ROPE_DIMS], ang), k[..., ROPE_DIMS:]], axis=-1)
    lam_init = 0.8 - 0.6 * math.exp(-0.3 * layer_idx)
    lv = lam_vecs.astype(jnp.float32)
    lam = jnp.exp(jnp.sum(lv[0] * lv[1])) - jnp.exp(jnp.sum(lv[2] * lv[3])) + lam_init
    scale = dh ** -0.5

    def block(qb):
        sc = jnp.einsum('bqhcd,bshcd->bhcqs', qb, k).astype(jnp.float32) * scale
        p = jax.nn.softmax(sc, axis=-1)
        a = (p[:, :, 0] - lam * p[:, :, 1]).astype(v.dtype)
        return jnp.einsum('bhqs,bshe->bqhe', a, v)

    o = _from_blocks(lax.map(block, _to_blocks(q)))
    o = _rmsnorm(o, subln_g) * (1.0 - lam_init)
    return o.reshape(b, s, nh * 2 * dh) @ w_out

def _neighborhood_attention(h, w_in, w_out, rpb):
    b, s, _ = h.shape
    nh, dh = NA_HEADS, NA_HEAD_DIM
    rows = s // GRID_W
    kh = min(NA_WIN_H, rows)
    kw = NA_WIN_W
    q, k, v = jnp.split(h @ w_in, 3, axis=-1)
    q = q.reshape(b, rows, GRID_W, nh, dh)
    k = k.reshape(b, rows, GRID_W, nh, dh)
    v = v.reshape(b, rows, GRID_W, nh, dh)
    cols = jnp.arange(GRID_W)
    col_start = jnp.clip(cols - kw // 2, 0, GRID_W - kw)
    col_idx = col_start[:, None] + jnp.arange(kw)[None, :]
    dc = col_idx - cols[:, None] + (NA_WIN_W - 1)
    scale = dh ** -0.5

    def row_step(r):
        r0 = jnp.clip(r - kh // 2, 0, rows - kh)
        dr = r0 + jnp.arange(kh) - r + (NA_WIN_H - 1)
        k_band = lax.dynamic_slice_in_dim(k, r0, kh, axis=1)
        v_band = lax.dynamic_slice_in_dim(v, r0, kh, axis=1)
        k_win = k_band[:, :, col_idx]
        v_win = v_band[:, :, col_idx]
        q_row = lax.dynamic_index_in_dim(q, r, axis=1, keepdims=False)
        bias = rpb[:, dr[None, :, None], dc[:, None, :]]
        sc = jnp.einsum('bqhd,brqjhd->bhqrj', q_row, k_win).astype(jnp.float32) * scale
        sc = sc + bias.astype(jnp.float32)[None]
        p = jax.nn.softmax(sc.reshape(b, nh, GRID_W, kh * kw), axis=-1)
        p = p.reshape(sc.shape).astype(v.dtype)
        return jnp.einsum('bhqrj,brqjhd->bqhd', p, v_win)

    o = lax.map(row_step, jnp.arange(rows))
    o = jnp.moveaxis(o, 0, 1).reshape(b, s, nh * dh)
    return o @ w_out

def _gqa_axial(h, w_in, w_out, qk_g):
    b, s, _ = h.shape
    nq, nkv, dh = GQA_Q_HEADS, GQA_KV_HEADS, GQA_HEAD_DIM
    grp = nq // nkv
    qkv = h @ w_in
    q = qkv[..., :nq * dh].reshape(b, s, nkv, grp, dh)
    k = qkv[..., nq * dh:(nq + nkv) * dh].reshape(b, s, nkv, dh)
    v = qkv[..., (nq + nkv) * dh:].reshape(b, s, nkv, dh)
    q = _rmsnorm(q, qk_g[0])
    k = _rmsnorm(k, qk_g[1])
    t = jnp.arange(s)
    half = dh // 2
    ang_r = _rope_angles((t // GRID_W).astype(jnp.float32), half, AXIAL_THETA)
    ang_c = _rope_angles((t % GRID_W).astype(jnp.float32), half, AXIAL_THETA)
    q = jnp.concatenate([_rotate(q[..., :half], ang_r), _rotate(q[..., half:], ang_c)], axis=-1)
    k = jnp.concatenate([_rotate(k[..., :half], ang_r), _rotate(k[..., half:], ang_c)], axis=-1)
    scale = dh ** -0.5

    def block(qb):
        sc = jnp.einsum('bqkgd,bskd->bkgqs', qb, k).astype(jnp.float32) * scale
        p = jax.nn.softmax(sc, axis=-1).astype(v.dtype)
        return jnp.einsum('bkgqs,bskd->bqkgd', p, v)

    o = _from_blocks(lax.map(block, _to_blocks(q)))
    return o.reshape(b, s, nq * dh) @ w_out

def second_inputs(seed: int = 0) -> dict:
    key = jax.random.key(seed)
    ks = jax.random.split(key, 20)

    def w(k, shape, fan_in):
        return jax.random.normal(k, shape, jnp.float32) * fan_in ** -0.5

    def gain(k, shape):
        return 1.0 + 0.05 * jax.random.normal(k, shape, jnp.float32)

    diff_w = DIFF_HEADS * 2 * DIFF_HEAD_DIM
    na_w = NA_HEADS * NA_HEAD_DIM
    gqa_q = GQA_Q_HEADS * GQA_HEAD_DIM
    gqa_in = (GQA_Q_HEADS + 2 * GQA_KV_HEADS) * GQA_HEAD_DIM
    return {
        'x': jax.random.normal(ks[0], (BATCH, SEQ, D_MODEL), jnp.float32),
        'norm_g': gain(ks[1], (DEPTH_2, 6, D_MODEL)),
        'ffn1_wg': w(ks[2], (DEPTH_2, D_MODEL, D_FF), D_MODEL),
        'ffn1_wu': w(ks[3], (DEPTH_2, D_MODEL, D_FF), D_MODEL),
        'ffn1_wd': w(ks[4], (DEPTH_2, D_FF, D_MODEL), D_FF),
        'ffn2_wg': w(ks[5], (DEPTH_2, D_MODEL, D_FF), D_MODEL),
        'ffn2_wu': w(ks[6], (DEPTH_2, D_MODEL, D_FF), D_MODEL),
        'ffn2_wd': w(ks[7], (DEPTH_2, D_FF, D_MODEL), D_FF),
        'diff_w_in': w(ks[8], (N_A, D_MODEL, 3 * diff_w), D_MODEL),
        'diff_w_out': w(ks[9], (N_A, diff_w, D_MODEL), diff_w),
        'diff_lambda': 0.1 * jax.random.normal(ks[10], (N_A, 4, DIFF_HEAD_DIM), jnp.float32),
        'diff_subln': gain(ks[11], (N_A, 2 * DIFF_HEAD_DIM)),
        'na_w_in': w(ks[12], (N_B, D_MODEL, 3 * na_w), D_MODEL),
        'na_w_out': w(ks[13], (N_B, na_w, D_MODEL), na_w),
        'na_rpb': 0.1 * jax.random.normal(ks[14], (N_B, NA_HEADS, 2 * NA_WIN_H - 1, 2 * NA_WIN_W - 1), jnp.float32),
        'gqa_w_in': w(ks[15], (N_C, D_MODEL, gqa_in), D_MODEL),
        'gqa_w_out': w(ks[16], (N_C, gqa_q, D_MODEL), gqa_q),
        'gqa_qk_norm': gain(ks[17], (N_C, 2, GQA_HEAD_DIM)),
    }

def second_block(x, norm_g, ffn1_wg, ffn1_wu, ffn1_wd, ffn2_wg, ffn2_wu, ffn2_wd,
              diff_w_in, diff_w_out, diff_lambda, diff_subln,
              na_w_in, na_w_out, na_rpb,
              gqa_w_in, gqa_w_out, gqa_qk_norm):
    h = x
    for i in range(DEPTH_2):
        g = norm_g[i]
        h = h + FFN_RES * _rmsnorm(_swiglu(_rmsnorm(h, g[0]), ffn1_wg[i], ffn1_wu[i], ffn1_wd[i]), g[1])
        u = _rmsnorm(h, g[2])
        kind, j = i % N_MIXERS, i // N_MIXERS
        if kind == 0:
            m = _diff_attention(u, diff_w_in[j], diff_w_out[j], diff_lambda[j], diff_subln[j], i)
        elif kind == 1:
            m = _neighborhood_attention(u, na_w_in[j], na_w_out[j], na_rpb[j])
        else:
            m = _gqa_axial(u, gqa_w_in[j], gqa_w_out[j], gqa_qk_norm[j])
        h = h + _rmsnorm(m, g[3])
        h = h + FFN_RES * _rmsnorm(_swiglu(_rmsnorm(h, g[4]), ffn2_wg[i], ffn2_wu[i], ffn2_wd[i]), g[5])
    return h


def setup_inputs(seed=0):
    out = dict(first_inputs(seed))
    for name, value in second_inputs(seed + 1).items():
        if name != "x":
            out[name + "_2"] = value
    return out


def reference(
    x, mem, mem_norm, mix_norm, w_in, b_forget, w_alpha_up, b_alpha, fox_out_gain, gla_out_gain,
    w_out, cross_norm, w_xq, w_xk, w_xv, w_xo, moe_norm, w_router_group, b_router_group,
    w_router_expert, b_router_expert, w_expert_gate, w_expert_up, w_expert_down, final_norm,
    norm_g_2, ffn1_wg_2, ffn1_wu_2, ffn1_wd_2, ffn2_wg_2, ffn2_wu_2, ffn2_wd_2, diff_w_in_2,
    diff_w_out_2, diff_lambda_2, diff_subln_2, na_w_in_2, na_w_out_2, na_rpb_2, gqa_w_in_2,
    gqa_w_out_2, gqa_qk_norm_2,
):
    x = first_block(
        x, mem, mem_norm, mix_norm, w_in, b_forget, w_alpha_up, b_alpha, fox_out_gain,
        gla_out_gain, w_out, cross_norm, w_xq, w_xk, w_xv, w_xo, moe_norm, w_router_group,
        b_router_group, w_router_expert, b_router_expert, w_expert_gate, w_expert_up,
        w_expert_down, final_norm,
    )
    return second_block(
        x, norm_g_2, ffn1_wg_2, ffn1_wu_2, ffn1_wd_2, ffn2_wg_2, ffn2_wu_2, ffn2_wd_2,
        diff_w_in_2, diff_w_out_2, diff_lambda_2, diff_subln_2, na_w_in_2, na_w_out_2, na_rpb_2,
        gqa_w_in_2, gqa_w_out_2, gqa_qk_norm_2,
    )


_drawn_inputs = setup_inputs


def setup_inputs(seed=0):
    import zlib

    import numpy as np

    out = dict(_drawn_inputs(seed))
    spreads = {}
    factors = {'mem_norm': 5.818,
     'b_alpha': 3.219,
     'fox_out_gain': 2.744,
     'gla_out_gain': 4.023,
     'cross_norm': 8.0,
     'moe_norm': 2.809,
     'b_router_group': 4.709,
     'b_router_expert': 4.803,
     'na_rpb_2': 2.717}
    for name, (base, spread) in spreads.items():
        noise = np.random.default_rng([zlib.crc32(name.encode()), seed]).standard_normal(out[name].shape)
        drawn = base * np.exp(spread * noise) if base else spread * noise
        out[name] = jnp.asarray(drawn.astype(out[name].dtype))
    for name, factor in factors.items():
        out[name] = (out[name] * factor).astype(out[name].dtype)
    return out
```

```python
from contextlib import ExitStack

import numpy as np
import concourse.bass as bass
from concourse import mybir

F32 = mybir.dt.float32
F32R = mybir.dt.float32r
U8 = mybir.dt.uint8
I32 = mybir.dt.int32
U32 = mybir.dt.uint32
ALU = mybir.AluOpType
ACT = mybir.ActivationFunctionType
AX = mybir.AxisListType

P = 128
S = 256
NT = S // P
D = 1024
KD = D // P
EPS = 1e-6
NEG = -1e30
LOWEST = -3e38
CHUNK = 2048
RAW = 6
SPLIT = 3
LO_V = 1280
GROUP = 256
FF_GROUPS = 2816 // GROUP
MOE_GROUPS = 16 * 512 // GROUP
GLA_C = 64
LEVELS = 6

PHASES = [("mix_in", 12), ("mix_out", 4), ("mem_kv", 4), ("cross_q", 2), ("cross_out", 2),
          ("moe", 3 * MOE_GROUPS), ("ffn1_0", 3 * FF_GROUPS), ("diff_in", 12), ("diff_out", 4),
          ("ffn2_0", 3 * FF_GROUPS), ("ffn1_1", 3 * FF_GROUPS), ("na_in", 12), ("na_out", 4),
          ("ffn2_1", 3 * FF_GROUPS)]
START, _n = {}, 0
for _name, _count in PHASES:
    START[_name] = _n
    _n += _count
CHUNKS = _n

TURNS = ["mix", "mix_y", "mem", "cross", "cross_y", "moe", "ffn1_0", "diff", "diff_y", "ffn2_0",
         "ffn1_1", "na", "na_y", "ffn2_1"]
TURN_AT = {name: i for i, name in enumerate(TURNS)}
TURN_BANKS = {name: 2 if name == "cross_y" else 4 for name in TURNS}
TURN_BASE = {name: sum(TURN_BANKS[x] for x in TURNS[:i]) for i, name in enumerate(TURNS)}

NORMS = ["mix", "mem", "cross", "moe", "final", "ffn1_0", "ffn1_0_p", "diff", "diff_p", "ffn2_0",
         "ffn2_0_p", "ffn1_1", "ffn1_1_p", "na", "na_p", "ffn2_1", "ffn2_1_p"]
NORM_AT = {name: i for i, name in enumerate(NORMS)}
NORM_FACTOR = {"ffn1_0_p": 0.5, "ffn2_0_p": 0.5, "ffn1_1_p": 0.5, "ffn2_1_p": 0.5}
SCORE_SCALE = {"mix": 64 ** -0.5, "cross": 128 ** -0.5, "diff": 64 ** -0.5, "na": 64 ** -0.5}
SCALED = list(SCORE_SCALE)
MIX_LOADS = 9

SUMS = ["mix_out", "cross_out", "moe", "ffn1_0", "diff_out", "ffn2_0", "ffn1_1", "na_out", "ffn2_1"]
SUM_AT = {name: i for i, name in enumerate(SUMS)}

PROJ = ["gg", "gqk", "gv", "fq", "fk", "fv", "xk", "xv", "xq", "dq0", "dq1", "dk0", "dk1", "dv0",
        "dv1", "nq0", "nq1", "nk0", "nk1", "nv0", "nv1"]
PROJ_AT = {name: i for i, name in enumerate(PROJ)}
PROJ_CHUNK = {}
for _i, _name in enumerate(PROJ):
    _ph, _first = (("mix_in", 0) if _i < 6 else ("mem_kv", 6) if _i < 8 else ("cross_q", 8) if _i < 9
                   else ("diff_in", 9) if _i < 15 else ("na_in", 15))
    PROJ_CHUNK[_name] = START[_ph] + 2 * (_i - _first)

CORES = ["fox", "cross", "diff", "na"]
PAIRS = {"fox": 4, "cross": 2, "diff": 8, "na": 8}
GSIZE = {"fox": 4, "cross": 2, "diff": 2, "na": 4}
UNIT0 = {"fox": 0, "cross": 8, "diff": 12, "na": 28}
GROUP0 = {"fox": 0, "cross": 2, "diff": 4, "na": 12}


def score_map(name, p, j):
    return 2 * p + j if name == "cross" else 4 * (p // 2) + 2 * j + p % 2


QKT = ["gla", "fox", "cross", "diff", "na"]
QKT_BANKS = {"gla": 1, "fox": 2, "cross": 2, "diff": 4, "na": 4}
QKT0 = {"gla": 0, "fox": 1, "cross": 3, "diff": 5, "na": 9}
HEADNORMS = ["gla", "fox", "diff"]

C_IDENT, C_IOTA, C_NEGHALF, C_ROPE = 0, 128, 132, 148
C_TRI, C_ONES, C_CUM, C_SUF, C_CAUSAL = 180, 308, 436, 564, 692
C_NAMASK, C_END = 948, 1012


def shape_constants():
    c = np.zeros((P, C_END), np.float32)
    s, t = np.arange(P)[:, None], np.arange(P)[None, :]
    c[:, C_IDENT:C_IDENT + P] = s == t
    c[:, C_IOTA:C_IOTA + 4] = np.arange(4)
    c[:, C_NEGHALF:C_NEGHALF + 16] = -0.5
    inv = np.float32(500000.0) ** (-np.arange(0, 16, 2, dtype=np.float32) / np.float32(16))
    ang = np.arange(S, dtype=np.float32)[:, None] * inv[None, :]
    rope = np.stack([np.cos(ang), np.sin(ang)], 1).astype(np.float32)
    c[:, C_ROPE:C_ROPE + 32] = rope.reshape(NT, P, 16).transpose(1, 0, 2).reshape(P, 32)
    c[:, C_TRI:C_TRI + P] = s <= t
    c[:, C_ONES:C_ONES + P] = 1.0
    same = s // GLA_C == t // GLA_C
    c[:, C_CUM:C_CUM + P] = (same & (s <= t)) / 16.0
    c[:, C_SUF:C_SUF + P] = (same & (s > t)) / 16.0
    c[:, C_CAUSAL + P:C_CAUSAL + 2 * P] = np.where(t > s, NEG, 0.0)
    q, k = np.arange(64)[:, None], np.arange(64)[None, :]
    left = np.clip(q - 8, 0, 48)
    c[:, C_NAMASK:C_NAMASK + 64] = np.tile(np.where((k >= left) & (k < left + 16), 0.0, NEG), (2, 1))
    m = np.zeros((P, LEVELS + 1, P), np.uint8)
    for l in range(LEVELS):
        h = 1 << l
        m[:, l] = (s // (2 * h) == t // (2 * h)) & (s % (2 * h) < h) & (t % (2 * h) >= h)
    m[:, LEVELS] = s == t
    return c, m.reshape(P, (LEVELS + 1) * P).view(np.int32)


def two_blocks(nc, a, out):
    with ExitStack() as ctx:
        def sb(name, shape, dt=F32):
            return ctx.enter_context(nc.sbuf_tensor("sb_" + name, shape, dt))

        def sem(name):
            return ctx.enter_context(nc.semaphore(name))

        raw = sb("raw", [P, RAW, CHUNK])
        w_hi = sb("w_hi", [P, SPLIT, CHUNK], F32R)
        w_lo = sb("w_lo", [P, SPLIT, CHUNK], F32R)
        x = sb("x", [P, NT, D])
        x_hi = sb("x_hi", [P, NT, KD, P], F32R)
        x_lo = sb("x_lo", [P, NT, KD, P], F32R)
        y = sb("y", [P, NT, D])
        h_hi = sb("h_hi", [P, 2, 2, S], F32R)
        h_lo = sb("h_lo", [P, 2, 2, S], F32R)
        fb = sb("fb", [P, 2048])
        gain = sb("gain", [P, 2, D])
        arena = sb("arena", [P, 12800])
        const = sb("const", [P, C_TRI])
        sums = sb("sums", [P, len(NORMS), NT])
        rstd = sb("rstd", [P, len(NORMS), NT])
        rstd_q = sb("rstd_q", [P, 4, NT])
        vtmp, htmp = sb("vtmp", [P, 2]), sb("htmp", [P, 16])
        hsum = sb("hsum", [P, 16])
        hrstd = sb("hrstd", [P, 16])
        negmax = sb("negmax", [P, 3, 2])
        rows = sb("rows", [P, 44, 2])
        rrow = sb("rrow", [P, 8])
        rheads = sb("rheads", [P, 8])
        gates = sb("gates", [P, NT, 16])
        psum = ctx.enter_context(nc.psum_tensor("psum", [P, 8, 512], F32))

        ident = const[:, C_IDENT:C_IDENT + P]
        iota4 = const[:, C_IOTA:C_IOTA + 4]
        neghalf = const[:, C_NEGHALF:C_NEGHALF + 16]
        rope = const[:, C_ROPE:C_ROPE + 32].rearrange("p (t c j) -> p t c j", t=NT, c=2)
        silu = fb[:, 0:1024].rearrange("p (r t f) -> p r t f", r=2, t=NT)
        hid = fb[:, 1024:2048].rearrange("p (r t f) -> p r t f", r=2, t=NT)
        junk = fb[:, 0:D]

        def region(at, n):
            return arena[:, at:at + n]

        fq = region(0, 1024).rearrange("p (t c) -> p t c", t=NT)
        fk = region(1024, 1024).rearrange("p (t c) -> p t c", t=NT)
        fv = region(2048, 1024).rearrange("p (t c) -> p t c", t=NT)
        gg = region(3072, 1024).rearrange("p (t c) -> p t c", t=NT)
        gqk = region(4096, 1024).rearrange("p (t c) -> p t c", t=NT)
        gv = region(5120, 1024).rearrange("p (t c) -> p t c", t=NT)
        gb = region(6144, 512)
        lg = region(6656, 528).rearrange("p (t c) -> p t c", t=NT)
        ge = region(7184, 512)
        gz = region(7696, 1024).rearrange("p (r c) -> p r c", r=2)
        gs = region(8720, 512)
        st = region(9232, 768).rearrange("p (c f v) -> p c f v", c=3, f=2)
        fox_gain = region(10000, 512)
        gla_gain = region(10512, 512)
        bias_g = region(11024, 264)
        w_small = region(11288, 192).rearrange("p (k c) -> p k c", k=KD)
        w_alpha = region(11480, 256)
        mixc = region(11736, C_CAUSAL + 2 * P - C_TRI)
        tri, ones = mixc[:, 0:P], mixc[:, P:2 * P]
        cum, suf, causal = mixc[:, 2 * P:3 * P], mixc[:, 3 * P:4 * P], mixc[:, 4 * P:6 * P]
        mask_words = sb("masks", [P, (LEVELS + 1) * P // 4], I32)
        masks = mask_words[:, :].bitcast(U8)
        zeros = sb("zeros", [P, 512], mybir.dt.bfloat16)
        gaT = region(12504, 256)
        gqT, gkT = fb[:, 0:512], fb[:, 512:1024]
        at_ = fb[:, 1024:2048].rearrange("p (t h q) -> p t h q", t=NT, h=4)
        lsg = region(7696, 528).rearrange("p (t c) -> p t c", t=NT)
        gks = gqk[:, :, 256:512]
        gexp = region(6656, 512)
        fqT = region(4096, 1024).rearrange("p (f s) -> p f s", f=4)
        fkT = region(6144, 1024).rearrange("p (f s) -> p f s", f=4)
        probs_1 = region(7168, 1536).rearrange("p (r m k) -> p r m k", r=3, m=2)
        probsT_1 = region(8704, 1024).rearrange("p (r c) -> p r c", r=2)
        ct = region(12504, 256)
        mem = region(0, 2048).rearrange("p (t c) -> p t c", t=NT)
        xk = region(2048, 1024).rearrange("p (t c) -> p t c", t=NT)
        xv = region(3072, 1024).rearrange("p (t c) -> p t c", t=NT)
        xkT = region(4096, 1024).rearrange("p (f s) -> p f s", f=4)
        xq = region(5120, 1024).rearrange("p (t c) -> p t c", t=NT)
        xqT = region(6144, 1024).rearrange("p (f s) -> p f s", f=4)
        w_router = region(10000, 160).rearrange("p (k c) -> p k c", k=KD)
        b_router = region(10160, 20)
        rt = region(10192, 512).rearrange("p (t c) -> p t c", t=NT)
        q2 = region(0, 2048).rearrange("p (t c) -> p t c", t=NT)
        probs_2 = region(0, 1536).rearrange("p (r m k) -> p r m k", r=3, m=2)
        probsT_2 = region(1536, 1024).rearrange("p (r c) -> p r c", r=2)
        q2T = region(2560, 2048).rearrange("p (f s) -> p f s", f=8)
        k2T = region(4608, 2048).rearrange("p (f s) -> p f s", f=8)
        v2 = fb[:, :].rearrange("p (t c) -> p t c", t=NT)
        subln = region(6656, 128)
        lamv = region(6784, 256)
        lams = region(7040, 32)
        ropet = region(7168, 2048)
        nab = region(6656, 6144).rearrange("p (h r c) -> p h r c", h=16, r=6)
        namask = mask_words[:, 0:64].bitcast(F32)

        raw_landed = [sem(f"raw_landed{i}") for i in range(RAW)]
        hi_done, lo_v_done, lo_p_done = sem("hi_done"), sem("lo_v_done"), sem("lo_p_done")
        weights_used = sem("weights_used")
        x_landed, const_landed, mixw_landed, mem_landed = (
            sem("x_landed"), sem("const_landed"), sem("mixw_landed"), sem("mem_landed"))
        router_landed, diffw_landed = sem("router_landed"), sem("diffw_landed")
        nab_landed, namask_landed = sem("nab_landed"), sem("namask_landed")
        gain_landed = [sem("gain_landed0"), sem("gain_landed1")]
        gain_used = sem("gain_used")
        turn_src, turned, turn_hi, turn_lo = sem("turn_src"), sem("turned"), sem("turn_hi"), sem("turn_lo")
        squared, rstd_ready, rstdq_ready = sem("squared"), sem("rstd_ready"), sem("rstdq_ready")
        proj_t0, proj_out0, proj_out1 = sem("proj_t0"), sem("proj_out0"), sem("proj_out1")
        gu_t0, silu_done, hid_done = sem("gu_t0"), sem("silu_done"), sem("hid_done")
        hid_turned, hid_hi, hid_lo = sem("hid_turned"), sem("hid_hi"), sem("hid_lo")
        sum_t0, resid_done = sem("sum_t0"), sem("resid_done")
        qk_turned, q_out, k_out = sem("qk_turned"), sem("q_out"), sem("k_out")
        scores, max_done, probs_done = sem("scores"), sem("max_done"), sem("probs_done")
        probs_turned, probsT_done = sem("probs_turned"), sem("probsT_done")
        pv_done, pv_taken = sem("pv_done"), sem("pv_taken")
        head_sums, head_rstd = sem("head_sums"), sem("head_rstd")
        logits_done, logits_out = sem("logits_done"), sem("logits_out")
        ga_turned, ga_out, alpha_done, alpha_out = (
            sem("ga_turned"), sem("ga_out"), sem("alpha_done"), sem("alpha_out"))
        logits_in, logsig_abs, logsig_ln, logsig_done = sem("logits_in"), sem("logsig_abs"), sem("logsig_ln"), sem("logsig_done")
        decay_done, gb_out, suffix_out, ct_out = (
            sem("decay_done"), sem("gb_out"), sem("suffix_out"), sem("ct_out"))
        ks_ready, u_done, state_ready, qb_ready, expb_ready = (
            sem("ks_ready"), sem("u_done"), sem("state_ready"), sem("qb_ready"), sem("expb_ready"))
        diff_ready, decay_exp, z_ready, level_done, level_out = (
            sem("level_diff"), sem("level_exp"), sem("z_ready"), sem("level_done"), sem("level_out"))
        at_zero, gla_o_done, gla_o_out = sem("at_zero"), sem("gla_o_done"), sem("gla_o_out")
        route_exp, route_in, gates_ready = sem("route_exp"), sem("route_in"), sem("gates_ready")
        rope_done, lam_sum, lam_exp = sem("rope_done"), sem("lam_sum"), sem("lam_exp")
        nab_ready, zeros_ready = sem("nab_ready"), sem("zeros_ready")
        out_ready, out_landed = sem("out_ready"), sem("out_landed")
        dve_chain, act_chain, pool_chain = sem("dve_chain"), sem("act_chain"), sem("pool_chain")

        def columns(w, k0, c0):
            src = w.rearrange("(k p) c -> p k c", p=P)
            return [(slice(1024 * i, 1024 * i + 1024), src[:, k0 + 2 * i:k0 + 2 * i + 2, c0:c0 + 512], 2)
                    for i in range(2)]

        def full_rows(w, k0):
            src = w.rearrange("(k p) c -> p k c", p=P)
            return [(slice(1024 * i, 1024 * i + 1024), src[:, k0 + i:k0 + i + 1, :], 1) for i in range(2)]

        w_in = a["w_in"][0]
        OFF = {"fq": 0, "fk": 512, "fv": 1024, "gqk": 1544, "gv": 2056, "gg": 2568}
        PROJ_SRC = {n: (w_in, OFF[n]) for n in OFF}
        PROJ_SRC |= {"xk": (a["w_xk"][0], 0), "xv": (a["w_xv"][0], 0), "xq": (a["w_xq"][0], 0)}
        for i, n in enumerate(PROJ[9:15]):
            PROJ_SRC[n] = (a["diff_w_in_2"][0], 512 * i)
        for i, n in enumerate(PROJ[15:21]):
            PROJ_SRC[n] = (a["na_w_in_2"][0], 512 * i)
        SUM_SRC = {"mix_out": (a["w_out"][0], 4), "cross_out": (a["w_xo"][0], 2),
                   "diff_out": (a["diff_w_out_2"][0], 4), "na_out": (a["na_w_out_2"][0], 4)}
        FFN = {"moe": MOE_GROUPS, "ffn1_0": FF_GROUPS, "ffn2_0": FF_GROUPS, "ffn1_1": FF_GROUPS,
               "ffn2_1": FF_GROUPS}
        GU0 = {}
        for name in FFN:
            GU0[name] = sum(FFN[m] for m in list(FFN)[:list(FFN).index(name)])

        def swiglu_weights(name):
            if name == "moe":
                return a["w_expert_gate"][0], a["w_expert_up"][0], a["w_expert_down"][0]
            layer, which = int(name[-1]), name[:4]
            return a[which + "_wg_2"][layer], a[which + "_wu_2"][layer], a[which + "_wd_2"][layer]

        def gate_up(name, g, k0, it):
            parts = []
            for i, w in enumerate(swiglu_weights(name)[:2]):
                if name == "moe":
                    src = w[bass.ds(it + g // 2, 1)] if it is not None else w[g // 2:g // 2 + 1]
                    src = src.rearrange("e (k p) c -> p (e k) c", p=P)[:, k0:k0 + 4, GROUP * (g % 2):GROUP * (g % 2) + GROUP]
                else:
                    src = w.rearrange("(k p) c -> p k c", p=P)[:, k0:k0 + 4, :]
                    c = bass.ds(it * (2 * GROUP) + g * GROUP, GROUP) if it is not None else slice(g * GROUP, g * GROUP + GROUP)
                    src = src[:, :, c]
                parts.append((i, src, 4))
            return parts

        def down(name, g, it):
            w = swiglu_weights(name)[2]
            parts = []
            for i in (1, 0):
                if name == "moe":
                    src = w[bass.ds(it + g // 2, 1)] if it is not None else w[g // 2:g // 2 + 1]
                    src = src.rearrange("e (k p) c -> p (e k) c", p=P)[:, 2 * (g % 2) + i:2 * (g % 2) + i + 1, :]
                else:
                    r = bass.ds(it * (2 * GROUP) + g * GROUP + P * i, P) if it is not None else slice(g * GROUP + P * i, g * GROUP + P * i + P)
                    src = w[r, :].unsqueeze(1)
                parts.append((slice(1024 * i, 1024 * i + 1024), src, 1))
            return parts

        def shifted(value, it, per):
            return value if it is None else it * per + value

        def view(slot_ap, part, k):
            if isinstance(part, slice):
                return slot_ap[:, part].rearrange("p (k c) -> p k c", k=k)
            return slot_ap.rearrange("p (k u c) -> p k u c", k=k, u=2)[:, :, part, :]

        block = ctx.enter_context(nc.Block())

        @block.sync
        def _(sp):
            def load(n, parts, it=None):
                if n >= RAW:
                    sp.wait_ge(hi_done, shifted(n - RAW + 1, it, 6))
                    sp.wait_ge(lo_v_done, shifted(n - RAW + 1, it, 6))
                    sp.wait_ge(lo_p_done, shifted(n - RAW + 1, it, 6))
                for part, src, k in parts:
                    sp.dma_start(view(raw[:, n % RAW, :], part, k), src).then_inc(raw_landed[n % RAW], 16)

            def projection(name):
                w, c0 = PROJ_SRC[name]
                for half in range(2):
                    load(PROJ_CHUNK[name] + half, columns(w, 4 * half, c0))

            def out_projection(name):
                w, count = SUM_SRC[name]
                for i in range(count):
                    load(START[name] + i, full_rows(w, 2 * i))

            def swiglu(name):
                n, groups = START[name], FFN[name]

                def step(n, g, it=None):
                    load(n, gate_up(name, g + 1, 0, it), it)
                    load(n + 1, gate_up(name, g + 1, 4, it), it)
                    load(n + 2, down(name, g, it), it)

                load(n, gate_up(name, 0, 0, None))
                load(n + 1, gate_up(name, 0, 4, None))
                with sp.Fori(0, (groups - 1) // 2) as it:
                    step(n + 2, 0, it)
                    step(n + 5, 1, it)
                if groups % 2 == 0:
                    step(n + 3 * groups - 4, groups - 2)
                load(n + 3 * groups - 1, down(name, groups - 1, None))

            sp.dma_start(x[:, :, :], a["x"][0].rearrange("(t p) c -> p t c", p=P)).then_inc(x_landed, 16)
            sp.dma_start(const[:, :], a["consts"][:, 0:C_TRI]).then_inc(const_landed, 16)
            for name in PROJ[:6]:
                projection(name)
            out_projection("mix_out")
            projection("xk")
            projection("xv")
            projection("xq")
            out_projection("cross_out")
            swiglu("moe")
            swiglu("ffn1_0")
            for name in PROJ[9:15]:
                projection(name)
            out_projection("diff_out")
            swiglu("ffn2_0")
            swiglu("ffn1_1")
            for name in PROJ[15:21]:
                projection(name)
            out_projection("na_out")
            swiglu("ffn2_1")
            for t in range(NT):
                sp.wait_ge(out_ready, t + 1)
                sp.dma_start(out[0, t * P:t * P + P, :], x[:, t, :]).then_inc(out_landed, 16)
            sp.wait_ge(out_landed, 16 * NT)

        @block.tensor
        def _(pe):
            def products(bank, xh, xl, wh, wl, first, last):
                pe.matmul(bank, xh, wh, start=first, stop=False)
                pe.matmul(bank, xh, wl, start=False, stop=False)
                return pe.matmul(bank, xl, wh, start=False, stop=last)

            def weights(n, it=None):
                pe.wait_ge(lo_v_done, shifted(n + 1, it, 6))
                pe.wait_ge(lo_p_done, shifted(n + 1, it, 6))

            def turn(name):
                banks = TURN_BANKS[name]
                for i in range(banks):
                    t, kk = divmod(i, banks // NT)
                    if kk == 0:
                        pe.wait_ge(turn_src, NT * TURN_AT[name] + t + 1)
                    for k in range(4):
                        f = 4 * kk + k
                        last = pe.transpose(psum[:, i, k * P:k * P + P], y[:, t, f * P:f * P + P], ident)
                    last.then_inc(turned, 1)

            def input_ready(name):
                pe.wait_ge(turn_lo, TURN_BASE[name] + TURN_BANKS[name])

            def projection(name):
                j, n = PROJ_AT[name], PROJ_CHUNK[name]
                if j >= 2:
                    pe.wait_ge(proj_out0, j - 1)
                    pe.wait_ge(proj_out1, j - 1)
                for half in range(2):
                    weights(n + half)
                    for t in range(NT):
                        bank = psum[:, 2 * (j % 2) + t, :]
                        for k in range(4):
                            c = slice(512 * k, 512 * k + 512)
                            last = products(bank, x_hi[:, t, 4 * half + k, :], x_lo[:, t, 4 * half + k, :],
                                            w_hi[:, (n + half) % SPLIT, c], w_lo[:, (n + half) % SPLIT, c],
                                            half == 0 and k == 0, half == 1 and k == 3)
                        if t == 0 and half == 1:
                            last.then_inc(proj_t0, 1)
                    last.then_inc(weights_used, 1)

            def out_projection(name):
                count = SUM_SRC[name][1]
                for i in range(count):
                    n = START[name] + i
                    weights(n)
                    for t in range(NT):
                        for k in range(2):
                            for half in range(2):
                                c = slice(1024 * k + 512 * half, 1024 * k + 512 * half + 512)
                                last = products(psum[:, 4 + 2 * t + half, :], x_hi[:, t, 2 * i + k, :],
                                                x_lo[:, t, 2 * i + k, :], w_hi[:, n % SPLIT, c],
                                                w_lo[:, n % SPLIT, c], i == 0 and k == 0,
                                                i == count - 1 and k == 1)
                        if t == 0 and i == count - 1:
                            last.then_inc(sum_t0, 1)
                    last.then_inc(weights_used, 1)

            def swiglu(name):
                base, groups, gu0 = START[name], FFN[name], GU0[name]

                def gate_up_half(n, g, half, it=None):
                    par = (gu0 + g) % 2
                    weights(n, it)
                    for t in range(NT):
                        for k in range(4):
                            c = slice(512 * k, 512 * k + 512)
                            last = products(psum[:, 2 * par + t, :], x_hi[:, t, 4 * half + k, :],
                                            x_lo[:, t, 4 * half + k, :], w_hi[:, n % SPLIT, c],
                                            w_lo[:, n % SPLIT, c], half == 0 and k == 0,
                                            half == 1 and k == 3)
                        if t == 0 and half == 1:
                            last.then_inc(gu_t0, 1)
                    last.then_inc(weights_used, 1)

                def turn_hidden(g, it=None):
                    par = (gu0 + g) % 2
                    pe.wait_ge(hid_done, shifted(NT * (gu0 + g + 1), it, 2 * NT))
                    for f in range(2):
                        for t in range(NT):
                            last = pe.transpose(psum[:, 2 * par, f * S + t * P:f * S + t * P + P],
                                                hid[:, par, t, f * P:f * P + P], ident)
                    last.then_inc(hid_turned, 1)

                def down_sum(n, g, it=None, first=False, final=False):
                    par = (gu0 + g) % 2
                    weights(n, it)
                    pe.wait_ge(hid_lo, shifted(gu0 + g + 1, it, 2))
                    for t in range(NT):
                        for f in range(2):
                            for half in range(2):
                                c = slice(1024 * f + 512 * half, 1024 * f + 512 * half + 512)
                                bank = psum[:, 4 + 2 * t + half, :]
                                hh, hl = (h[:, par, f, t * P:t * P + P] for h in (h_hi, h_lo))
                                st0 = first and f == 0
                                sp0 = final and f == 1
                                pe.matmul(bank, hh, w_hi[:, n % SPLIT, c], start=st0, stop=False, skip_group_check=True)
                                pe.matmul(bank, hh, w_lo[:, n % SPLIT, c], start=False, stop=False, skip_group_check=True)
                                last = pe.matmul(bank, hl, w_hi[:, n % SPLIT, c], start=False, stop=sp0, skip_group_check=True)
                        if t == 0 and final:
                            last.then_inc(sum_t0, 1)
                    last.then_inc(weights_used, 1)

                def step(n, g, it=None, first=False):
                    gate_up_half(n, g + 1, 0, it)
                    turn_hidden(g, it)
                    gate_up_half(n + 1, g + 1, 1, it)
                    down_sum(n + 2, g, it, first)

                gate_up_half(base, 0, 0)
                gate_up_half(base + 1, 0, 1)
                for b in range(4, 8):
                    pe.matmul(psum[:, b, :], zeros[:, 0:P], zeros[:, :], start=True, stop=False, skip_group_check=True)
                with pe.Fori(0, (groups - 1) // 2) as it:
                    step(base + 2, 0, it)
                    step(base + 5, 1, it)
                if groups % 2 == 0:
                    step(base + 3 * groups - 4, groups - 2)
                turn_hidden(groups - 1)
                down_sum(base + 3 * groups - 1, groups - 1, final=True)

            def qk_turn(name, q, k):
                for b in range(QKT_BANKS[name]):
                    for i, src in enumerate((q, k)):
                        c = 2 * (QKT0[name] + b) + i
                        if QKT0[name] + b >= 2:
                            pe.wait_ge(q_out if i == 0 else k_out, QKT0[name] + b - 1)
                        for f in range(2):
                            for t in range(NT):
                                last = pe.transpose(psum[:, 4 + c % 4, f * S + t * P:f * S + t * P + P],
                                                    src[:, t, (2 * b + f) * P:(2 * b + f) * P + P], ident)
                        last.then_inc(qk_turned, 1)

            def attention(name, qT, kT, v, probs, probsT, d, last_proj):
                pairs, gsize, u0 = PAIRS[name], GSIZE[name], UNIT0[name]
                units = [(i, p) for i in range(NT) for p in range(pairs)]
                dv = {"fox": 64, "cross": 128, "diff": 128, "na": 64}[name]

                def keys(i):
                    return (i + 1) * P if name == "fox" else S

                def rows_of(T, m, c):
                    if d == P:
                        return T[:, m, c]
                    return T[(m % 2) * 64:(m % 2) * 64 + 64, m // 2, c]

                def score(n):
                    i, p = units[n]
                    u = u0 + n
                    if n >= 4:
                        pe.wait_ge(probs_done, u - 3)
                    for j in range(2):
                        m = score_map(name, p, j)
                        bank = psum[:, u % 4, j * S:j * S + keys(i)]
                        last = pe.matmul(bank, rows_of(qT, m, slice(i * P, i * P + P)),
                                         rows_of(kT, m, slice(0, keys(i))), start=True, stop=name != "fox")
                        if name == "fox":
                            last = pe.matmul(bank, ident[0:8, m:m + 1].to_broadcast([8, P]), ct[0:8, 0:keys(i)],
                                             start=False, stop=True)
                    last.then_inc(scores, 1)

                def turn_probs(n):
                    i, p = units[n]
                    u = u0 + n
                    pe.wait_ge(probs_done, u + 1)
                    if n >= 2:
                        pe.wait_ge(probsT_done, u - 1)
                    for j in range(2):
                        for kt in range(keys(i) // P):
                            last = pe.transpose(psum[:, 4 + u % 2, (2 * j + kt) * P:(2 * j + kt) * P + P],
                                                probs[:, u % 3, j, kt * P:kt * P + P], ident)
                    last.then_inc(probs_turned, 1)

                def apply(n):
                    i, p = units[n]
                    u = u0 + n
                    grp = GROUP0[name] + n // gsize
                    pe.wait_ge(probsT_done, u + 1)
                    if n % gsize == 0 and n // gsize >= 2:
                        pe.wait_ge(pv_taken, grp - 1)
                    nk = keys(i) // P
                    for j in range(2):
                        m = score_map(name, p, j)
                        at = m % (2 * gsize) * dv
                        vc = (m // 2 if name == "diff" else m) * dv
                        for kt in range(nk):
                            last = pe.matmul(psum[:, 6 + grp % 2, at:at + dv],
                                             probsT[:, u % 2, (2 * j + kt) * P:(2 * j + kt) * P + P],
                                             v[:, kt, vc:vc + dv], start=kt == 0, stop=kt == nk - 1)
                    if n % gsize == gsize - 1:
                        last.then_inc(pv_done, 1)

                pe.wait_ge(q_out, QKT0[name] + QKT_BANKS[name])
                pe.wait_ge(k_out, QKT0[name] + QKT_BANKS[name])
                pe.wait_ge(proj_out0, PROJ_AT[last_proj] + 1)
                pe.wait_ge(proj_out1, PROJ_AT[last_proj] + 1)
                score(0)
                score(1)
                for n in range(len(units)):
                    if n + 2 < len(units):
                        score(n + 2)
                    turn_probs(n)
                    if n >= 1:
                        apply(n - 1)
                apply(len(units) - 1)

            def small(bank, w, columns_):
                for t in range(NT):
                    for k in range(KD):
                        for part in (x_hi, x_lo):
                            last = pe.matmul(psum[:, bank, t * 64:t * 64 + columns_],
                                             part[:, t, k, :].bitcast(F32), w[:, k, :],
                                             start=k == 0 and part is x_hi, stop=k == KD - 1 and part is x_lo)
                last.then_inc(logits_done, 1)

            pe.wait_ge(const_landed, 16)
            turn("mix")
            input_ready("mix")
            pe.wait_ge(mixw_landed, 16 * MIX_LOADS)
            small(4, w_small, 24)
            projection("gg")
            pe.wait_ge(logits_out, 1)
            for t in range(NT):
                last = pe.transpose(psum[0:16, 5, t * P:t * P + P], lg[:, t, 8:24], ident)
            last.then_inc(ga_turned, 1)
            projection("gqk")
            pe.wait_ge(ga_out, 1)
            for t in range(NT):
                last = pe.matmul(psum[:, 6, t * S:t * S + S], gaT[0:16, t * P:t * P + P], w_alpha[0:16, :],
                                 start=True, stop=True)
            last.then_inc(alpha_done, 1)
            pe.wait_ge(proj_out0, 2)
            pe.wait_ge(proj_out1, 2)
            qk_turn("gla", gqk[:, :, 0:256], gqk[:, :, 256:512])
            projection("gv")
            pe.wait_ge(logsig_done, 1)
            pe.wait_ge(q_out, 1)
            for t in range(NT):
                for f in range(2):
                    last = pe.matmul(psum[:, 4, f * S + t * P:f * S + t * P + P],
                                     lg[:, t, 8 + f * P:8 + f * P + P], cum, start=True, stop=True)
            last.then_inc(decay_done, 1)
            pe.wait_ge(k_out, 1)
            for t in range(NT):
                last = pe.matmul(psum[:, 5, t * S:t * S + S], suf, lg[:, t, 8:264], start=True, stop=True)
            last.then_inc(decay_done, 1)
            pe.matmul(psum[0:8, 7, 0:P], lg[:, 0, 0:8], tri, start=True, stop=True)
            pe.matmul(psum[0:8, 7, P:S], lg[:, 0, 0:8], ones, start=True, stop=False)
            pe.matmul(psum[0:8, 7, P:S], lg[:, 1, 0:8], tri, start=False, stop=True).then_inc(decay_done, 1)
            projection("fq")
            pe.wait_ge(ks_ready, 1)
            pe.wait_ge(ct_out, 1)
            pe.wait_ge(proj_out0, 3)
            for c in range(3):
                r = slice((c % 2) * 64, (c % 2) * 64 + 64)
                for h in range(4):
                    at = (c // 2) * 256 + (h // 2) * P
                    last = pe.matmul(psum[(h % 2) * 64:(h % 2) * 64 + 64, 6 + c % 2, at:at + P],
                                     gks[r, c // 2, h * 64:h * 64 + 64], gv[r, c // 2, h * P:h * P + P],
                                     start=True, stop=True)
            last.then_inc(u_done, 1)

            def level(l):
                if l < LEVELS:
                    pe.wait_ge(z_ready, l + 1)
                if l == 0:
                    pe.wait_ge(gb_out, 1)
                    pe.wait_ge(suffix_out, 1)
                if l == 1:
                    pe.wait_ge(state_ready, 1)
                if l >= 2:
                    pe.wait_ge(level_out, l - 1)
                for t in range(NT):
                    for h in range(4):
                        r = slice((h % 2) * 64, (h % 2) * 64 + 64)
                        c = slice((h // 2) * S + t * P, (h // 2) * S + t * P + P)
                        lhs, rhs = (gz[r, l % 2, c], gz[r, l % 2, c]) if l < LEVELS else (gkT[r, c], gqT[r, c])
                        at = t * 256 + (h // 2) * P
                        last = pe.matmul(psum[:, 4 + 2 * (l % 2) + h % 2, at:at + P], lhs, rhs,
                                         start=True, stop=True)
                last.then_inc(level_done, 1)

            level(0)
            level(1)
            projection("fk")
            level(2)
            level(3)
            projection("fv")
            level(4)
            level(5)
            level(6)
            pe.wait_ge(level_out, LEVELS + 1)
            pe.wait_ge(qb_ready, 1)
            for h in (0, 2, 1, 3):
                r = slice((h % 2) * 64, (h % 2) * 64 + 64)
                for t in range(NT):
                    at = slice(t * 256 + (h // 2) * P, t * 256 + (h // 2) * P + P)
                    last = pe.matmul(psum[:, 6 + h % 2, at], at_[:, t, h, :], gv[:, t, h * P:h * P + P],
                                     start=True, stop=False, skip_group_check=True)
                    for c in range(2 * t, 2 * t + 2):
                        if c == 0:
                            continue
                        q = slice((h // 2) * S + c * 64, (h // 2) * S + c * 64 + 64)
                        last = pe.matmul(psum[(c % 2) * 64:(c % 2) * 64 + 64, 6 + h % 2, at],
                                         gs[r, q], st[r, c - 1, h // 2, :], start=False, stop=True,
                                         skip_group_check=True)
            last.then_inc(gla_o_done, 1)
            pe.wait_ge(gla_o_out, 1)
            pe.wait_ge(proj_out0, 6)
            pe.wait_ge(proj_out1, 6)
            qk_turn("fox", fq, fk)
            attention("fox", fqT, fkT, fv, probs_1, probsT_1, 64, "fv")
            turn("mix_y")
            input_ready("mix_y")
            out_projection("mix_out")

            turn("mem")
            input_ready("mem")
            projection("xk")
            projection("xv")
            pe.wait_ge(proj_out0, 8)
            pe.wait_ge(proj_out1, 8)
            turn("cross")
            input_ready("cross")
            projection("xq")
            pe.wait_ge(proj_out0, 9)
            pe.wait_ge(proj_out1, 9)
            qk_turn("cross", xq, xk)
            attention("cross", xqT, xkT, xv, probs_1, probsT_1, P, "xq")
            turn("cross_y")
            input_ready("cross_y")
            out_projection("cross_out")

            turn("moe")
            input_ready("moe")
            pe.wait_ge(router_landed, 16 * 4)
            pe.wait_ge(zeros_ready, 1)
            small(4, w_router, 20)
            pe.wait_ge(logits_out, 2)
            swiglu("moe")

            turn("ffn1_0")
            input_ready("ffn1_0")
            swiglu("ffn1_0")
            turn("diff")
            input_ready("diff")
            for name in PROJ[9:15]:
                projection(name)
            pe.wait_ge(rope_done, 2)
            qk_turn("diff", q2, y)
            attention("diff", q2T, k2T, v2, probs_2, probsT_2, 64, "dv1")
            turn("diff_y")
            input_ready("diff_y")
            out_projection("diff_out")
            turn("ffn2_0")
            input_ready("ffn2_0")
            swiglu("ffn2_0")
            turn("ffn1_1")
            input_ready("ffn1_1")
            swiglu("ffn1_1")
            turn("na")
            input_ready("na")
            for name in PROJ[15:21]:
                projection(name)
            pe.wait_ge(proj_out0, 21)
            pe.wait_ge(proj_out1, 21)
            qk_turn("na", q2, y)
            attention("na", q2T, k2T, v2, probs_2, probsT_2, 64, "nv1")
            turn("na_y")
            input_ready("na_y")
            out_projection("na_out")
            turn("ffn2_1")
            input_ready("ffn2_1")
            swiglu("ffn2_1")

        def outlets(name, t):
            r, q = (lambda n: rstd[:, NORM_AT[n], t:t + 1]), (lambda n: rstd_q[:, SCALED.index(n), t:t + 1])
            half = int(name[-1]) * 512 if name[-1] in "01" else 0
            return {
                "gg": lambda: [(0, 512, gg[:, t, :], r("mix"))],
                "gqk": lambda: [(0, 256, gqk[:, t, 0:256], q("mix")), (256, 512, gqk[:, t, 256:512], r("mix"))],
                "gv": lambda: [(0, 512, gv[:, t, :], r("mix"))],
                "fq": lambda: [(0, 512, fq[:, t, :], q("mix"))],
                "fk": lambda: [(0, 512, fk[:, t, :], r("mix"))],
                "fv": lambda: [(0, 512, fv[:, t, :], r("mix"))],
                "xk": lambda: [(0, 512, xk[:, t, :], r("mem"))],
                "xv": lambda: [(0, 512, xv[:, t, :], r("mem"))],
                "xq": lambda: [(0, 512, xq[:, t, :], q("cross"))],
                "dq": lambda: [(0, 512, q2[:, t, half:half + 512], q("diff"))],
                "dk": lambda: [(0, 512, y[:, t, half:half + 512], r("diff"))],
                "dv": lambda: [(0, 512, v2[:, t, half:half + 512], r("diff"))],
                "nq": lambda: [(0, 512, q2[:, t, half:half + 512], q("na"))],
                "nk": lambda: [(0, 512, y[:, t, half:half + 512], r("na"))],
                "nv": lambda: [(0, 512, v2[:, t, half:half + 512], r("na"))],
            }[name.rstrip("01")]()

        def norm_of(name):
            return {"x": "mem" if name in ("xk", "xv") else "cross", "d": "diff", "n": "na"}.get(name[0], "mix")

        def row(vector, n):
            return vector.unsqueeze(0).to_broadcast([P, n])

        def gain_row(name):
            own = {"mix": "mix_norm", "cross": "cross_norm", "moe": "moe_norm"}
            if name in own:
                return a[own[name]][0]
            if name in ("mem", "final"):
                return a[name + "_norm"]
            layer = {"diff": 0, "na": 1}.get(name.split("_")[0])
            which = 2
            if layer is None:
                layer, which = int(name.split("_")[1]), 0 if name[3] == "1" else 4
            return a["norm_g_2"][layer, which + name.endswith("_p")]

        @block.scalar
        def _(act):
            ahead, gains, squares = [0], [0], [0]

            def hi(n, it=None):
                act.wait_ge(raw_landed[n % RAW], shifted(32 * (n // RAW + 1), it, 32))
                if n >= SPLIT:
                    act.wait_ge(weights_used, shifted(n - SPLIT + 1, it, 6))
                act.activation(w_hi[:, n % SPLIT, :], raw[:, n % RAW, :], ACT.Copy).then_inc(hi_done, 1)

            def split_through(n):
                while ahead[0] <= min(n, CHUNKS - 1):
                    hi(ahead[0])
                    ahead[0] += 1

            def load_gains(through):
                while gains[0] <= min(through, len(NORMS) - 1):
                    i = gains[0]
                    if i >= 2:
                        act.wait_ge(gain_used, i - 1)
                    act.dma_start(gain[:, i % 2, :], row(gain_row(NORMS[i]), D)).then_inc(gain_landed[i % 2], 16)
                    gains[0] += 1

            def square(name, t, src):
                if squares[0]:
                    act.wait_ge(squared, squares[0])
                squares[0] += 1
                act.activation(junk, src, ACT.Square, accum_out=sums[:, NORM_AT[name], t:t + 1]).then_inc(squared, 1)

            def take_turns(name, t=None):
                banks = TURN_BANKS[name]
                for i in range(banks):
                    tt, kk = divmod(i, banks // NT)
                    if t is not None and tt != t:
                        continue
                    act.wait_ge(turned, TURN_BASE[name] + i + 1)
                    act.activation(x_hi[:, tt, 4 * kk:4 * kk + 4, :], psum[:, i, :].rearrange("p (k c) -> p k c", k=4),
                                   ACT.Copy).then_inc(turn_hi, 1)

            def norm_turn(name, src):
                for t in range(NT):
                    square(name, t, src[:, t, :])
                    take_turns(name, t)
                load_gains(NORM_AT[name] + 2)

            def take_projection(name):
                j, n = PROJ_AT[name], PROJ_CHUNK[name]
                split_through(n + 3)
                act.wait_ge(proj_t0, j + 1)
                act.wait_ge(rstdq_ready, SCALED.index("mix" if norm_of(name) == "mem" else norm_of(name)) + 1)
                act.wait_ge(rstd_ready, NORM_AT[norm_of(name)] + 1)
                for t in range(NT if name == "gg" else 1):
                    if t == 1:
                        act.wait_ge(weights_used, n + 2)
                    for c0, c1, dst, scale in outlets(name, t):
                        last = act.activation(dst, psum[:, 2 * (j % 2) + t, c0:c1],
                                              ACT.Silu if name == "gg" else ACT.Copy, scale=scale)
                    last.then_inc(proj_out0 if t == 0 else proj_out1, 1)

            def take_q(name, dst):
                for b in range(QKT_BANKS[name]):
                    act.wait_ge(qk_turned, 2 * (QKT0[name] + b) + 1)
                    act.activation(dst[:, 512 * b:512 * b + 512], psum[:, 4 + 2 * ((QKT0[name] + b) % 2), :],
                                   ACT.Copy).then_inc(q_out, 1)

            def attention(name, probs):
                u0 = UNIT0[name]
                for n in range(NT * PAIRS[name]):
                    u, i = u0 + n, n // PAIRS[name]
                    keys = (i + 1) * P if name == "fox" else S
                    act.wait_ge(max_done, u + 1)
                    if n >= 3:
                        act.wait_ge(probs_turned, u - 2)
                    for j in range(2):
                        p_ = probs[:, u % 3, j, 0:keys]
                        src = p_ if name in ("fox", "na") else psum[:, u % 4, j * S:j * S + keys]
                        last = act.activation(p_, src, ACT.Exp, bias=negmax[:, u % 3, j:j + 1],
                                              accum_out=rows[:, u, j:j + 1])
                    last.then_inc(probs_done, 1)

            def square_sum(name, total):
                last = START[total] + dict(PHASES)[total] - 1
                split_through(last + 2)
                act.wait_ge(sum_t0, SUM_AT[total] + 1)
                square(name, 0, psum[:, 4:6, :].rearrange("p b c -> p (b c)"))
                act.wait_ge(weights_used, last + 1)
                square(name, 1, psum[:, 6:8, :].rearrange("p b c -> p (b c)"))

            def residual_squares(name, count):
                for t in range(NT):
                    act.wait_ge(resid_done, count + t + 1)
                    square(name, t, x[:, t, :])

            def norm_turn_resid(name, count):
                for t in range(NT):
                    act.wait_ge(resid_done, count + t + 1)
                    square(name, t, x[:, t, :])
                    take_turns(name, t)
                load_gains(NORM_AT[name] + 2)

            def swiglu(name):
                base, groups, gu0 = START[name], FFN[name], GU0[name]

                def gated(n, g, it=None):
                    par = (gu0 + g) % 2
                    for t in range(NT):
                        if t == 0:
                            act.wait_ge(gu_t0, shifted(gu0 + g + 1, it, 2))
                        else:
                            act.wait_ge(weights_used, shifted(n + 2, it, 6))
                        act.activation(silu[:, par, t, :], psum[:, 2 * par + t, 0:GROUP], ACT.Silu,
                                       scale=rstd[:, NORM_AT[name], t:t + 1]).then_inc(silu_done, 1)

                def take_hidden(g, it=None):
                    par = (gu0 + g) % 2
                    act.wait_ge(hid_turned, shifted(gu0 + g + 1, it, 2))
                    act.activation(h_hi[:, par, :, :], psum[:, 2 * par, :].rearrange("p (f s) -> p f s", f=2),
                                   ACT.Copy).then_inc(hid_hi, 1)

                def split(n, it):
                    if n < CHUNKS:
                        hi(n, it)

                def step(n, g, it=None):
                    split(n + 2, it)
                    take_hidden(g, it)
                    split(n + 3, it)
                    gated(n, g + 1, it)
                    split(n + 4, it)

                split_through(base + 3)
                act.wait_ge(rstd_ready, NORM_AT[name] + 1)
                gated(base, 0)
                peel = name == "ffn2_1"
                with act.Fori(0, (groups - 1) // 2 - peel) as it:
                    step(base + 2, 0, it)
                    step(base + 5, 1, it)
                for g in range((groups - 1) // 2 * 2 - 2 * peel, groups - 1):
                    step(base + 2 + 3 * g, g)
                ahead[0] = base + 3 * groups + 1
                take_hidden(groups - 1)

            load_gains(1)
            act.dma_start(w_small[:, :, 0:8], w_in[:, 1536:1544].rearrange("(k p) c -> p k c", p=P)).then_inc(mixw_landed, 16)
            act.dma_start(w_small[:, :, 8:24], w_in[:, 3080:3096].rearrange("(k p) c -> p k c", p=P)).then_inc(mixw_landed, 16)
            act.dma_start(bias_g[:, 0:8], row(a["b_forget"][0], 8)).then_inc(mixw_landed, 16)
            act.dma_start(bias_g[:, 8:264], row(a["b_alpha"][0], 256)).then_inc(mixw_landed, 16)
            act.dma_start(w_alpha[0:16, :], a["w_alpha_up"][0]).then_inc(mixw_landed, 16)
            act.dma_start(mixc, a["consts"][:, C_TRI:C_CAUSAL + 2 * P]).then_inc(mixw_landed, 16)
            act.dma_start(mask_words[:, :], a["masks"]).then_inc(mixw_landed, 16)
            act.dma_start(fox_gain, row(a["fox_out_gain"][0], 512)).then_inc(mixw_landed, 16)
            act.dma_start(gla_gain, row(a["gla_out_gain"][0], 512)).then_inc(mixw_landed, 16)
            act.wait_ge(x_landed, 16)
            norm_turn("mix", x)
            take_projection("gg")
            take_projection("gqk")
            take_q("gla", gqT)
            act.wait_ge(logits_in, 1)
            act.activation(lsg, lg, ACT.Abs).then_inc(logsig_abs, 1)
            act.wait_ge(logsig_abs, 1)
            act.activation(lsg, lsg, ACT.Exp, scale=-1.0).then_inc(act_chain, 1)
            act.wait_ge(act_chain, 1)
            act.activation(lsg, lsg, ACT.Ln, bias=1.0).then_inc(logsig_ln, 1)
            take_projection("gv")
            act.wait_ge(decay_done, 2)
            act.activation(gs, psum[:, 5, :], ACT.Exp).then_inc(suffix_out, 1)
            act.wait_ge(decay_done, 3)
            act.wait_ge(gb_out, 1)
            act.activation(gexp, gb, ACT.Exp).then_inc(expb_ready, 1)
            take_projection("fq")

            def decay(l):
                act.wait_ge(diff_ready, l + 1)
                act.activation(ge, ge, ACT.Abs).then_inc(act_chain, 1)
                act.wait_ge(act_chain, l + 2)
                act.activation(ge, ge, ACT.Exp, scale=-1.0).then_inc(decay_exp, 1)

            decay(0)
            decay(1)
            take_projection("fk")
            decay(2)
            decay(3)
            take_projection("fv")
            decay(4)
            decay(5)
            act.wait_ge(gla_o_out, 1)
            take_q("fox", region(4096, 1024))
            attention("fox", probs_1)
            act.wait_ge(turned, TURN_BASE["mix_y"] + 4)
            act.dma_start(mem[:, :, :], a["mem"][0].rearrange("(t p) c -> p t c", p=P)).then_inc(mem_landed, 16)
            act.dma_start(w_router[:, :, 0:4], a["w_router_group"][0].rearrange("(k p) c -> p k c", p=P)).then_inc(router_landed, 16)
            act.dma_start(w_router[:, :, 4:20], a["w_router_expert"][0].rearrange("(k p) c -> p k c", p=P)).then_inc(router_landed, 16)
            act.dma_start(b_router[:, 0:4], row(a["b_router_group"][0], 4)).then_inc(router_landed, 16)
            act.dma_start(b_router[:, 4:20], row(a["b_router_expert"][0], 16)).then_inc(router_landed, 16)
            take_turns("mix_y")
            split_through(START["mix_out"] + 5)
            act.wait_ge(mem_landed, 16)
            norm_turn("mem", mem)
            take_projection("xk")
            take_projection("xv")
            norm_turn_resid("cross", 0)
            take_projection("xq")
            take_q("cross", region(6144, 1024))
            attention("cross", probs_1)
            take_turns("cross_y")
            split_through(START["cross_out"] + 3)
            norm_turn_resid("moe", NT)
            split_through(START["moe"] + 2)
            for t in range(NT):
                g8, top, sc = rt[:, t, 24:32], rt[:, t, 40:48], rt[:, t, 64:80]
                act.wait_ge(route_in, 2 * t + 1)
                act.activation(rt[:, t, 80:84], g8[:, 0:4], ACT.Exp, bias=sc[:, 0:1], accum_out=sc[:, 1:2]).then_inc(route_exp, 1)
                act.wait_ge(route_in, 2 * t + 2)
                act.activation(sc[:, 3:4], sc[:, 2:3], ACT.Exp).then_inc(route_exp, 1)
            swiglu("moe")
            split_through(START["moe"] + 3 * MOE_GROUPS + 1)
            residual_squares("final", 2 * NT)
            norm_turn_resid("ffn1_0", 3 * NT)
            act.dma_start(subln, row(a["diff_subln_2"][0], P)).then_inc(diffw_landed, 16)
            act.dma_start(lamv, row(a["diff_lambda_2"][0].rearrange("a b -> (a b)"), 256)).then_inc(diffw_landed, 16)
            act.dma_start(namask, a["consts"][:, C_NAMASK:C_END]).then_inc(namask_landed, 16)
            act.wait_ge(lam_sum, 1)
            act.activation(lams[:, 2:4], lams[:, 0:2], ACT.Exp).then_inc(lam_exp, 1)
            swiglu("ffn1_0")
            square_sum("ffn1_0_p", "ffn1_0")
            norm_turn_resid("diff", 4 * NT)
            for name in PROJ[9:15]:
                take_projection(name)
            take_q("diff", region(2560, 2048))
            attention("diff", probs_2)
            take_turns("diff_y")
            square_sum("diff_p", "diff_out")
            norm_turn_resid("ffn2_0", 5 * NT)
            act.dma_start(region(6656, 6144), a["na_biases"]).then_inc(nab_landed, 16)
            swiglu("ffn2_0")
            square_sum("ffn2_0_p", "ffn2_0")
            norm_turn_resid("ffn1_1", 6 * NT)
            swiglu("ffn1_1")
            square_sum("ffn1_1_p", "ffn1_1")
            norm_turn_resid("na", 7 * NT)
            for name in PROJ[15:21]:
                take_projection(name)
            take_q("na", region(2560, 2048))
            attention("na", probs_2)
            take_turns("na_y")
            square_sum("na_p", "na_out")
            norm_turn_resid("ffn2_1", 8 * NT)
            swiglu("ffn2_1")
            square_sum("ffn2_1_p", "ffn2_1")

        @block.vector
        def _(dve):
            ahead, chained, resid = [0], [0], [0]

            def lo(n, it=None):
                dve.wait_ge(hi_done, shifted(n + 1, it, 6))
                dve.tensor_tensor(w_lo[:, n % SPLIT, 0:LO_V], raw[:, n % RAW, 0:LO_V],
                                  w_hi[:, n % SPLIT, 0:LO_V].bitcast(F32), ALU.subtract).then_inc(lo_v_done, 1)

            def split_through(n):
                while ahead[0] <= min(n, CHUNKS - 1):
                    lo(ahead[0])
                    ahead[0] += 1

            def link(ins):
                chained[0] += 1
                ins.then_inc(dve_chain, 1)
                dve.wait_ge(dve_chain, chained[0])

            def scaled(name, src):
                i = NORM_AT[name]
                dve.wait_ge(gain_landed[i % 2], 16 * (i // 2 + 1))
                if TURN_BASE[name]:
                    dve.wait_ge(turned, TURN_BASE[name])
                for t in range(NT):
                    ins = dve.tensor_tensor(y[:, t, :], src[:, t, :], gain[:, i % 2, :], ALU.mult)
                    ins.then_inc(turn_src, 1)
                dve.wait_ge(turn_src, NT * TURN_AT[name] + NT)
                dve.sem_inc(gain_used, 1)

            def take_turns(name):
                banks = TURN_BANKS[name]
                for i in range(banks):
                    t, kk = divmod(i, banks // NT)
                    dve.wait_ge(turn_hi, TURN_BASE[name] + i + 1)
                    xh = x_hi[:, t, 4 * kk:4 * kk + 4, :].bitcast(F32)
                    dve.tensor_tensor(x_lo[:, t, 4 * kk:4 * kk + 4, :], psum[:, i, :].rearrange("p (k c) -> p k c", k=4),
                                      xh, ALU.subtract).then_inc(turn_lo, 1)

            def take_projection(name):
                j, n = PROJ_AT[name], PROJ_CHUNK[name]
                split_through(n + 3)
                if name == "gg":
                    return
                dve.wait_ge(weights_used, n + 2)
                dve.wait_ge(rstdq_ready, SCALED.index("mix" if norm_of(name) == "mem" else norm_of(name)) + 1)
                dve.wait_ge(rstd_ready, NORM_AT[norm_of(name)] + 1)
                if j == 1:
                    dve.wait_ge(proj_out1, 1)
                for c0, c1, dst, scale in outlets(name, 1):
                    last = dve.tensor_scalar(dst, psum[:, 2 * (j % 2) + 1, c0:c1], scale, None, ALU.mult)
                last.then_inc(proj_out1, 1)

            def take_k(name, dst):
                for b in range(QKT_BANKS[name]):
                    dve.wait_ge(qk_turned, 2 * (QKT0[name] + b) + 2)
                    dve.tensor_copy(dst[:, 512 * b:512 * b + 512],
                                    psum[:, 5 + 2 * ((QKT0[name] + b) % 2), :]).then_inc(k_out, 1)

            def attention(name, probs, probsT, take_group):
                pairs, gsize, u0 = PAIRS[name], GSIZE[name], UNIT0[name]
                units = NT * pairs
                masked = name in ("fox", "na")

                def keys(n):
                    return (n // pairs + 1) * P if name == "fox" else S

                def maxima(n):
                    u, i = u0 + n, n // pairs
                    dve.wait_ge(scores, u + 1)
                    nm = negmax[:, u % 3, :]
                    if not masked:
                        dve.tensor_reduce(nm, psum[:, u % 4, :].rearrange("p (m k) -> p m k", m=2), AX.X,
                                          ALU.max, negate=True).then_inc(max_done, 1)
                        return
                    if n >= 3:
                        dve.wait_ge(probs_turned, u - 2)
                    if u:
                        dve.wait_ge(max_done, u)
                    for j in range(2):
                        m = score_map(name, n % pairs, j)
                        if name == "fox":
                            mask = causal[:, P - i * P:2 * P]
                        else:
                            mask = nab[:, m, 2 - 2 * i:6 - 2 * i, :].rearrange("p r c -> p (r c)")
                        last = dve.tensor_tensor_reduce(probs[:, u % 3, j, 0:keys(n)], psum[:, u % 4, j * S:j * S + keys(n)],
                                                        mask, 1.0, LOWEST, ALU.add, ALU.max, rrow[:, 6 + j:7 + j])
                    link(last)
                    dve.tensor_scalar(nm, rrow[:, 6:8], -1.0, None, ALU.mult).then_inc(max_done, 1)

                def copy_turned(n):
                    u = u0 + n
                    dve.wait_ge(probs_turned, u + 1)
                    src, dst = psum[:, 4 + u % 2, :], probsT[:, u % 2, :]
                    if keys(n) < S:
                        src, dst = (z.rearrange("p (m k) -> p m k", m=2)[:, :, 0:P] for z in (src, dst))
                    dve.tensor_copy(dst, src).then_inc(probsT_done, 1)

                maxima(0)
                maxima(1)
                for n in range(units):
                    if n + 2 < units:
                        maxima(n + 2)
                    copy_turned(n)
                    if n >= 1 and n % gsize == 0:
                        take_group(n // gsize - 1)
                take_group(units // gsize - 1)

            def weighted(name, dst):
                def take(g):
                    gsize, grp = GSIZE[name], GROUP0[name] + g
                    heads = 2 * gsize
                    dve.wait_ge(pv_done, grp + 1)
                    u = UNIT0[name] + g * gsize
                    r_ = rheads[:, 0:heads]
                    if name == "cross":
                        link(dve.reciprocal(r_, rows[:, u:u + gsize, :].rearrange("p u m -> p (u m)")))
                    else:
                        link(dve.reciprocal(r_.rearrange("p (r j h) -> p r j h", r=2, j=2),
                                            rows[:, u:u + gsize, :].rearrange("p (r h) j -> p r j h", r=2)))
                    last = dve.tensor_tensor(dst(g).rearrange("p (h d) -> p h d", h=heads),
                                             psum[:, 6 + grp % 2, :].rearrange("p (h d) -> p h d", h=heads),
                                             r_.unsqueeze(2).to_broadcast([P, heads, 512 // heads]), ALU.mult)
                    link(last)
                    dve.sem_inc(pv_taken, 1)
                return take

            def take_diff(g):
                grp = GROUP0["diff"] + g
                i, h = divmod(2 * g, 8)
                dve.wait_ge(pv_done, grp + 1)
                u = UNIT0["diff"] + 2 * g
                link(dve.reciprocal(rrow[:, 0:4].rearrange("p (j h) -> p j h", j=2), rows[:, u:u + 2, :].rearrange("p h j -> p j h")))
                link(dve.tensor_scalar(rrow[:, 4:6], rrow[:, 0:4].rearrange("p (h m) -> p h m", m=2)[:, :, 1],
                                       lams[:, 5:6], None, ALU.mult))
                for k in range(2):
                    pv = psum[:, 6 + grp % 2, :]
                    link(dve.tensor_scalar(ropet[:, 0:P], pv[:, 256 * k:256 * k + P], rrow[:, 2 * k:2 * k + 1], None, ALU.mult))
                    link(dve.scalar_tensor_tensor(y[:, i, (h + k) * P:(h + k) * P + P], pv[:, 256 * k + P:256 * k + 2 * P],
                                                  rrow[:, 4 + k:5 + k], ropet[:, 0:P], ALU.mult, ALU.add))
                dve.sem_inc(pv_taken, 1)

            def head_norm(name, view, tmp, heads, gain_, more=None):
                k = HEADNORMS.index(name)
                d = view.shape[3]
                link(dve.tensor_tensor(tmp, view, view, ALU.mult))
                dve.tensor_reduce(hsum[:, 0:NT * heads].rearrange("p (t h) -> p t h", t=NT), tmp, AX.X, ALU.add).then_inc(head_sums, 1)
                dve.wait_ge(head_rstd, k + 1)
                r_ = hrstd[:, 0:NT * heads].rearrange("p (t h) -> p t h", t=NT)
                link(dve.tensor_tensor(view, view, r_.unsqueeze(3).to_broadcast([P, NT, heads, d]), ALU.mult))
                if more is not None:
                    link(dve.tensor_tensor(view, view, more, ALU.mult))
                return dve.tensor_tensor(view, view, gain_, ALU.mult)

            def residual(total):
                last = START[total] + dict(PHASES)[total] - 1
                split_through(last + 2)
                for t in range(NT):
                    if t == 0:
                        dve.wait_ge(sum_t0, SUM_AT[total] + 1)
                    else:
                        dve.wait_ge(weights_used, last + 1)
                    dve.tensor_tensor(x[:, t, :], psum[:, 4 + 2 * t:6 + 2 * t, :].rearrange("p b c -> p (b c)"),
                                      x[:, t, :], ALU.add).then_inc(resid_done, 1)
                    resid[0] += 1
                dve.wait_ge(resid_done, resid[0])

            def residual_norm(name, total):
                i, last = NORM_AT[name], START[total] + dict(PHASES)[total] - 1
                split_through(last + 2)
                dve.wait_ge(rstd_ready, i + 1)
                dve.wait_ge(gain_landed[i % 2], 16 * (i // 2 + 1))
                for t in range(NT):
                    link(dve.scalar_tensor_tensor(y[:, t, :], psum[:, 4 + 2 * t:6 + 2 * t, :].rearrange("p b c -> p (b c)"),
                                                  rstd[:, i, t:t + 1], gain[:, i % 2, :], ALU.mult, ALU.mult))
                    dve.tensor_tensor(x[:, t, :], x[:, t, :], y[:, t, :], ALU.add).then_inc(resid_done, 1)
                    resid[0] += 1
                dve.wait_ge(resid_done, resid[0])
                dve.sem_inc(gain_used, 1)

            def swiglu(name):
                base, groups, gu0 = START[name], FFN[name], GU0[name]

                def hidden(g, it=None):
                    par = (gu0 + g) % 2
                    for t in range(NT):
                        if name == "moe":
                            e = bass.ds(it + g // 2, 1) if it is not None else slice(g // 2, g // 2 + 1)
                            scale = gates[:, t, e]
                        else:
                            scale = rstd[:, NORM_AT[name], t:t + 1]
                        dve.wait_ge(silu_done, shifted(NT * (gu0 + g) + t + 1, it, 2 * NT))
                        dve.scalar_tensor_tensor(hid[:, par, t, :], psum[:, 2 * par + t, GROUP:2 * GROUP], scale,
                                                 silu[:, par, t, :], ALU.mult, ALU.mult).then_inc(hid_done, 1)

                def take_hidden(g, it=None):
                    par = (gu0 + g) % 2
                    dve.wait_ge(hid_hi, shifted(gu0 + g + 1, it, 2))
                    dve.tensor_tensor(h_lo[:, par, :, :], psum[:, 2 * par, :].rearrange("p (f s) -> p f s", f=2),
                                      h_hi[:, par, :, :].bitcast(F32), ALU.subtract).then_inc(hid_lo, 1)

                def split(n, it):
                    if n < CHUNKS:
                        lo(n, it)

                def step(n, g, it=None):
                    split(n + 2, it)
                    take_hidden(g, it)
                    split(n + 3, it)
                    hidden(g + 1, it)
                    split(n + 4, it)

                split_through(base + 3)
                hidden(0)
                peel = name == "ffn2_1"
                with dve.Fori(0, (groups - 1) // 2 - peel) as it:
                    step(base + 2, 0, it)
                    step(base + 5, 1, it)
                for g in range((groups - 1) // 2 * 2 - 2 * peel, groups - 1):
                    step(base + 2 + 3 * g, g)
                ahead[0] = base + 3 * groups + 1
                take_hidden(groups - 1)

            dve.wait_ge(x_landed, 16)
            dve.wait_ge(const_landed, 16)
            scaled("mix", x)
            take_turns("mix")
            split_through(2)
            dve.wait_ge(logits_done, 1)
            dve.wait_ge(mixw_landed, 16 * MIX_LOADS)
            dve.wait_ge(rstd_ready, 1)
            for t in range(NT):
                link(dve.tensor_scalar(lg[:, t, 0:24], psum[:, 4, t * 64:t * 64 + 24], rstd[:, 0, t:t + 1], None, ALU.mult))
            link(dve.tensor_tensor(lg[:, :, 0:8], lg[:, :, 0:8], bias_g[:, 0:8].unsqueeze(1).to_broadcast([P, NT, 8]), ALU.add))
            dve.sem_inc(logits_out, 1)
            take_projection("gg")
            dve.wait_ge(ga_turned, 1)
            dve.tensor_copy(gaT[0:16, :], psum[0:16, 5, 0:S]).then_inc(ga_out, 1)
            take_projection("gqk")
            dve.wait_ge(alpha_done, 1)
            dve.tensor_tensor(lg[:, :, 8:264], psum[:, 6, :].rearrange("p (t c) -> p t c", t=NT),
                              bias_g[:, 8:264].unsqueeze(1).to_broadcast([P, NT, 256]), ALU.add).then_inc(logits_in, 1)
            take_k("gla", gkT)
            dve.wait_ge(logsig_ln, 1)
            dve.scalar_tensor_tensor(lg, lg, 0.0, lsg, ALU.min, ALU.subtract).then_inc(logsig_done, 1)
            take_projection("gv")
            dve.wait_ge(decay_done, 1)
            dve.tensor_copy(gb, psum[:, 4, :]).then_inc(gb_out, 1)
            dve.wait_ge(decay_done, 3)
            dve.tensor_scalar(ct[0:8, :], psum[0:8, 7, 0:S], -1.0, None, ALU.mult).then_inc(ct_out, 1)
            dve.wait_ge(suffix_out, 1)
            dve.wait_ge(proj_out0, 2)
            dve.wait_ge(k_out, 1)
            dve.tensor_tensor(gks, gqk[:, :, 256:512], gs.rearrange("p (t c) -> p t c", t=NT), ALU.mult).then_inc(ks_ready, 1)
            take_projection("fq")
            dve.wait_ge(expb_ready, 1)
            dve.wait_ge(q_out, 1)
            dve.wait_ge(ks_ready, 1)
            dve.tensor_tensor(gs, gqT, gexp, ALU.mult).then_inc(qb_ready, 1)
            dve.wait_ge(u_done, 1)
            u_ = [psum[:, 6, 0:256], psum[:, 7, 0:256], psum[:, 6, 256:512]]
            link(dve.tensor_copy(st[:, 0, :, :], u_[0].rearrange("p (f v) -> p f v", f=2)))
            for c in (1, 2):
                for f in range(2):
                    last = dve.scalar_tensor_tensor(st[:, c, f, :], st[:, c - 1, f, :],
                                                    gexp[:, f * S + c * 64 + 63:f * S + c * 64 + 64],
                                                    u_[c][:, f * P:f * P + P], ALU.mult, ALU.add)
                link(last)
            dve.sem_inc(state_ready, 1)

            def level_start(l):
                h = 1 << l
                if l:
                    dve.wait_ge(z_ready, l)
                v = gb.rearrange("p (n c) -> p n c", c=2 * h)
                dve.tensor_tensor(ge.rearrange("p (n c) -> p n c", c=2 * h), v,
                                  v[:, :, h - 1:h].to_broadcast([P, 512 // (2 * h), 2 * h]), ALU.subtract).then_inc(diff_ready, 1)

            def level_operand(l):
                h = 1 << l
                dve.wait_ge(decay_exp, l + 1)
                if l >= 2:
                    dve.wait_ge(level_done, l - 1)
                v = [z.rearrange("p (n c) -> p n c", c=2 * h) for z in (gz[:, l % 2, :], gkT, gqT, ge)]
                dve.tensor_tensor(v[0][:, :, 0:h], v[1][:, :, 0:h], v[3][:, :, 0:h], ALU.mult)
                dve.tensor_tensor(v[0][:, :, h:2 * h], v[2][:, :, h:2 * h], v[3][:, :, h:2 * h], ALU.mult).then_inc(z_ready, 1)

            def level_take(l):
                dve.wait_ge(level_done, l + 1)
                dve.wait_ge(level_out if l else at_zero, max(l, 1))
                mask = masks[:, l * P:l * P + P].unsqueeze(1).unsqueeze(1).to_broadcast([P, NT, 2, P])
                for h in range(2):
                    last = dve.copy_predicated(at_.rearrange("p t (g h) q -> p t g h q", h=2)[:, :, :, h, :], mask,
                                               psum[:, 4 + 2 * (l % 2) + h, :].rearrange("p (t g q) -> p t g q", t=NT, g=2))
                last.then_inc(level_out, 1)

            dve.wait_ge(gb_out, 1)
            for l in range(LEVELS):
                if l >= 2 and l % 2 == 0:
                    take_projection("fk" if l == 2 else "fv")
                level_start(l)
                if l >= 1:
                    level_take(l - 1)
                level_operand(l)
            level_take(LEVELS - 1)
            level_take(LEVELS)
            dve.wait_ge(gla_o_done, 1)
            for h in range(2):
                dst = y[:, :, 512:1024].rearrange("p t (g h v) -> p t g h v", g=2, h=2)[:, :, :, h, :]
                last = dve.tensor_copy(dst, psum[:, 6 + h, :].rearrange("p (t g v) -> p t g v", t=NT, g=2))
            last.then_inc(gla_o_out, 1)
            take_k("fox", region(6144, 1024))
            attention("fox", probs_1, probsT_1, weighted("fox", lambda g: y[:, g, 0:512]))
            tmp = fb[:, 0:1024].rearrange("p (t c) -> p t c", t=NT)
            h4, h8 = "p t (h d) -> p t h d", "p t (h d) -> p t h d"
            link(head_norm("gla", y[:, :, 512:1024].rearrange(h4, h=4), tmp.rearrange(h4, h=4), 4,
                           gla_gain.rearrange("p (h d) -> p h d", h=4).unsqueeze(1).to_broadcast([P, NT, 4, P]),
                           gg.rearrange(h4, h=4)))
            head_norm("fox", y[:, :, 0:512].rearrange(h8, h=8), tmp.rearrange(h8, h=8), 8,
                      fox_gain.rearrange("p (h d) -> p h d", h=8).unsqueeze(1).to_broadcast([P, NT, 8, 64])).then_inc(turn_src, 2)
            take_turns("mix_y")
            split_through(START["mix_out"] + 5)
            dve.wait_ge(mem_landed, 16)
            scaled("mem", mem)
            take_turns("mem")
            residual("mix_out")
            scaled("cross", x)
            take_projection("xk")
            take_projection("xv")
            take_turns("cross")
            take_projection("xq")
            take_k("cross", region(4096, 1024))
            attention("cross", probs_1, probsT_1, weighted("cross", lambda g: y[:, g, 0:512]))
            dve.sem_inc(turn_src, 2)
            take_turns("cross_y")
            residual("cross_out")
            scaled("moe", x)
            take_turns("moe")
            split_through(START["moe"] + 2)
            dve.wait_ge(logits_done, 2)
            dve.wait_ge(router_landed, 16 * 4)
            dve.wait_ge(rstd_ready, NORM_AT["moe"] + 1)
            link(dve.memset(rt[:, :, 24:40], NEG))
            for t in range(NT):
                link(dve.scalar_tensor_tensor(rt[:, t, 0:20], psum[:, 4, t * 64:t * 64 + 20], rstd[:, NORM_AT["moe"], t:t + 1],
                                              b_router, ALU.mult, ALU.add))
            dve.sem_inc(logits_out, 1)
            for t in range(NT):
                v = rt[:, t, :]
                g8, e8, top, idx, sc = v[:, 24:32], v[:, 32:40], v[:, 40:48], v[:, 48:56].bitcast(U32), v[:, 64:80]
                hot, pick = v[:, 56:60], v[:, 84:92]
                link(dve.tensor_copy(g8[:, 0:4], v[:, 0:4]))
                link(dve.max(top, g8))
                link(dve.max_index(idx, top, g8))
                dve.tensor_scalar(sc[:, 0:1], top[:, 0:1], -1.0, None, ALU.mult).then_inc(route_in, 1)
                link(dve.tensor_copy(sc[:, 4:5], idx[:, 0:1]))
                link(dve.tensor_scalar(hot, iota4, sc[:, 4:5], None, ALU.is_equal))
                link(dve.tensor_scalar(e8[:, 0:4], v[:, 4:8], hot[:, 0:1], None, ALU.mult))
                for g in range(1, 4):
                    link(dve.scalar_tensor_tensor(e8[:, 0:4], v[:, 4 + 4 * g:8 + 4 * g], hot[:, g:g + 1], e8[:, 0:4], ALU.mult, ALU.add))
                link(dve.max(top, e8))
                link(dve.max_index(idx, top, e8))
                dve.tensor_tensor(sc[:, 2:3], top[:, 1:2], top[:, 0:1], ALU.subtract).then_inc(route_in, 1)
                link(dve.tensor_copy(sc[:, 4:6], idx[:, 0:2]))
                dve.wait_ge(route_exp, 2 * t + 2)
                link(dve.tensor_scalar(sc[:, 6:7], sc[:, 3:4], 1.0, None, ALU.add))
                link(dve.tensor_tensor(sc[:, 6:7], sc[:, 6:7], sc[:, 1:2], ALU.mult))
                link(dve.reciprocal(sc[:, 7:8], sc[:, 6:7]))
                link(dve.tensor_tensor(sc[:, 7:8], sc[:, 7:8], rstd[:, NORM_AT["moe"], t:t + 1], ALU.mult))
                link(dve.tensor_tensor(sc[:, 8:9], sc[:, 7:8], sc[:, 3:4], ALU.mult))
                dve.tensor_scalar(pick[:, 0:4], iota4, sc[:, 4:5], sc[:, 7:8], ALU.is_equal, ALU.mult)
                link(dve.tensor_scalar(pick[:, 4:8], iota4, sc[:, 5:6], sc[:, 8:9], ALU.is_equal, ALU.mult))
                link(dve.tensor_tensor(pick[:, 0:4], pick[:, 0:4], pick[:, 4:8], ALU.add))
                for g in range(4):
                    last = dve.tensor_scalar(gates[:, t, 4 * g:4 * g + 4], pick[:, 0:4], hot[:, g:g + 1], None, ALU.mult)
                link(last)
            swiglu("moe")
            residual("moe")
            i = NORM_AT["final"]
            dve.wait_ge(rstd_ready, i + 1)
            dve.wait_ge(gain_landed[i % 2], 16 * (i // 2 + 1))
            for t in range(NT):
                dve.scalar_tensor_tensor(x[:, t, :], x[:, t, :], rstd[:, i, t:t + 1], gain[:, i % 2, :], ALU.mult,
                                         ALU.mult).then_inc(resid_done, 1)
                resid[0] += 1
            dve.wait_ge(resid_done, resid[0])
            dve.sem_inc(gain_used, 1)
            scaled("ffn1_0", x)
            take_turns("ffn1_0")
            dve.wait_ge(diffw_landed, 32)
            for k in range(2):
                last = dve.tensor_tensor_reduce(ropet[:, 64 * k:64 * k + 64], lamv[:, 128 * k:128 * k + 64], lamv[:, 128 * k + 64:128 * k + 128],
                                                1.0, 0.0, ALU.mult, ALU.add, lams[:, k:k + 1])
            last.then_inc(lam_sum, 1)
            dve.wait_ge(lam_exp, 1)
            link(dve.tensor_tensor(lams[:, 4:5], lams[:, 2:3], lams[:, 3:4], ALU.subtract))
            link(dve.tensor_scalar(lams[:, 5:6], lams[:, 4:5], 0.2, -1.0, ALU.add, ALU.mult))
            swiglu("ffn1_0")
            residual_norm("ffn1_0_p", "ffn1_0")
            scaled("diff", x)
            take_turns("diff")
            for name in PROJ[9:15]:
                take_projection(name)
            dve.wait_ge(proj_out0, 15)
            dve.wait_ge(proj_out1, 15)
            for turn_, z in enumerate((q2, y)):
                if turn_:
                    dve.wait_ge(rope_done, 1)
                z4 = z.rearrange("p t (m c) -> p t m c", m=16)
                x1, x2 = z4[:, :, :, 0:8], z4[:, :, :, 8:16]
                cos, sin = (rope[:, :, k, :].unsqueeze(2).to_broadcast([P, NT, 16, 8]) for k in range(2))
                tt = [ropet[:, 256 * k:256 * k + 256].rearrange("p (t m c) -> p t m c", t=NT, m=16) for k in range(4)]
                dve.tensor_tensor(tt[0], x1, cos, ALU.mult)
                dve.tensor_tensor(tt[1], x2, sin, ALU.mult)
                dve.tensor_tensor(tt[2], x2, cos, ALU.mult)
                link(dve.tensor_tensor(tt[3], x1, sin, ALU.mult))
                link(dve.tensor_tensor(x1, tt[0], tt[1], ALU.subtract))
                dve.tensor_tensor(x2, tt[2], tt[3], ALU.add).then_inc(rope_done, 1)
            take_k("diff", region(4608, 2048))
            attention("diff", probs_2, probsT_2, take_diff)
            head_norm("diff", y.rearrange("p t (h d) -> p t h d", h=8), v2.rearrange("p t (h d) -> p t h d", h=8), 8,
                      subln.unsqueeze(1).unsqueeze(1).to_broadcast([P, NT, 8, P])).then_inc(turn_src, 2)
            take_turns("diff_y")
            residual_norm("diff_p", "diff_out")
            scaled("ffn2_0", x)
            take_turns("ffn2_0")
            swiglu("ffn2_0")
            residual_norm("ffn2_0_p", "ffn2_0")
            scaled("ffn1_1", x)
            take_turns("ffn1_1")
            swiglu("ffn1_1")
            residual_norm("ffn1_1_p", "ffn1_1")
            scaled("na", x)
            take_turns("na")
            dve.wait_ge(nab_landed, 16)
            dve.wait_ge(namask_landed, 16)
            for name in PROJ[15:21]:
                take_projection(name)
                if name in PROJ[15:19]:
                    k = PROJ[15:19].index(name)
                    v = nab[:, 4 * k:4 * k + 4, :, :]
                    dve.tensor_tensor(v, v, namask.unsqueeze(1).unsqueeze(1).to_broadcast([P, 4, 6, 64]), ALU.add).then_inc(nab_ready, 1)
            dve.wait_ge(nab_ready, 4)
            take_k("na", region(4608, 2048))
            attention("na", probs_2, probsT_2, weighted("na", lambda g: y[:, g // 2, (g % 2) * 512:(g % 2) * 512 + 512]))
            dve.sem_inc(turn_src, 2)
            take_turns("na_y")
            residual_norm("na_p", "na_out")
            scaled("ffn2_1", x)
            take_turns("ffn2_1")
            swiglu("ffn2_1")
            residual_norm("ffn2_1_p", "ffn2_1")
            dve.sem_inc(out_ready, 2)

        @block.gpsimd
        def _(pool):
            ahead, chained = [0], [0]

            def lo(n, it=None):
                pool.wait_ge(hi_done, shifted(n + 1, it, 6))
                pool.tensor_tensor(w_lo[:, n % SPLIT, LO_V:CHUNK], raw[:, n % RAW, LO_V:CHUNK],
                                   w_hi[:, n % SPLIT, LO_V:CHUNK].bitcast(F32), ALU.subtract).then_inc(lo_p_done, 1)

            def split_through(n):
                while ahead[0] <= min(n, CHUNKS - 1):
                    lo(ahead[0])
                    ahead[0] += 1

            def link(ins):
                chained[0] += 1
                ins.then_inc(pool_chain, 1)
                pool.wait_ge(pool_chain, chained[0])

            def inverse_rms(name):
                i = NORM_AT[name]
                if i:
                    pool.wait_ge(rstd_ready, i)
                pool.wait_ge(squared, NT * (i + 1))
                link(pool.tensor_scalar(vtmp[:, 0:2], sums[:, i, :], 1.0 / D, EPS, ALU.mult, ALU.add))
                last = pool.tensor_tensor(rstd[:, i, :], vtmp[:, 0:2], neghalf[:, 0:2], ALU.pow)
                if name in NORM_FACTOR:
                    link(last)
                    last = pool.tensor_scalar(rstd[:, i, :], rstd[:, i, :], NORM_FACTOR[name], None, ALU.mult)
                last.then_inc(rstd_ready, 1)
                if name in SCALED:
                    pool.wait_ge(rstd_ready, i + 1)
                    pool.tensor_scalar(rstd_q[:, SCALED.index(name), :], rstd[:, i, :], SCORE_SCALE[name], None,
                                       ALU.mult).then_inc(rstdq_ready, 1)

            def inverse_head_rms(name, n, d, factor=None):
                k = HEADNORMS.index(name)
                pool.wait_ge(head_sums, k + 1)
                if k:
                    pool.wait_ge(head_rstd, k)
                link(pool.tensor_scalar(htmp[:, 0:n], hsum[:, 0:n], 1.0 / d, EPS, ALU.mult, ALU.add))
                last = pool.tensor_tensor(hrstd[:, 0:n], htmp[:, 0:n], neghalf[:, 0:n], ALU.pow)
                if factor:
                    link(last)
                    last = pool.tensor_scalar(hrstd[:, 0:n], hrstd[:, 0:n], factor, None, ALU.mult)
                last.then_inc(head_rstd, 1)

            def swiglu(name):
                base, groups = START[name], FFN[name]
                peel = name == "ffn2_1"

                def splits(n, it=None):
                    for k in range(2, 8 if it is not None else 5):
                        if n + k < CHUNKS:
                            lo(n + k, it)

                split_through(base + 3)
                with pool.Fori(0, (groups - 1) // 2 - peel) as it:
                    splits(base + 2, it)
                for g in range((groups - 1) // 2 * 2 - 2 * peel, groups - 1):
                    splits(base + 2 + 3 * g)
                ahead[0] = base + 3 * groups + 1

            pool.memset(zeros[:, :], 0.0).then_inc(zeros_ready, 1)
            pool.wait_ge(const_landed, 16)
            split_through(2)
            inverse_rms("mix")
            pool.memset(fb[:, 1024:2048], 0.0).then_inc(at_zero, 1)
            split_through(START["mix_in"] + 13)
            inverse_head_rms("gla", 8, P)
            inverse_head_rms("fox", 16, 64)
            split_through(START["mix_out"] + 5)
            inverse_rms("mem")
            split_through(START["mem_kv"] + 3 + 2)
            inverse_rms("cross")
            split_through(START["cross_out"] + 3)
            inverse_rms("moe")
            swiglu("moe")
            split_through(START["moe"] + 3 * MOE_GROUPS + 1)
            inverse_rms("final")
            inverse_rms("ffn1_0")
            swiglu("ffn1_0")
            split_through(START["ffn1_0"] + 3 * FF_GROUPS + 1)
            inverse_rms("ffn1_0_p")
            inverse_rms("diff")
            split_through(START["diff_in"] + 13)
            inverse_head_rms("diff", 16, P, 1.0 - (0.8 - 0.6))
            split_through(START["diff_out"] + 5)
            inverse_rms("diff_p")
            inverse_rms("ffn2_0")
            swiglu("ffn2_0")
            split_through(START["ffn2_0"] + 3 * FF_GROUPS + 1)
            inverse_rms("ffn2_0_p")
            inverse_rms("ffn1_1")
            swiglu("ffn1_1")
            split_through(START["ffn1_1"] + 3 * FF_GROUPS + 1)
            inverse_rms("ffn1_1_p")
            inverse_rms("na")
            split_through(START["na_out"] + 5)
            inverse_rms("na_p")
            inverse_rms("ffn2_1")
            swiglu("ffn2_1")
            inverse_rms("ffn2_1_p")


def toeplitz(rpb):
    j, c, s, k = np.ix_(range(2), range(64), range(6), range(64))
    laid = rpb[0][:, 5 - j + s, np.clip(k - c + 15, 0, 30)]
    return np.ascontiguousarray(laid.transpose(1, 2, 0, 3, 4)).reshape(P, 16 * 6 * 64)


_INS = ["x", "mem", "mem_norm", "mix_norm", "w_in", "b_forget", "w_alpha_up", "b_alpha", "fox_out_gain",
        "gla_out_gain", "w_out", "cross_norm", "w_xq", "w_xk", "w_xv", "w_xo", "moe_norm", "w_router_group",
        "b_router_group", "w_router_expert", "b_router_expert", "w_expert_gate", "w_expert_up",
        "w_expert_down", "final_norm", "norm_g_2", "ffn1_wg_2", "ffn1_wu_2", "ffn1_wd_2", "ffn2_wg_2",
        "ffn2_wu_2", "ffn2_wd_2", "diff_w_in_2", "diff_w_out_2", "diff_lambda_2", "diff_subln_2",
        "na_w_in_2", "na_w_out_2"]


def kernel(**inputs):
    import numpy as _np
    import concourse.bacc as _bacc
    from concourse import mybir as _mybir
    from concourse.bass_utils import run_bass_kernel_spmd as _run

    nc = _bacc.Bacc("TRN2", target_bir_lowering=False, num_devices=1)
    consts, masks = shape_constants()
    arrays = {name: _np.ascontiguousarray(inputs[name]) for name in _INS}
    arrays["consts"], arrays["masks"] = consts, masks
    arrays["na_biases"] = toeplitz(_np.asarray(inputs["na_rpb_2"]))
    aps = {}
    for name, v in arrays.items():
        aps[name] = nc.dram_tensor(name, v.shape, _mybir.dt.from_np(v.dtype), kind="ExternalInput").ap()
    out = nc.dram_tensor("out", (1, S, D), _mybir.dt.float32, kind="ExternalOutput").ap()
    two_blocks(nc, aps, out)
    r = _run(nc, [arrays], core_ids=[0])
    return r.results[0]["out"]
```

```python
from contextlib import ExitStack

import numpy as np
import concourse.bass as bass
from concourse import mybir

F32 = mybir.dt.float32
F32R = mybir.dt.float32r
U8 = mybir.dt.uint8
I32 = mybir.dt.int32
U32 = mybir.dt.uint32
ALU = mybir.AluOpType
ACT = mybir.ActivationFunctionType
AX = mybir.AxisListType

P = 128
S = 256
NT = S // P
D = 1024
KD = D // P
EPS = 1e-6
NEG = -1e30
LOWEST = -3e38
CHUNK = 2048
RAW = 6
SPLIT = 3
LO_V = 1280
GROUP = 256
FF_GROUPS = 2816 // GROUP
MOE_GROUPS = 16 * 512 // GROUP
WINDOWS = 4
GLA_C = 64
LEVELS = 6

PHASES = [("mix_in", 12), ("mem_kv", 4), ("mix_out", 4), ("cross_q", 2), ("cross_out", 2),
          ("moe", 3 * MOE_GROUPS), ("ffn1_0", 3 * FF_GROUPS), ("diff_in", 12), ("diff_out", 4),
          ("ffn2_0", 3 * FF_GROUPS), ("ffn1_1", 3 * FF_GROUPS), ("na_in", 12), ("na_out", 4),
          ("ffn2_1", 3 * FF_GROUPS)]
START, _n = {}, 0
for _name, _count in PHASES:
    START[_name] = _n
    _n += _count
CHUNKS = _n

TURNS = ["mix", "mem", "mix_y", "cross", "cross_y", "moe", "ffn1_0", "diff", "diff_y", "ffn2_0",
         "ffn1_1", "na", "na_y", "ffn2_1"]
TURN_AT = {name: i for i, name in enumerate(TURNS)}
TURN_BANKS = {name: 2 if name == "cross_y" else 4 for name in TURNS}
TURN_BASE = {name: sum(TURN_BANKS[x] for x in TURNS[:i]) for i, name in enumerate(TURNS)}

NORMS = ["mix", "mem", "cross", "moe", "final", "ffn1_0", "ffn1_0_p", "diff", "diff_p", "ffn2_0",
         "ffn2_0_p", "ffn1_1", "ffn1_1_p", "na", "na_p", "ffn2_1", "ffn2_1_p"]
NORM_AT = {name: i for i, name in enumerate(NORMS)}
NORM_FACTOR = {"ffn1_0_p": 0.5, "ffn2_0_p": 0.5, "ffn1_1_p": 0.5, "ffn2_1_p": 0.5}
SCORE_SCALE = {"mix": 64 ** -0.5, "cross": 128 ** -0.5, "diff": 64 ** -0.5, "na": 64 ** -0.5}
SCALED = list(SCORE_SCALE)
MIX_LOADS = 9

SUMS = ["mix_out", "cross_out", "ffn1_0", "diff_out", "ffn2_0", "ffn1_1", "na_out", "ffn2_1"]
SUM_AT = {name: i for i, name in enumerate(SUMS)}

PROJ = ["gg", "gqk", "gv", "fq", "fk", "fv", "xk", "xv", "xq", "dq0", "dq1", "dk0", "dk1", "dv0",
        "dv1", "nq0", "nq1", "nk0", "nk1", "nv0", "nv1"]
PROJ_AT = {name: i for i, name in enumerate(PROJ)}
PROJ_CHUNK = {}
for _i, _name in enumerate(PROJ):
    _ph, _first = (("mix_in", 0) if _i < 6 else ("mem_kv", 6) if _i < 8 else ("cross_q", 8) if _i < 9
                   else ("diff_in", 9) if _i < 15 else ("na_in", 15))
    PROJ_CHUNK[_name] = START[_ph] + 2 * (_i - _first)

CORES = ["fox", "cross", "diff", "na"]
PAIRS = {"fox": 4, "cross": 2, "diff": 8, "na": 8}
GSIZE = {"fox": 4, "cross": 2, "diff": 2, "na": 4}
UNIT0 = {"fox": 0, "cross": 8, "diff": 12, "na": 28}
GROUP0 = {"fox": 0, "cross": 2, "diff": 4, "na": 12}


def score_map(name, p, j):
    return 2 * p + j if name == "cross" else 4 * (p // 2) + 2 * j + p % 2


QKT = ["gla", "fox", "cross", "diff", "na"]
QKT_BANKS = {"gla": 1, "fox": 2, "cross": 2, "diff": 4, "na": 4}
QKT0 = {"gla": 0, "fox": 1, "cross": 3, "diff": 5, "na": 9}
HEADNORMS = ["fox", "diff"]

C_IDENT, C_IOTA, C_NEGHALF, C_ROPE = 0, 128, 132, 148
C_TRI, C_ONES, C_CUM, C_SUF, C_CAUSAL = 180, 308, 436, 564, 692
C_NAMASK, C_SLOT, C_END = 948, 1012, 1140


def shape_constants():
    c = np.zeros((P, C_END), np.float32)
    s, t = np.arange(P)[:, None], np.arange(P)[None, :]
    c[:, C_IDENT:C_IDENT + P] = s == t
    c[:, C_IOTA:C_IOTA + 4] = np.arange(4)
    c[:, C_NEGHALF:C_NEGHALF + 16] = -0.5
    inv = np.float32(500000.0) ** (-np.arange(0, 16, 2, dtype=np.float32) / np.float32(16))
    ang = np.arange(S, dtype=np.float32)[:, None] * inv[None, :]
    rope = np.stack([np.cos(ang), np.sin(ang)], 1).astype(np.float32)
    c[:, C_ROPE:C_ROPE + 32] = rope.reshape(NT, P, 16).transpose(1, 0, 2).reshape(P, 32)
    c[:, C_TRI:C_TRI + P] = s <= t
    c[:, C_ONES:C_ONES + P] = 1.0
    same = s // GLA_C == t // GLA_C
    c[:, C_CUM:C_CUM + P] = (same & (s <= t)) / 16.0
    c[:, C_SUF:C_SUF + P] = (same & (s > t)) / 16.0
    c[:, C_CAUSAL + P:C_CAUSAL + 2 * P] = np.where(t > s, NEG, 0.0)
    q, k = np.arange(64)[:, None], np.arange(64)[None, :]
    left = np.clip(q - 8, 0, 48)
    c[:, C_NAMASK:C_NAMASK + 64] = np.tile(np.where((k >= left) & (k < left + 16), 0.0, NEG), (2, 1))
    c[:, C_SLOT:C_SLOT + P] = 1 + np.arange(P)
    m = np.zeros((P, LEVELS + 1, P), np.uint8)
    for l in range(LEVELS):
        h = 1 << l
        m[:, l] = (s // (2 * h) == t // (2 * h)) & (s % (2 * h) < h) & (t % (2 * h) >= h)
    m[:, LEVELS] = s == t
    return c, m.reshape(P, (LEVELS + 1) * P).view(np.int32)


def two_blocks(nc, a, out):
    with ExitStack() as ctx:
        def sb(name, shape, dt=F32):
            return ctx.enter_context(nc.sbuf_tensor("sb_" + name, shape, dt))

        def sem(name):
            return ctx.enter_context(nc.semaphore(name))

        raw = sb("raw", [P, RAW, CHUNK])
        w_hi = sb("w_hi", [P, SPLIT, CHUNK], F32R)
        w_lo = sb("w_lo", [P, SPLIT, CHUNK], F32R)
        x = sb("x", [P, NT, D])
        x_hi = sb("x_hi", [P, NT, KD, P], F32R)
        x_lo = sb("x_lo", [P, NT, KD, P], F32R)
        y = sb("y", [P, NT, D])
        h_hi = sb("h_hi", [P, 2, 2, S], F32R)
        h_lo = sb("h_lo", [P, 2, 2, S], F32R)
        fb = sb("fb", [P, 2048])
        gain = sb("gain", [P, 2, D])
        arena = sb("arena", [P, 12800])
        const = sb("const", [P, C_TRI])
        sums = sb("sums", [P, len(NORMS), NT])
        rstd = sb("rstd", [P, len(NORMS), NT])
        rstd_q = sb("rstd_q", [P, 4, NT])
        vtmp, htmp = sb("vtmp", [P, 2]), sb("htmp", [P, 16])
        hsum = sb("hsum", [P, 16])
        hrstd = sb("hrstd", [P, 16])
        pool_heads = sb("pool_heads", [P, 16])
        negmax = sb("negmax", [P, 3, 2])
        rows = sb("rows", [P, 44, 2])
        rrow = sb("rrow", [P, 8])
        rheads = sb("rheads", [P, 8])
        gates = sb("gates", [P, NT, 17])
        psum = ctx.enter_context(nc.psum_tensor("psum", [P, 8, 512], F32))

        ident = const[:, C_IDENT:C_IDENT + P]
        iota4 = const[:, C_IOTA:C_IOTA + 4]
        neghalf = const[:, C_NEGHALF:C_NEGHALF + 16]
        rope = const[:, C_ROPE:C_ROPE + 32].rearrange("p (t c j) -> p t c j", t=NT, c=2)
        silu = fb[:, 0:1024].rearrange("p (r t f) -> p r t f", r=2, t=NT)
        hid = fb[:, 1024:2048].rearrange("p (r t f) -> p r t f", r=2, t=NT)
        junk = fb[:, 0:D]

        def region(at, n):
            return arena[:, at:at + n]

        fq = region(0, 1024).rearrange("p (t c) -> p t c", t=NT)
        fk = region(1024, 1024).rearrange("p (t c) -> p t c", t=NT)
        fv = region(2048, 1024).rearrange("p (t c) -> p t c", t=NT)
        gg = region(3072, 1024).rearrange("p (t c) -> p t c", t=NT)
        gqk = region(4096, 1024).rearrange("p (t c) -> p t c", t=NT)
        gv = region(5120, 1024).rearrange("p (t c) -> p t c", t=NT)
        gb = region(6144, 512)
        lg = region(6656, 528).rearrange("p (t c) -> p t c", t=NT)
        ge = region(7184, 512)
        gz = region(7696, 1024).rearrange("p (r c) -> p r c", r=2)
        gs = region(8720, 512)
        st = region(9232, 768).rearrange("p (c f v) -> p c f v", c=3, f=2)
        fox_gain = region(10000, 512)
        gla_gain = region(10512, 512)
        bias_g = region(11024, 264)
        w_small = region(11288, 192).rearrange("p (k c) -> p k c", k=KD)
        w_alpha = region(11480, 256)
        mixc = region(11736, C_CAUSAL + 2 * P - C_TRI)
        tri, ones = mixc[:, 0:P], mixc[:, P:2 * P]
        cum, suf, causal = mixc[:, 2 * P:3 * P], mixc[:, 3 * P:4 * P], mixc[:, 4 * P:6 * P]
        mask_words = sb("masks", [P, (LEVELS + 1) * P // 4], I32)
        masks = mask_words[:, :].bitcast(U8)
        zeros = sb("zeros", [P, 512], mybir.dt.bfloat16)
        gaT = region(12504, 256)
        gqT, gkT = fb[:, 0:512], fb[:, 512:1024]
        at_ = fb[:, 1024:2048].rearrange("p (t h q) -> p t h q", t=NT, h=4)
        lsg = region(7696, 528).rearrange("p (t c) -> p t c", t=NT)
        gks = gqk[:, :, 256:512]
        gexp = region(6656, 512)
        fqT = region(4096, 1024).rearrange("p (f s) -> p f s", f=4)
        fkT = region(6144, 1024).rearrange("p (f s) -> p f s", f=4)
        probs_1 = region(7168, 1536).rearrange("p (r m k) -> p r m k", r=3, m=2)
        probsT_1 = region(8704, 1024).rearrange("p (r c) -> p r c", r=2)
        ct = region(12504, 256)
        mem = region(0, 2048).rearrange("p (t c) -> p t c", t=NT)
        xk = region(2048, 1024).rearrange("p (t c) -> p t c", t=NT)
        xv = region(5120, 1024).rearrange("p (t c) -> p t c", t=NT)
        xkT = region(4096, 1024).rearrange("p (f s) -> p f s", f=4)
        xq = region(3072, 1024).rearrange("p (t c) -> p t c", t=NT)
        xqT = region(6144, 1024).rearrange("p (f s) -> p f s", f=4)
        w_router = region(10000, 160).rearrange("p (k c) -> p k c", k=KD)
        b_router = region(10160, 20)
        rt = region(10192, 512).rearrange("p (t c) -> p t c", t=NT)
        slots = region(10704, P)
        pick = region(0, 1024).rearrange("p (w t s) -> p w t s", w=WINDOWS, t=NT)
        pickT = region(1024, 1024).rearrange("p (w t s) -> p w t s", w=WINDOWS, t=NT)
        slot_y = region(2048, 1024)
        slotv = region(3072, 17 * WINDOWS).rearrange("p (w c) -> p w c", w=WINDOWS)
        over_slotv = region(3140, 17)
        over_pick = region(3200, 256).rearrange("p (t s) -> p t s", t=NT)
        over_pickT = region(3456, 256).rearrange("p (t s) -> p t s", t=NT)
        over_x = region(3712, 1024).rearrange("p (k s) -> p k s", k=KD)
        over_w = region(4736, 4096)
        over_silu, over_hidT, over_hid = fb[:, 0:512], fb[:, 512:1024], fb[:, 1024:1536]
        is_over = rt[0:1, 0, 139:140].bitcast(I32)
        over_group = rt[0:1, 0, 128:129].bitcast(I32)
        q2 = region(0, 2048).rearrange("p (t c) -> p t c", t=NT)
        probs_2 = region(0, 1536).rearrange("p (r m k) -> p r m k", r=3, m=2)
        probsT_2 = region(1536, 1024).rearrange("p (r c) -> p r c", r=2)
        q2T = region(2560, 2048).rearrange("p (f s) -> p f s", f=8)
        k2T = region(4608, 2048).rearrange("p (f s) -> p f s", f=8)
        v2 = fb[:, :].rearrange("p (t c) -> p t c", t=NT)
        subln = region(6656, 128)
        lamv = region(6784, 256)
        lams = region(7040, 32)
        ropet = region(7168, 2048)
        nab = region(6656, 6144).rearrange("p (h r c) -> p h r c", h=16, r=6)
        namask = mask_words[:, 0:64].bitcast(F32)

        raw_landed = [sem(f"raw_landed{i}") for i in range(RAW)]
        hi_done, lo_v_done, lo_p_done = sem("hi_done"), sem("lo_v_done"), sem("lo_p_done")
        weights_used = sem("weights_used")
        x_landed, const_landed, mixw_landed, mem_landed = (
            [sem("x_landed0"), sem("x_landed1")], sem("const_landed"), sem("mixw_landed"), sem("mem_landed"))
        router_landed, diffw_landed = sem("router_landed"), sem("diffw_landed")
        nab_landed, namask_landed = sem("nab_landed"), sem("namask_landed")
        gain_landed = [sem("gain_landed0"), sem("gain_landed1")]
        gain_used = sem("gain_used")
        turn_src, turned, turn_hi, turn_lo = sem("turn_src"), sem("turned"), sem("turn_hi"), sem("turn_lo")
        squared, rstd_ready, rstdq_ready = sem("squared"), sem("rstd_ready"), sem("rstdq_ready")
        proj_t0, proj_out0, proj_out1 = sem("proj_t0"), sem("proj_out0"), sem("proj_out1")
        gu_t0, silu_done, hid_done = sem("gu_t0"), sem("silu_done"), sem("hid_done")
        hid_turned, hid_hi, hid_lo = sem("hid_turned"), sem("hid_hi"), sem("hid_lo")
        sum_t0, resid_done = sem("sum_t0"), sem("resid_done")
        qk_turned, q_out, k_out = sem("qk_turned"), sem("q_out"), sem("k_out")
        scores, max_done, probs_done = sem("scores"), sem("max_done"), sem("probs_done")
        probs_turned, probsT_done = sem("probs_turned"), sem("probsT_done")
        pv_done, pv_taken = sem("pv_done"), sem("pv_taken")
        head_sums, head_rstd, heads_normed = sem("head_sums"), sem("head_rstd"), sem("heads_normed")
        logits_done, logits_out = sem("logits_done"), sem("logits_out")
        ga_turned, ga_out, alpha_done, alpha_out = (
            sem("ga_turned"), sem("ga_out"), sem("alpha_done"), sem("alpha_out"))
        logits_in, logsig_abs, logsig_ln, logsig_done = sem("logits_in"), sem("logsig_abs"), sem("logsig_ln"), sem("logsig_done")
        decay_done, gb_out, suffix_out, ct_out = (
            sem("decay_done"), sem("gb_out"), sem("suffix_out"), sem("ct_out"))
        ks_ready, u_done, state_ready, qb_ready, expb_ready = (
            sem("ks_ready"), sem("u_done"), sem("state_ready"), sem("qb_ready"), sem("expb_ready"))
        diff_ready, decay_exp, z_ready, level_done, level_out = (
            sem("level_diff"), sem("level_exp"), sem("z_ready"), sem("level_done"), sem("level_out"))
        at_zero, gla_o_done, gla_o_out = sem("at_zero"), sem("gla_o_done"), sem("gla_o_out")
        route_exp, route_in, gates_ready = sem("route_exp"), sem("route_in"), sem("gates_ready")
        hot_ready, ranked, pick_ready, pick_turned, pickT_out = (
            sem("hot_ready"), sem("ranked"), sem("pick_ready"), sem("pick_turned"), sem("pickT_out"))
        slotv_done, slotv_out = sem("slotv_done"), sem("slotv_out")
        gathered, gathered_hi, gathered_lo = sem("gathered"), sem("gathered_hi"), sem("gathered_lo")
        slot_y_out, scattered, scatter_taken = sem("slot_y_out"), sem("scattered"), sem("scatter_taken")
        over_known, over_in, over_taken, over_landed = (
            sem("over_known"), sem("over_in"), sem("over_taken"), sem("over_landed"))
        over_gate, over_up, over_silued, over_hidden = (
            sem("over_gate"), sem("over_up"), sem("over_silued"), sem("over_hidden"))
        over_turned, over_hidT_out, over_down = sem("over_turned"), sem("over_hidT_out"), sem("over_down")
        over_y_out, over_scattered, over_added = sem("over_y_out"), sem("over_scattered"), sem("over_added")
        rope_done, lam_sum, lam_exp = sem("rope_done"), sem("lam_sum"), sem("lam_exp")
        nab_ready, zeros_ready = sem("nab_ready"), sem("zeros_ready")
        out_ready, out_landed = sem("out_ready"), sem("out_landed")
        dve_chain, act_chain, pool_chain = sem("dve_chain"), sem("act_chain"), sem("pool_chain")

        def columns(w, k0, c0):
            src = w.rearrange("(k p) c -> p k c", p=P)
            return [(slice(1024 * i, 1024 * i + 1024), src[:, k0 + 2 * i:k0 + 2 * i + 2, c0:c0 + 512], 2)
                    for i in range(2)]

        def full_rows(w, k0):
            src = w.rearrange("(k p) c -> p k c", p=P)
            return [(slice(1024 * i, 1024 * i + 1024), src[:, k0 + i:k0 + i + 1, :], 1) for i in range(2)]

        w_in = a["w_in"][0]
        OFF = {"fq": 0, "fk": 512, "fv": 1024, "gqk": 1544, "gv": 2056, "gg": 2568}
        PROJ_SRC = {n: (w_in, OFF[n]) for n in OFF}
        PROJ_SRC |= {"xk": (a["w_xk"][0], 0), "xv": (a["w_xv"][0], 0), "xq": (a["w_xq"][0], 0)}
        for i, n in enumerate(PROJ[9:15]):
            PROJ_SRC[n] = (a["diff_w_in_2"][0], 512 * i)
        for i, n in enumerate(PROJ[15:21]):
            PROJ_SRC[n] = (a["na_w_in_2"][0], 512 * i)
        SUM_SRC = {"mix_out": (a["w_out"][0], 4), "cross_out": (a["w_xo"][0], 2),
                   "diff_out": (a["diff_w_out_2"][0], 4), "na_out": (a["na_w_out_2"][0], 4)}
        FFN = {"moe": MOE_GROUPS, "ffn1_0": FF_GROUPS, "ffn2_0": FF_GROUPS, "ffn1_1": FF_GROUPS,
               "ffn2_1": FF_GROUPS}
        GU0 = {}
        for name in FFN:
            GU0[name] = sum(FFN[m] for m in list(FFN)[:list(FFN).index(name)])

        def swiglu_weights(name):
            if name == "moe":
                return a["w_expert_gate"][0], a["w_expert_up"][0], a["w_expert_down"][0]
            layer, which = int(name[-1]), name[:4]
            return a[which + "_wg_2"][layer], a[which + "_wu_2"][layer], a[which + "_wd_2"][layer]

        def gate_up(name, g, k0, it):
            parts = []
            for i, w in enumerate(swiglu_weights(name)[:2]):
                if name == "moe":
                    src = w[bass.ds(it + g // 2, 1)] if it is not None else w[g // 2:g // 2 + 1]
                    src = src.rearrange("e (k p) c -> p (e k) c", p=P)[:, k0:k0 + 4, GROUP * (g % 2):GROUP * (g % 2) + GROUP]
                else:
                    src = w.rearrange("(k p) c -> p k c", p=P)[:, k0:k0 + 4, :]
                    c = bass.ds(it * (2 * GROUP) + g * GROUP, GROUP) if it is not None else slice(g * GROUP, g * GROUP + GROUP)
                    src = src[:, :, c]
                parts.append((i, src, 4))
            return parts

        def down(name, g, it):
            w = swiglu_weights(name)[2]
            parts = []
            for i in (1, 0):
                if name == "moe":
                    src = w[bass.ds(it + g // 2, 1)] if it is not None else w[g // 2:g // 2 + 1]
                    src = src.rearrange("e (k p) c -> p (e k) c", p=P)[:, 2 * (g % 2) + i:2 * (g % 2) + i + 1, :]
                else:
                    r = bass.ds(it * (2 * GROUP) + g * GROUP + P * i, P) if it is not None else slice(g * GROUP + P * i, g * GROUP + P * i + P)
                    src = w[r, :].unsqueeze(1)
                parts.append((slice(1024 * i, 1024 * i + 1024), src, 1))
            return parts

        def shifted(value, it, per):
            return value if it is None else it * per + value

        def view(slot_ap, part, k):
            if isinstance(part, slice):
                return slot_ap[:, part].rearrange("p (k c) -> p k c", k=k)
            return slot_ap.rearrange("p (k u c) -> p k u c", k=k, u=2)[:, :, part, :]

        def row(vector, n):
            return vector.unsqueeze(0).to_broadcast([P, n])

        block = ctx.enter_context(nc.Block())

        @block.sync
        def _(sp):
            def load(n, parts, it=None):
                if n >= RAW:
                    sp.wait_ge(hi_done, shifted(n - RAW + 1, it, 6))
                    sp.wait_ge(lo_v_done, shifted(n - RAW + 1, it, 6))
                    sp.wait_ge(lo_p_done, shifted(n - RAW + 1, it, 6))
                for part, src, k in parts:
                    sp.dma_start(view(raw[:, n % RAW, :], part, k), src).then_inc(raw_landed[n % RAW], 16)

            def projection(name):
                w, c0 = PROJ_SRC[name]
                for half in range(2):
                    load(PROJ_CHUNK[name] + half, columns(w, 4 * half, c0))

            def out_projection(name):
                w, count = SUM_SRC[name]
                for i in range(count):
                    load(START[name] + i, full_rows(w, 2 * i))

            def swiglu(name):
                n, groups = START[name], FFN[name]

                def step(n, g, it=None):
                    load(n, gate_up(name, g + 1, 0, it), it)
                    load(n + 1, gate_up(name, g + 1, 4, it), it)
                    load(n + 2, down(name, g, it), it)

                load(n, gate_up(name, 0, 0, None))
                load(n + 1, gate_up(name, 0, 4, None))
                with sp.Fori(0, (groups - 1) // 2) as it:
                    step(n + 2, 0, it)
                    step(n + 5, 1, it)
                if groups % 2 == 0:
                    step(n + 3 * groups - 4, groups - 2)
                load(n + 3 * groups - 1, down(name, groups - 1, None))

            for t in range(NT):
                sp.dma_start(x[:, t, :], a["x"][0, t * P:t * P + P, :]).then_inc(x_landed[t], 16)
            sp.dma_start(const[:, :], a["consts"][:, 0:C_TRI]).then_inc(const_landed, 16)
            for name in PROJ[:3]:
                projection(name)
            sp.dma_start(w_small[:, :, 0:8], w_in[:, 1536:1544].rearrange("(k p) c -> p k c", p=P)).then_inc(mixw_landed, 16)
            sp.dma_start(w_small[:, :, 8:24], w_in[:, 3080:3096].rearrange("(k p) c -> p k c", p=P)).then_inc(mixw_landed, 16)
            sp.dma_start(bias_g[:, 0:8], row(a["b_forget"][0], 8)).then_inc(mixw_landed, 16)
            sp.dma_start(bias_g[:, 8:264], row(a["b_alpha"][0], 256)).then_inc(mixw_landed, 16)
            sp.dma_start(w_alpha[0:16, :], a["w_alpha_up"][0]).then_inc(mixw_landed, 16)
            sp.dma_start(mixc, a["consts"][:, C_TRI:C_CAUSAL + 2 * P]).then_inc(mixw_landed, 16)
            sp.dma_start(mask_words[:, :], a["masks"]).then_inc(mixw_landed, 16)
            sp.dma_start(fox_gain, row(a["fox_out_gain"][0], 512)).then_inc(mixw_landed, 16)
            sp.dma_start(gla_gain, row(a["gla_out_gain"][0], 512)).then_inc(mixw_landed, 16)
            for name in PROJ[3:6]:
                projection(name)
            projection("xk")
            projection("xv")
            out_projection("mix_out")
            projection("xq")
            out_projection("cross_out")
            swiglu("moe")
            swiglu("ffn1_0")
            for name in PROJ[9:15]:
                projection(name)
            out_projection("diff_out")
            swiglu("ffn2_0")
            swiglu("ffn1_1")
            for name in PROJ[15:21]:
                projection(name)
            out_projection("na_out")
            swiglu("ffn2_1")
            for t in range(NT):
                sp.wait_ge(resid_done, 9 * NT + t + 1)
                sp.dma_start(out[0, t * P:t * P + P, :], x[:, t, :]).then_inc(out_landed, 16)
            sp.wait_ge(out_landed, 16 * NT)

        @block.tensor
        def _(pe):
            def products(bank, xh, xl, wh, wl, first, last):
                pe.matmul(bank, xh, wh, start=first, stop=False)
                pe.matmul(bank, xh, wl, start=False, stop=False)
                return pe.matmul(bank, xl, wh, start=False, stop=last)

            def weights(n, it=None):
                pe.wait_ge(lo_v_done, shifted(n + 1, it, 6))
                pe.wait_ge(lo_p_done, shifted(n + 1, it, 6))

            def turn(name, src=y):
                banks = TURN_BANKS[name]
                for i in range(banks):
                    t, kk = divmod(i, banks // NT)
                    pe.wait_ge(turn_src, TURN_BASE[name] + i + 1)
                    for k in range(4):
                        f = 4 * kk + k
                        last = pe.transpose(psum[:, i, k * P:k * P + P], src[:, t, f * P:f * P + P], ident)
                    last.then_inc(turned, 1)

            def input_ready(name):
                pe.wait_ge(turn_lo, TURN_BASE[name] + TURN_BANKS[name])

            def projection(name, between=None):
                j, n = PROJ_AT[name], PROJ_CHUNK[name]
                if j >= 2:
                    pe.wait_ge(proj_out0, j - 1)
                    pe.wait_ge(proj_out1, j - 1)
                for half in range(2):
                    weights(n + half)
                    for t in range(NT):
                        bank = psum[:, 2 * (j % 2) + t, :]
                        for k in range(4):
                            c = slice(512 * k, 512 * k + 512)
                            last = products(bank, x_hi[:, t, 4 * half + k, :], x_lo[:, t, 4 * half + k, :],
                                            w_hi[:, (n + half) % SPLIT, c], w_lo[:, (n + half) % SPLIT, c],
                                            half == 0 and k == 0, half == 1 and k == 3)
                        if t == 0 and half == 1:
                            last.then_inc(proj_t0, 1)
                    last.then_inc(weights_used, 1)
                    if half == 0 and between is not None:
                        between()

            def out_projection(name):
                count = SUM_SRC[name][1]
                for i in range(count):
                    n = START[name] + i
                    weights(n)
                    for t in range(NT):
                        for k in range(2):
                            for half in range(2):
                                c = slice(1024 * k + 512 * half, 1024 * k + 512 * half + 512)
                                last = products(psum[:, 4 + 2 * t + half, :], x_hi[:, t, 2 * i + k, :],
                                                x_lo[:, t, 2 * i + k, :], w_hi[:, n % SPLIT, c],
                                                w_lo[:, n % SPLIT, c], i == 0 and k == 0,
                                                i == count - 1 and k == 1)
                        if t == 0 and i == count - 1:
                            last.then_inc(sum_t0, 1)
                    last.then_inc(weights_used, 1)

            def swiglu(name):
                base, groups, gu0 = START[name], FFN[name], GU0[name]

                def gate_up_half(n, g, half, it=None):
                    par = (gu0 + g) % 2
                    weights(n, it)
                    for t in range(NT):
                        for k in range(4):
                            c = slice(512 * k, 512 * k + 512)
                            last = products(psum[:, 2 * par + t, :], x_hi[:, t, 4 * half + k, :],
                                            x_lo[:, t, 4 * half + k, :], w_hi[:, n % SPLIT, c],
                                            w_lo[:, n % SPLIT, c], half == 0 and k == 0,
                                            half == 1 and k == 3)
                        if t == 0 and half == 1:
                            last.then_inc(gu_t0, 1)
                    last.then_inc(weights_used, 1)

                def turn_hidden(g, it=None):
                    par = (gu0 + g) % 2
                    pe.wait_ge(hid_done, shifted(NT * (gu0 + g + 1), it, 2 * NT))
                    for f in range(2):
                        for t in range(NT):
                            last = pe.transpose(psum[:, 2 * par, f * S + t * P:f * S + t * P + P],
                                                hid[:, par, t, f * P:f * P + P], ident)
                    last.then_inc(hid_turned, 1)

                def down_sum(n, g, it=None, first=False, final=False):
                    par = (gu0 + g) % 2
                    weights(n, it)
                    pe.wait_ge(hid_lo, shifted(gu0 + g + 1, it, 2))
                    for t in range(NT):
                        for f in range(2):
                            for half in range(2):
                                c = slice(1024 * f + 512 * half, 1024 * f + 512 * half + 512)
                                bank = psum[:, 4 + 2 * t + half, :]
                                hh, hl = (h[:, par, f, t * P:t * P + P] for h in (h_hi, h_lo))
                                st0 = first and f == 0
                                sp0 = final and f == 1
                                pe.matmul(bank, hh, w_hi[:, n % SPLIT, c], start=st0, stop=False, skip_group_check=True)
                                pe.matmul(bank, hh, w_lo[:, n % SPLIT, c], start=False, stop=False, skip_group_check=True)
                                last = pe.matmul(bank, hl, w_hi[:, n % SPLIT, c], start=False, stop=sp0, skip_group_check=True)
                        if t == 0 and final:
                            last.then_inc(sum_t0, 1)
                    last.then_inc(weights_used, 1)

                def step(n, g, it=None, first=False):
                    gate_up_half(n, g + 1, 0, it)
                    turn_hidden(g, it)
                    gate_up_half(n + 1, g + 1, 1, it)
                    down_sum(n + 2, g, it, first)

                gate_up_half(base, 0, 0)
                gate_up_half(base + 1, 0, 1)
                for b in range(4, 8):
                    pe.matmul(psum[:, b, :], zeros[:, 0:P], zeros[:, :], start=True, stop=False, skip_group_check=True)
                with pe.Fori(0, (groups - 1) // 2) as it:
                    step(base + 2, 0, it)
                    step(base + 5, 1, it)
                if groups % 2 == 0:
                    step(base + 3 * groups - 4, groups - 2)
                turn_hidden(groups - 1)
                down_sum(base + 3 * groups - 1, groups - 1, final=True)

            def experts():
                base = START["moe"]

                def gather(w):
                    pe.wait_ge(pick_ready, NT * (w + 1))
                    if w >= 2:
                        pe.wait_ge(scatter_taken, NT * (w - 2) + 1)
                    for kk in range(2):
                        for k in range(4):
                            f = slice((4 * kk + k) * P, (4 * kk + k) * P + P)
                            for t in range(NT):
                                last = pe.matmul(psum[:, 2 + kk, k * P:k * P + P], y[:, t, f], pick[:, w, t, :],
                                                 start=t == 0, stop=t == NT - 1)
                        last.then_inc(gathered, 1)

                def scatter(w):
                    pe.wait_ge(slot_y_out, w + 1)
                    for t in range(NT):
                        for half in range(2):
                            bank = 2 + half if t == 0 else 4 + 2 * (w % 2) + half
                            last = pe.matmul(psum[:, bank, :], pickT[:, w, t, :], slot_y[:, 512 * half:512 * half + 512],
                                             start=True, stop=True)
                        last.then_inc(scattered, 1)

                def gate_up_half(n, w, g, half, it=None):
                    weights(n, it)
                    if half == 0 and g % 8 == 0:
                        pe.wait_ge(gathered_lo, 2 * w + 2)
                    for k in range(4):
                        c = slice(512 * k, 512 * k + 512)
                        last = products(psum[:, g % 2, :], x_hi[:, w % 2, 4 * half + k, :],
                                        x_lo[:, w % 2, 4 * half + k, :], w_hi[:, n % SPLIT, c],
                                        w_lo[:, n % SPLIT, c], half == 0 and k == 0, half == 1 and k == 3)
                    last.then_inc(weights_used, 1)

                def turn_hidden(g, it=None):
                    pe.wait_ge(hid_done, shifted(NT * (g + 1), it, 2 * NT))
                    for f in range(2):
                        last = pe.transpose(psum[:, g % 2, f * P:f * P + P], hid[:, g % 2, 0, f * P:f * P + P], ident)
                    last.then_inc(hid_turned, 1)

                def down_sum(n, w, g, it=None):
                    weights(n, it)
                    pe.wait_ge(hid_lo, shifted(g + 1, it, 2))
                    for f in range(2):
                        for half in range(2):
                            c = slice(1024 * f + 512 * half, 1024 * f + 512 * half + 512)
                            bank = psum[:, 4 + 2 * (w % 2) + half, :]
                            hh, hl = (h[:, g % 2, f, 0:P] for h in (h_hi, h_lo))
                            pe.matmul(bank, hh, w_hi[:, n % SPLIT, c], start=False, stop=False, skip_group_check=True)
                            pe.matmul(bank, hh, w_lo[:, n % SPLIT, c], start=False, stop=False, skip_group_check=True)
                            last = pe.matmul(bank, hl, w_hi[:, n % SPLIT, c], start=False, stop=False, skip_group_check=True)
                    last.then_inc(weights_used, 1)

                def step(w, g, it=None, between=None):
                    n, w_next = base + 2 + 3 * g, (g + 1) // 8
                    gate_up_half(n, w_next, g + 1, 0, it)
                    if between is not None:
                        between()
                    turn_hidden(g, it)
                    gate_up_half(n + 1, w_next, g + 1, 1, it)
                    down_sum(n + 2, w, g, it)

                pe.wait_ge(hot_ready, 1)
                hot0, hot1 = rt[:, 0, 56:60], rt[:, 1, 56:60]
                pe.matmul(psum[:, 5, 0:4], tri, hot0, start=True, stop=True)
                pe.matmul(psum[:, 5, 8:12], ones, hot0, start=True, stop=False)
                pe.matmul(psum[:, 5, 8:12], tri, hot1, start=False, stop=True)
                pe.matmul(psum[:, 5, 16:20], ones, hot0, start=True, stop=False)
                pe.matmul(psum[:, 5, 16:20], ones, hot1, start=False, stop=True).then_inc(ranked, 1)
                gather(0)
                pe.wait_ge(pick_ready, NT * WINDOWS)
                for w in range(WINDOWS):
                    for t in range(NT):
                        last = pe.transpose(psum[:, 6 + w // 2, (w % 2) * 256 + t * P:(w % 2) * 256 + t * P + P],
                                            pick[:, w, t, :], ident)
                last.then_inc(pick_turned, 1)
                gate_up_half(base, 0, 0, 0)
                gate_up_half(base + 1, 0, 0, 1)
                pe.wait_ge(gates_ready, 1)
                for w in range(WINDOWS):
                    for t in range(NT):
                        last = pe.matmul(psum[:, 5, 32 + 32 * w:32 + 32 * w + 17], pick[:, w, t, :], gates[:, t, :],
                                         start=t == 0, stop=t == NT - 1)
                last.then_inc(slotv_done, 1)
                pe.wait_ge(slotv_out, 1)
                pe.wait_ge(pickT_out, 1)
                for w in range(WINDOWS):
                    if w >= 2:
                        pe.wait_ge(scatter_taken, NT * (w - 1))
                    for b in range(2):
                        pe.matmul(psum[:, 4 + 2 * (w % 2) + b, :], zeros[:, 0:P], zeros[:, :], start=True, stop=False,
                                  skip_group_check=True)
                    with pe.Fori(0, 3) as it:
                        step(w, 8 * w, it)
                        step(w, 8 * w + 1, it)
                    if w:
                        scatter(w - 1)
                    step(w, 8 * w + 6, None, (lambda: gather(w + 1)) if w < WINDOWS - 1 else None)
                    if w < WINDOWS - 1:
                        step(w, 8 * w + 7)
                turn_hidden(8 * WINDOWS - 1)
                down_sum(base + 24 * WINDOWS - 1, WINDOWS - 1, 8 * WINDOWS - 1)
                scatter(WINDOWS - 1)
                pe.wait_ge(over_known, 1)
                with pe.If(pe.value_load(is_over, min_val=0, max_val=1) > 0):
                    pe.wait_ge(scatter_taken, NT * WINDOWS)
                    for k in range(KD):
                        for t in range(NT):
                            pe.matmul(psum[:, k // 4, (k % 4) * P:(k % 4) * P + P], y[:, t, k * P:k * P + P],
                                      over_pick[:, t, :], start=t == 0, stop=t == NT - 1)
                    for t in range(NT):
                        pe.transpose(psum[:, 2, t * P:t * P + P], over_pick[:, t, :], ident)
                    for t in range(NT):
                        last = pe.matmul(psum[:, 3, 0:17], over_pick[:, t, :], gates[:, t, :], start=t == 0, stop=t == NT - 1)
                    last.then_inc(over_in, 1)
                    pe.wait_ge(over_taken, 1)
                    for b in (4, 5):
                        last = pe.matmul(psum[:, b, :], zeros[:, 0:P], zeros[:, :], start=True, stop=False, skip_group_check=True)
                    last.then_inc(over_down, 1)
                    with pe.Fori(0, 4) as it:
                        for which, done in enumerate((over_gate, over_up)):
                            pe.wait_ge(over_landed, it * 48 + (16 + 16 * which))
                            for k in range(KD):
                                last = pe.matmul(psum[:, which, :], over_x[:, k, :], over_w[:, 512 * k:512 * k + 512],
                                                 start=k == 0, stop=k == KD - 1)
                            last.then_inc(done, 1)
                        pe.wait_ge(over_hidden, it + 1)
                        for f in range(4):
                            last = pe.transpose(psum[:, 2, f * P:f * P + P], over_hid[:, f * P:f * P + P], ident)
                        last.then_inc(over_turned, 1)
                        pe.wait_ge(over_landed, it * 48 + 48)
                        pe.wait_ge(over_hidT_out, it + 1)
                        for f in range(4):
                            for half in range(2):
                                c = slice(1024 * f + 512 * half, 1024 * f + 512 * half + 512)
                                last = pe.matmul(psum[:, 4 + half, :], over_hidT[:, f * P:f * P + P], over_w[:, c],
                                                 start=False, stop=False, skip_group_check=True)
                        last.then_inc(over_down, 1)
                    pe.wait_ge(over_y_out, 1)
                    for t in range(NT):
                        for half in range(2):
                            last = pe.matmul(psum[:, 2 * t + half, :], over_pickT[:, t, :],
                                             slot_y[:, 512 * half:512 * half + 512], start=True, stop=True)
                    last.then_inc(over_scattered, 1)

            def qk_turn(name, q, k):
                for b in range(QKT_BANKS[name]):
                    for i, src in enumerate((q, k)):
                        c = 2 * (QKT0[name] + b) + i
                        if QKT0[name] + b >= 2:
                            pe.wait_ge(q_out if i == 0 else k_out, QKT0[name] + b - 1)
                        for f in range(2):
                            for t in range(NT):
                                last = pe.transpose(psum[:, 4 + c % 4, f * S + t * P:f * S + t * P + P],
                                                    src[:, t, (2 * b + f) * P:(2 * b + f) * P + P], ident)
                        last.then_inc(qk_turned, 1)

            def attention(name, qT, kT, v, probs, probsT, d, last_proj):
                pairs, gsize, u0 = PAIRS[name], GSIZE[name], UNIT0[name]
                units = [(i, p) for i in range(NT) for p in range(pairs)]
                dv = {"fox": 64, "cross": 128, "diff": 128, "na": 64}[name]

                def keys(i):
                    return (i + 1) * P if name == "fox" else S

                def rows_of(T, m, c):
                    if d == P:
                        return T[:, m, c]
                    return T[(m % 2) * 64:(m % 2) * 64 + 64, m // 2, c]

                def score(n):
                    i, p = units[n]
                    u = u0 + n
                    if n >= 4:
                        pe.wait_ge(probs_done, u - 3)
                    for j in range(2):
                        m = score_map(name, p, j)
                        bank = psum[:, u % 4, j * S:j * S + keys(i)]
                        last = pe.matmul(bank, rows_of(qT, m, slice(i * P, i * P + P)),
                                         rows_of(kT, m, slice(0, keys(i))), start=True, stop=name != "fox")
                        if name == "fox":
                            last = pe.matmul(bank, ident[0:8, m:m + 1].to_broadcast([8, P]), ct[0:8, 0:keys(i)],
                                             start=False, stop=True)
                    last.then_inc(scores, 1)

                def turn_probs(n):
                    i, p = units[n]
                    u = u0 + n
                    pe.wait_ge(probs_done, u + 1)
                    if n >= 2:
                        pe.wait_ge(probsT_done, u - 1)
                    for j in range(2):
                        for kt in range(keys(i) // P):
                            last = pe.transpose(psum[:, 4 + u % 2, (2 * j + kt) * P:(2 * j + kt) * P + P],
                                                probs[:, u % 3, j, kt * P:kt * P + P], ident)
                    last.then_inc(probs_turned, 1)

                def apply(n):
                    i, p = units[n]
                    u = u0 + n
                    grp = GROUP0[name] + n // gsize
                    pe.wait_ge(probsT_done, u + 1)
                    if n % gsize == 0 and n // gsize >= 2:
                        pe.wait_ge(pv_taken, grp - 1)
                    nk = keys(i) // P
                    for j in range(2):
                        m = score_map(name, p, j)
                        at = m % (2 * gsize) * dv
                        vc = (m // 2 if name == "diff" else m) * dv
                        for kt in range(nk):
                            last = pe.matmul(psum[:, 6 + grp % 2, at:at + dv],
                                             probsT[:, u % 2, (2 * j + kt) * P:(2 * j + kt) * P + P],
                                             v[:, kt, vc:vc + dv], start=kt == 0, stop=kt == nk - 1)
                    if n % gsize == gsize - 1:
                        last.then_inc(pv_done, 1)

                pe.wait_ge(q_out, QKT0[name] + QKT_BANKS[name])
                pe.wait_ge(k_out, QKT0[name] + QKT_BANKS[name])
                pe.wait_ge(proj_out0, PROJ_AT[last_proj] + 1)
                pe.wait_ge(proj_out1, PROJ_AT[last_proj] + 1)
                score(0)
                score(1)
                for n in range(len(units)):
                    if n + 2 < len(units):
                        score(n + 2)
                    turn_probs(n)
                    if n >= 1:
                        apply(n - 1)
                apply(len(units) - 1)

            def small(bank, w, columns_):
                for t in range(NT):
                    for k in range(KD):
                        for part in (x_hi, x_lo):
                            last = pe.matmul(psum[:, bank, t * 64:t * 64 + columns_],
                                             part[:, t, k, :].bitcast(F32), w[:, k, :],
                                             start=k == 0 and part is x_hi, stop=k == KD - 1 and part is x_lo)
                last.then_inc(logits_done, 1)

            pe.wait_ge(const_landed, 16)
            turn("mix")
            input_ready("mix")
            projection("gg")
            pe.wait_ge(mixw_landed, 16 * MIX_LOADS)
            small(4, w_small, 24)

            def turn_gate_inputs():
                pe.wait_ge(logits_out, 1)
                for t in range(NT):
                    last = pe.transpose(psum[0:16, 5, t * P:t * P + P], lg[:, t, 8:24], ident)
                last.then_inc(ga_turned, 1)

            projection("gqk", turn_gate_inputs)
            pe.wait_ge(ga_out, 1)
            for t in range(NT):
                last = pe.matmul(psum[:, 6, t * S:t * S + S], gaT[0:16, t * P:t * P + P], w_alpha[0:16, :],
                                 start=True, stop=True)
            last.then_inc(alpha_done, 1)
            pe.wait_ge(proj_out0, 2)
            pe.wait_ge(proj_out1, 2)
            qk_turn("gla", gqk[:, :, 0:256], gqk[:, :, 256:512])
            projection("gv")
            pe.wait_ge(logsig_done, 1)
            pe.wait_ge(q_out, 1)
            for t in range(NT):
                for f in range(2):
                    last = pe.matmul(psum[:, 4, f * S + t * P:f * S + t * P + P],
                                     lg[:, t, 8 + f * P:8 + f * P + P], cum, start=True, stop=True)
            last.then_inc(decay_done, 1)
            pe.wait_ge(k_out, 1)
            for t in range(NT):
                last = pe.matmul(psum[:, 5, t * S:t * S + S], suf, lg[:, t, 8:264], start=True, stop=True)
            last.then_inc(decay_done, 1)
            pe.matmul(psum[0:8, 7, 0:P], lg[:, 0, 0:8], tri, start=True, stop=True)
            pe.matmul(psum[0:8, 7, P:S], lg[:, 0, 0:8], ones, start=True, stop=False)
            pe.matmul(psum[0:8, 7, P:S], lg[:, 1, 0:8], tri, start=False, stop=True).then_inc(decay_done, 1)
            projection("fq")
            pe.wait_ge(ks_ready, 1)
            pe.wait_ge(ct_out, 1)
            pe.wait_ge(proj_out0, 3)
            for c in range(3):
                r = slice((c % 2) * 64, (c % 2) * 64 + 64)
                for h in range(4):
                    at = (c // 2) * 256 + (h // 2) * P
                    last = pe.matmul(psum[(h % 2) * 64:(h % 2) * 64 + 64, 6 + c % 2, at:at + P],
                                     gks[r, c // 2, h * 64:h * 64 + 64], gv[r, c // 2, h * P:h * P + P],
                                     start=True, stop=True)
            last.then_inc(u_done, 1)

            def level(l):
                if l < LEVELS:
                    pe.wait_ge(z_ready, l + 1)
                if l == 0:
                    pe.wait_ge(gb_out, 1)
                    pe.wait_ge(suffix_out, 1)
                if l == 1:
                    pe.wait_ge(state_ready, 1)
                if l >= 2:
                    pe.wait_ge(level_out, l - 1)
                for t in range(NT):
                    for h in range(4):
                        r = slice((h % 2) * 64, (h % 2) * 64 + 64)
                        c = slice((h // 2) * S + t * P, (h // 2) * S + t * P + P)
                        lhs, rhs = (gz[r, l % 2, c], gz[r, l % 2, c]) if l < LEVELS else (gkT[r, c], gqT[r, c])
                        at = t * 256 + (h // 2) * P
                        last = pe.matmul(psum[:, 4 + 2 * (l % 2) + h % 2, at:at + P], lhs, rhs,
                                         start=True, stop=True)
                last.then_inc(level_done, 1)

            level(0)
            level(1)
            projection("fk")
            level(2)
            level(3)
            projection("fv")
            level(4)
            level(5)
            level(6)
            pe.wait_ge(level_out, LEVELS + 1)
            pe.wait_ge(qb_ready, 1)
            for h in (0, 2, 1, 3):
                r = slice((h % 2) * 64, (h % 2) * 64 + 64)
                for t in range(NT):
                    at = slice(t * 256 + (h // 2) * P, t * 256 + (h // 2) * P + P)
                    last = pe.matmul(psum[:, 6 + h % 2, at], at_[:, t, h, :], gv[:, t, h * P:h * P + P],
                                     start=True, stop=False, skip_group_check=True)
                    for c in range(2 * t, 2 * t + 2):
                        if c == 0:
                            continue
                        q = slice((h // 2) * S + c * 64, (h // 2) * S + c * 64 + 64)
                        last = pe.matmul(psum[(c % 2) * 64:(c % 2) * 64 + 64, 6 + h % 2, at],
                                         gs[r, q], st[r, c - 1, h // 2, :], start=False, stop=True,
                                         skip_group_check=True)
            last.then_inc(gla_o_done, 1)
            pe.wait_ge(gla_o_out, 1)
            pe.wait_ge(proj_out0, 6)
            pe.wait_ge(proj_out1, 6)
            qk_turn("fox", fq, fk)
            attention("fox", fqT, fkT, fv, probs_1, probsT_1, 64, "fv")
            turn("mem", mem)
            input_ready("mem")
            projection("xk")
            projection("xv")
            pe.wait_ge(proj_out0, 8)
            pe.wait_ge(proj_out1, 8)
            turn("mix_y")
            input_ready("mix_y")
            out_projection("mix_out")

            turn("cross")
            input_ready("cross")
            projection("xq")
            pe.wait_ge(proj_out0, 9)
            pe.wait_ge(proj_out1, 9)
            qk_turn("cross", xq, xk)
            attention("cross", xqT, xkT, xv, probs_1, probsT_1, P, "xq")
            turn("cross_y")
            input_ready("cross_y")
            out_projection("cross_out")

            turn("moe")
            input_ready("moe")
            pe.wait_ge(router_landed, 16 * 5)
            pe.wait_ge(zeros_ready, 1)
            small(4, w_router, 20)
            pe.wait_ge(logits_out, 2)
            experts()

            turn("ffn1_0")
            input_ready("ffn1_0")
            swiglu("ffn1_0")
            turn("diff")
            input_ready("diff")
            for name in PROJ[9:15]:
                projection(name)
            pe.wait_ge(rope_done, 2)
            qk_turn("diff", q2, y)
            attention("diff", q2T, k2T, v2, probs_2, probsT_2, 64, "dv1")
            turn("diff_y")
            input_ready("diff_y")
            out_projection("diff_out")
            turn("ffn2_0")
            input_ready("ffn2_0")
            swiglu("ffn2_0")
            turn("ffn1_1")
            input_ready("ffn1_1")
            swiglu("ffn1_1")
            turn("na")
            input_ready("na")
            for name in PROJ[15:21]:
                projection(name)
            pe.wait_ge(proj_out0, 21)
            pe.wait_ge(proj_out1, 21)
            qk_turn("na", q2, y)
            attention("na", q2T, k2T, v2, probs_2, probsT_2, 64, "nv1")
            turn("na_y")
            input_ready("na_y")
            out_projection("na_out")
            turn("ffn2_1")
            input_ready("ffn2_1")
            swiglu("ffn2_1")

        def outlets(name, t):
            r, q = (lambda n: rstd[:, NORM_AT[n], t:t + 1]), (lambda n: rstd_q[:, SCALED.index(n), t:t + 1])
            half = int(name[-1]) * 512 if name[-1] in "01" else 0
            return {
                "gg": lambda: [(0, 512, gg[:, t, :], r("mix"))],
                "gqk": lambda: [(0, 256, gqk[:, t, 0:256], q("mix")), (256, 512, gqk[:, t, 256:512], r("mix"))],
                "gv": lambda: [(0, 512, gv[:, t, :], r("mix"))],
                "fq": lambda: [(0, 512, fq[:, t, :], q("mix"))],
                "fk": lambda: [(0, 512, fk[:, t, :], r("mix"))],
                "fv": lambda: [(0, 512, fv[:, t, :], r("mix"))],
                "xk": lambda: [(0, 512, xk[:, t, :], r("mem"))],
                "xv": lambda: [(0, 512, xv[:, t, :], r("mem"))],
                "xq": lambda: [(0, 512, xq[:, t, :], q("cross"))],
                "dq": lambda: [(0, 512, q2[:, t, half:half + 512], q("diff"))],
                "dk": lambda: [(0, 512, y[:, t, half:half + 512], r("diff"))],
                "dv": lambda: [(0, 512, v2[:, t, half:half + 512], r("diff"))],
                "nq": lambda: [(0, 512, q2[:, t, half:half + 512], q("na"))],
                "nk": lambda: [(0, 512, y[:, t, half:half + 512], r("na"))],
                "nv": lambda: [(0, 512, v2[:, t, half:half + 512], r("na"))],
            }[name.rstrip("01")]()

        def norm_of(name):
            return {"x": "mem" if name in ("xk", "xv") else "cross", "d": "diff", "n": "na"}.get(name[0], "mix")

        def gain_row(name):
            own = {"mix": "mix_norm", "cross": "cross_norm", "moe": "moe_norm"}
            if name in own:
                return a[own[name]][0]
            if name in ("mem", "final"):
                return a[name + "_norm"]
            layer = {"diff": 0, "na": 1}.get(name.split("_")[0])
            which = 2
            if layer is None:
                layer, which = int(name.split("_")[1]), 0 if name[3] == "1" else 4
            return a["norm_g_2"][layer, which + name.endswith("_p")]

        @block.scalar
        def _(act):
            ahead, gains, squares = [0], [0], [0]

            def hi(n, it=None):
                act.wait_ge(raw_landed[n % RAW], shifted(32 * (n // RAW + 1), it, 32))
                if n >= SPLIT:
                    act.wait_ge(weights_used, shifted(n - SPLIT + 1, it, 6))
                act.activation(w_hi[:, n % SPLIT, :], raw[:, n % RAW, :], ACT.Copy).then_inc(hi_done, 1)

            def split_through(n):
                while ahead[0] <= min(n, CHUNKS - 1):
                    hi(ahead[0])
                    ahead[0] += 1

            def load_gains(through):
                while gains[0] <= min(through, len(NORMS) - 1):
                    i = gains[0]
                    if i >= 2:
                        act.wait_ge(gain_used, i - 1)
                    act.dma_start(gain[:, i % 2, :], row(gain_row(NORMS[i]), D)).then_inc(gain_landed[i % 2], 16)
                    gains[0] += 1

            def square(name, t, src, junk=junk):
                if squares[0]:
                    act.wait_ge(squared, squares[0])
                squares[0] += 1
                act.activation(junk, src, ACT.Square, accum_out=sums[:, NORM_AT[name], t:t + 1]).then_inc(squared, 1)

            def take_turns(name, t=None):
                banks = TURN_BANKS[name]
                for i in range(banks):
                    tt, kk = divmod(i, banks // NT)
                    if t is not None and tt != t:
                        continue
                    act.wait_ge(turned, TURN_BASE[name] + i + 1)
                    act.activation(x_hi[:, tt, 4 * kk:4 * kk + 4, :], psum[:, i, :].rearrange("p (k c) -> p k c", k=4),
                                   ACT.Copy).then_inc(turn_hi, 1)

            def norm_turn(name, src):
                for t in range(NT):
                    if name == "mix":
                        act.wait_ge(x_landed[t], 16)
                    take_turns(name, t)
                    square(name, t, src[:, t, :])
                load_gains(NORM_AT[name] + 2)

            def take_projection(name):
                j, n = PROJ_AT[name], PROJ_CHUNK[name]
                split_through(n + 3)
                act.wait_ge(proj_t0, j + 1)
                act.wait_ge(rstdq_ready, SCALED.index("mix" if norm_of(name) == "mem" else norm_of(name)) + 1)
                act.wait_ge(rstd_ready, NT * (NORM_AT[norm_of(name)] + 1))
                for t in range(NT if name == "gg" else 1):
                    if t == 1:
                        act.wait_ge(weights_used, n + 2)
                    for c0, c1, dst, scale in outlets(name, t):
                        last = act.activation(dst, psum[:, 2 * (j % 2) + t, c0:c1],
                                              ACT.Silu if name == "gg" else ACT.Copy, scale=scale)
                    last.then_inc(proj_out0 if t == 0 else proj_out1, 1)

            def take_q(name, dst):
                for b in range(QKT_BANKS[name]):
                    act.wait_ge(qk_turned, 2 * (QKT0[name] + b) + 1)
                    act.activation(dst[:, 512 * b:512 * b + 512], psum[:, 4 + 2 * ((QKT0[name] + b) % 2), :],
                                   ACT.Copy).then_inc(q_out, 1)

            def attention(name, probs, midway=None):
                u0 = UNIT0[name]
                for n in range(NT * PAIRS[name]):
                    if n == PAIRS[name] and midway:
                        midway()
                    u, i = u0 + n, n // PAIRS[name]
                    keys = (i + 1) * P if name == "fox" else S
                    act.wait_ge(max_done, u + 1)
                    if n >= 3:
                        act.wait_ge(probs_turned, u - 2)
                    for j in range(2):
                        p_ = probs[:, u % 3, j, 0:keys]
                        src = p_ if name in ("fox", "na") else psum[:, u % 4, j * S:j * S + keys]
                        last = act.activation(p_, src, ACT.Exp, bias=negmax[:, u % 3, j:j + 1],
                                              accum_out=rows[:, u, j:j + 1])
                    last.then_inc(probs_done, 1)

            def square_sum(name, total):
                last = START[total] + dict(PHASES)[total] - 1
                split_through(last + 2)
                act.wait_ge(sum_t0, SUM_AT[total] + 1)
                square(name, 0, psum[:, 4:6, :].rearrange("p b c -> p (b c)"))
                act.wait_ge(weights_used, last + 1)
                square(name, 1, psum[:, 6:8, :].rearrange("p b c -> p (b c)"))

            def residual_squares(name, count):
                for t in range(NT):
                    act.wait_ge(resid_done, count + t + 1)
                    square(name, t, x[:, t, :])

            def norm_turn_resid(name, count):
                for t in range(NT):
                    take_turns(name, t)
                    act.wait_ge(resid_done, count + t + 1)
                    square(name, t, x[:, t, :])
                load_gains(NORM_AT[name] + 2)

            def swiglu(name):
                base, groups, gu0 = START[name], FFN[name], GU0[name]

                def gated(n, g, it=None):
                    par = (gu0 + g) % 2
                    for t in range(NT):
                        if t == 0:
                            act.wait_ge(gu_t0, shifted(gu0 - MOE_GROUPS + g + 1, it, 2))
                        else:
                            act.wait_ge(weights_used, shifted(n + 2, it, 6))
                        act.activation(silu[:, par, t, :], psum[:, 2 * par + t, 0:GROUP], ACT.Silu,
                                       scale=rstd[:, NORM_AT[name], t:t + 1]).then_inc(silu_done, 1)

                def take_hidden(g, it=None):
                    par = (gu0 + g) % 2
                    act.wait_ge(hid_turned, shifted(gu0 + g + 1, it, 2))
                    act.activation(h_hi[:, par, :, :], psum[:, 2 * par, :].rearrange("p (f s) -> p f s", f=2),
                                   ACT.Copy).then_inc(hid_hi, 1)

                def split(n, it):
                    if n < CHUNKS:
                        hi(n, it)

                def step(n, g, it=None):
                    split(n + 2, it)
                    take_hidden(g, it)
                    split(n + 3, it)
                    gated(n, g + 1, it)
                    split(n + 4, it)

                split_through(base + 3)
                act.wait_ge(rstd_ready, NT * (NORM_AT[name] + 1))
                gated(base, 0)
                peel = name == "ffn2_1"
                with act.Fori(0, (groups - 1) // 2 - peel) as it:
                    step(base + 2, 0, it)
                    step(base + 5, 1, it)
                for g in range((groups - 1) // 2 * 2 - 2 * peel, groups - 1):
                    step(base + 2 + 3 * g, g)
                ahead[0] = base + 3 * groups + 1
                take_hidden(groups - 1)

            def experts():
                base = START["moe"]

                def take_gather(w):
                    for kk in range(2):
                        act.wait_ge(gathered, 2 * w + kk + 1)
                        act.activation(x_hi[:, w % 2, 4 * kk:4 * kk + 4, :],
                                       psum[:, 2 + kk, :].rearrange("p (k c) -> p k c", k=4), ACT.Copy).then_inc(gathered_hi, 1)

                def gated(n, w, g, it=None):
                    act.wait_ge(weights_used, shifted(n + 2, it, 6))
                    act.activation(silu[:, g % 2, 0, :], psum[:, g % 2, 0:GROUP], ACT.Silu,
                                   scale=slotv[:, w, 16:17]).then_inc(silu_done, NT)

                def take_hidden(g, it=None):
                    act.wait_ge(hid_turned, shifted(g + 1, it, 2))
                    act.activation(h_hi[:, g % 2, :, 0:P], psum[:, g % 2, 0:2 * P].rearrange("p (f s) -> p f s", f=2),
                                   ACT.Copy).then_inc(hid_hi, 1)

                def step(g, it=None, between=None):
                    n = base + 2 + 3 * g
                    hi(n + 2, it)
                    if between is not None:
                        between()
                    take_hidden(g, it)
                    hi(n + 3, it)
                    gated(n, (g + 1) // 8, g + 1, it)
                    hi(n + 4, it)

                def take_slot_y(w):
                    act.wait_ge(weights_used, base + 24 * (w + 1) + (2 if w < WINDOWS - 1 else 0))
                    if w:
                        act.wait_ge(scattered, NT * w)
                    act.activation(slot_y, psum[:, 4 + 2 * (w % 2):6 + 2 * (w % 2), :].rearrange("p b c -> p (b c)"),
                                   ACT.Copy).then_inc(slot_y_out, 1)

                for t in range(NT):
                    act.wait_ge(route_in, t + 1)
                    act.activation(rt[:, t, 80:84], rt[:, t, 24:28], ACT.Exp, bias=rt[:, t, 64:65],
                                   accum_out=rt[:, t, 65:66]).then_inc(route_exp, 1)
                take_gather(0)
                act.wait_ge(pick_turned, 1)
                act.activation(pickT.rearrange("p w t s -> p (w t s)"), psum[:, 6:8, :].rearrange("p b c -> p (b c)"),
                               ACT.Copy).then_inc(pickT_out, 1)
                for t in range(NT):
                    act.wait_ge(route_in, NT + t + 1)
                    act.activation(rt[:, t, 67:68], rt[:, t, 66:67], ACT.Exp).then_inc(route_exp, 1)
                split_through(base + 3)
                act.wait_ge(slotv_out, 1)
                gated(base, 0, 0)
                for w in range(WINDOWS):
                    with act.Fori(0, 3) as it:
                        step(8 * w, it)
                        step(8 * w + 1, it)
                    step(8 * w + 6, None, (lambda: take_gather(w + 1)) if w < WINDOWS - 1 else None)
                    if w < WINDOWS - 1:
                        step(8 * w + 7)
                        take_slot_y(w)
                ahead[0] = base + 24 * WINDOWS + 1
                take_hidden(8 * WINDOWS - 1)
                split_through(base + 24 * WINDOWS + 1)
                take_slot_y(WINDOWS - 1)
                act.wait_ge(over_known, 1)
                with act.If(act.value_load(is_over, min_val=0, max_val=1) > 0):
                    group = act.value_load(over_group, min_val=0, max_val=WINDOWS - 1)
                    with act.Fori(0, 4) as it:
                        e = bass.ds(group * 4 + it, 1)
                        act.wait_ge(over_down, it + 1)
                        act.dma_start(over_w.rearrange("p (k c) -> p k c", k=KD),
                                      a["w_expert_gate"][0][e].rearrange("e (k p) c -> p (e k) c", p=P)).then_inc(over_landed, 16)
                        act.wait_ge(over_gate, it + 1)
                        act.dma_start(over_w.rearrange("p (k c) -> p k c", k=KD),
                                      a["w_expert_up"][0][e].rearrange("e (k p) c -> p (e k) c", p=P)).then_inc(over_landed, 16)
                        act.activation(over_silu, psum[:, 0, :], ACT.Silu, scale=over_slotv[:, 16:17]).then_inc(over_silued, 1)
                        act.wait_ge(over_up, it + 1)
                        act.dma_start(over_w.rearrange("p (k c) -> p k c", k=4),
                                      a["w_expert_down"][0][e].rearrange("e (k p) c -> p (e k) c", p=P)).then_inc(over_landed, 16)

            load_gains(1)
            norm_turn("mix", x)
            take_projection("gg")
            take_projection("gqk")
            take_q("gla", gqT)
            act.wait_ge(logits_in, 1)
            act.activation(lsg, lg, ACT.Abs).then_inc(logsig_abs, 1)
            act.wait_ge(logsig_abs, 1)
            act.activation(lsg, lsg, ACT.Exp, scale=-1.0).then_inc(act_chain, 1)
            act.wait_ge(act_chain, 1)
            act.activation(lsg, lsg, ACT.Ln, bias=1.0).then_inc(logsig_ln, 1)
            take_projection("gv")
            act.wait_ge(decay_done, 2)
            act.activation(gs, psum[:, 5, :], ACT.Exp).then_inc(suffix_out, 1)
            act.wait_ge(decay_done, 3)
            act.wait_ge(gb_out, 1)
            act.activation(gexp, gb, ACT.Exp).then_inc(expb_ready, 1)
            take_projection("fq")

            def decay(l):
                act.wait_ge(diff_ready, l + 1)
                act.activation(ge, ge, ACT.Abs).then_inc(act_chain, 1)
                act.wait_ge(act_chain, l + 2)
                act.activation(ge, ge, ACT.Exp, scale=-1.0).then_inc(decay_exp, 1)

            decay(0)
            decay(1)
            take_projection("fk")
            decay(2)
            decay(3)
            take_projection("fv")
            decay(4)
            decay(5)
            act.wait_ge(gla_o_out, 1)
            take_q("fox", region(4096, 1024))
            act.wait_ge(qk_turned, 2 * (QKT0["fox"] + QKT_BANKS["fox"]))
            act.dma_start(mem[:, :, :], a["mem"][0].rearrange("(t p) c -> p t c", p=P)).then_inc(mem_landed, 16)

            def mem_squares():
                act.wait_ge(mem_landed, 16)
                for t in range(NT):
                    square("mem", t, mem[:, t, :], fb[:, 1024:2048])

            attention("fox", probs_1, mem_squares)
            for t in range(NT):
                take_turns("mem", t)
            load_gains(NORM_AT["mem"] + 2)
            take_projection("xk")
            take_projection("xv")
            act.wait_ge(turned, TURN_BASE["mix_y"] + 4)
            take_turns("mix_y")
            split_through(START["mix_out"] + 5)
            act.dma_start(w_router[:, :, 0:4], a["w_router_group"][0].rearrange("(k p) c -> p k c", p=P)).then_inc(router_landed, 16)
            act.dma_start(w_router[:, :, 4:20], a["w_router_expert"][0].rearrange("(k p) c -> p k c", p=P)).then_inc(router_landed, 16)
            act.dma_start(slots, a["consts"][:, C_SLOT:C_END]).then_inc(router_landed, 16)
            act.dma_start(b_router[:, 0:4], row(a["b_router_group"][0], 4)).then_inc(router_landed, 16)
            act.dma_start(b_router[:, 4:20], row(a["b_router_expert"][0], 16)).then_inc(router_landed, 16)
            norm_turn_resid("cross", 0)
            take_projection("xq")
            take_q("cross", region(6144, 1024))
            attention("cross", probs_1)
            take_turns("cross_y")
            split_through(START["cross_out"] + 3)
            norm_turn_resid("moe", NT)
            split_through(START["moe"] + 2)
            experts()
            split_through(START["moe"] + 3 * MOE_GROUPS + 1)
            residual_squares("final", 2 * NT)
            norm_turn_resid("ffn1_0", 3 * NT)
            act.dma_start(subln, row(a["diff_subln_2"][0], P)).then_inc(diffw_landed, 16)
            act.dma_start(lamv, row(a["diff_lambda_2"][0].rearrange("a b -> (a b)"), 256)).then_inc(diffw_landed, 16)
            act.dma_start(namask, a["consts"][:, C_NAMASK:C_SLOT]).then_inc(namask_landed, 16)
            act.wait_ge(lam_sum, 1)
            act.activation(lams[:, 2:4], lams[:, 0:2], ACT.Exp).then_inc(lam_exp, 1)
            swiglu("ffn1_0")
            square_sum("ffn1_0_p", "ffn1_0")
            norm_turn_resid("diff", 4 * NT)
            for name in PROJ[9:15]:
                take_projection(name)
            take_q("diff", region(2560, 2048))
            attention("diff", probs_2)
            take_turns("diff_y")
            square_sum("diff_p", "diff_out")
            norm_turn_resid("ffn2_0", 5 * NT)
            act.dma_start(region(6656, 6144), a["na_biases"]).then_inc(nab_landed, 16)
            swiglu("ffn2_0")
            square_sum("ffn2_0_p", "ffn2_0")
            norm_turn_resid("ffn1_1", 6 * NT)
            swiglu("ffn1_1")
            square_sum("ffn1_1_p", "ffn1_1")
            norm_turn_resid("na", 7 * NT)
            for name in PROJ[15:21]:
                take_projection(name)
            take_q("na", region(2560, 2048))
            attention("na", probs_2)
            take_turns("na_y")
            square_sum("na_p", "na_out")
            norm_turn_resid("ffn2_1", 8 * NT)
            swiglu("ffn2_1")
            square_sum("ffn2_1_p", "ffn2_1")

        @block.vector
        def _(dve):
            ahead, chained, resid = [0], [0], [0]

            def lo(n, it=None):
                dve.wait_ge(hi_done, shifted(n + 1, it, 6))
                dve.tensor_tensor(w_lo[:, n % SPLIT, 0:LO_V], raw[:, n % RAW, 0:LO_V],
                                  w_hi[:, n % SPLIT, 0:LO_V].bitcast(F32), ALU.subtract).then_inc(lo_v_done, 1)

            def split_through(n):
                while ahead[0] <= min(n, CHUNKS - 1):
                    lo(ahead[0])
                    ahead[0] += 1

            def link(ins):
                chained[0] += 1
                ins.then_inc(dve_chain, 1)
                dve.wait_ge(dve_chain, chained[0])

            def scaled(name, src):
                i = NORM_AT[name]
                dve.wait_ge(gain_landed[i % 2], 16 * (i // 2 + 1))
                if TURN_BASE[name]:
                    dve.wait_ge(turned, TURN_BASE[name])
                for t in range(NT):
                    if name == "mix":
                        dve.wait_ge(x_landed[t], 16)
                    for half in range(2):
                        c = slice(512 * half, 512 * half + 512)
                        dve.tensor_tensor(y[:, t, c], src[:, t, c], gain[:, i % 2, c], ALU.mult).then_inc(turn_src, 1)
                dve.wait_ge(turn_src, TURN_BASE[name] + 4)
                dve.sem_inc(gain_used, 1)

            def take_turns(name, t=None):
                banks = TURN_BANKS[name]
                for i in range(banks):
                    tt, kk = divmod(i, banks // NT)
                    if t is not None and tt != t:
                        continue
                    dve.wait_ge(turn_hi, TURN_BASE[name] + i + 1)
                    xh = x_hi[:, tt, 4 * kk:4 * kk + 4, :].bitcast(F32)
                    dve.tensor_tensor(x_lo[:, tt, 4 * kk:4 * kk + 4, :], psum[:, i, :].rearrange("p (k c) -> p k c", k=4),
                                      xh, ALU.subtract).then_inc(turn_lo, 1)

            def take_projection(name):
                j, n = PROJ_AT[name], PROJ_CHUNK[name]
                split_through(n + 3)
                if name == "gg":
                    return
                dve.wait_ge(weights_used, n + 2)
                dve.wait_ge(rstdq_ready, SCALED.index("mix" if norm_of(name) == "mem" else norm_of(name)) + 1)
                dve.wait_ge(rstd_ready, NT * (NORM_AT[norm_of(name)] + 1))
                if j == 1:
                    dve.wait_ge(proj_out1, 1)
                for c0, c1, dst, scale in outlets(name, 1):
                    last = dve.tensor_scalar(dst, psum[:, 2 * (j % 2) + 1, c0:c1], scale, None, ALU.mult)
                last.then_inc(proj_out1, 1)

            def take_k(name, dst):
                for b in range(QKT_BANKS[name]):
                    dve.wait_ge(qk_turned, 2 * (QKT0[name] + b) + 2)
                    dve.tensor_copy(dst[:, 512 * b:512 * b + 512],
                                    psum[:, 5 + 2 * ((QKT0[name] + b) % 2), :]).then_inc(k_out, 1)

            def attention(name, probs, probsT, take_group):
                pairs, gsize, u0 = PAIRS[name], GSIZE[name], UNIT0[name]
                units = NT * pairs
                masked = name in ("fox", "na")

                def keys(n):
                    return (n // pairs + 1) * P if name == "fox" else S

                def maxima(n):
                    u, i = u0 + n, n // pairs
                    dve.wait_ge(scores, u + 1)
                    nm = negmax[:, u % 3, :]
                    if not masked:
                        dve.tensor_reduce(nm, psum[:, u % 4, :].rearrange("p (m k) -> p m k", m=2), AX.X,
                                          ALU.max, negate=True).then_inc(max_done, 1)
                        return
                    if n >= 3:
                        dve.wait_ge(probs_turned, u - 2)
                    if u:
                        dve.wait_ge(max_done, u)
                    for j in range(2):
                        m = score_map(name, n % pairs, j)
                        if name == "fox":
                            mask = causal[:, P - i * P:2 * P]
                        else:
                            mask = nab[:, m, 2 - 2 * i:6 - 2 * i, :].rearrange("p r c -> p (r c)")
                        last = dve.tensor_tensor_reduce(probs[:, u % 3, j, 0:keys(n)], psum[:, u % 4, j * S:j * S + keys(n)],
                                                        mask, 1.0, LOWEST, ALU.add, ALU.max, rrow[:, 6 + j:7 + j])
                    link(last)
                    dve.tensor_scalar(nm, rrow[:, 6:8], -1.0, None, ALU.mult).then_inc(max_done, 1)

                def copy_turned(n):
                    u = u0 + n
                    dve.wait_ge(probs_turned, u + 1)
                    src, dst = psum[:, 4 + u % 2, :], probsT[:, u % 2, :]
                    if keys(n) < S:
                        src, dst = (z.rearrange("p (m k) -> p m k", m=2)[:, :, 0:P] for z in (src, dst))
                    dve.tensor_copy(dst, src).then_inc(probsT_done, 1)

                maxima(0)
                maxima(1)
                for n in range(units):
                    if n + 2 < units:
                        maxima(n + 2)
                    copy_turned(n)
                    if n >= 1 and n % gsize == 0:
                        take_group(n // gsize - 1)
                take_group(units // gsize - 1)

            def weighted(name, dst):
                def take(g):
                    gsize, grp = GSIZE[name], GROUP0[name] + g
                    heads = 2 * gsize
                    dve.wait_ge(pv_done, grp + 1)
                    u = UNIT0[name] + g * gsize
                    r_ = rheads[:, 0:heads]
                    if name == "cross":
                        link(dve.reciprocal(r_, rows[:, u:u + gsize, :].rearrange("p u m -> p (u m)")))
                    else:
                        link(dve.reciprocal(r_.rearrange("p (r j h) -> p r j h", r=2, j=2),
                                            rows[:, u:u + gsize, :].rearrange("p (r h) j -> p r j h", r=2)))
                    last = dve.tensor_tensor(dst(g).rearrange("p (h d) -> p h d", h=heads),
                                             psum[:, 6 + grp % 2, :].rearrange("p (h d) -> p h d", h=heads),
                                             r_.unsqueeze(2).to_broadcast([P, heads, 512 // heads]), ALU.mult)
                    link(last)
                    dve.sem_inc(pv_taken, 1)
                return take

            def take_diff(g):
                grp = GROUP0["diff"] + g
                i, h = divmod(2 * g, 8)
                dve.wait_ge(pv_done, grp + 1)
                u = UNIT0["diff"] + 2 * g
                link(dve.reciprocal(rrow[:, 0:4].rearrange("p (j h) -> p j h", j=2), rows[:, u:u + 2, :].rearrange("p h j -> p j h")))
                link(dve.tensor_scalar(rrow[:, 4:6], rrow[:, 0:4].rearrange("p (h m) -> p h m", m=2)[:, :, 1],
                                       lams[:, 5:6], None, ALU.mult))
                for k in range(2):
                    pv = psum[:, 6 + grp % 2, :]
                    link(dve.tensor_scalar(ropet[:, 0:P], pv[:, 256 * k:256 * k + P], rrow[:, 2 * k:2 * k + 1], None, ALU.mult))
                    link(dve.scalar_tensor_tensor(y[:, i, (h + k) * P:(h + k) * P + P], pv[:, 256 * k + P:256 * k + 2 * P],
                                                  rrow[:, 4 + k:5 + k], ropet[:, 0:P], ALU.mult, ALU.add))
                dve.sem_inc(pv_taken, 1)

            def head_norm(name, view, tmp, gain_):
                k, (heads, d) = HEADNORMS.index(name), view.shape[1:]
                link(dve.tensor_tensor(tmp, view, view, ALU.mult))
                dve.tensor_reduce(hsum[:, 0:heads], tmp, AX.X, ALU.add).then_inc(head_sums, 1)
                dve.wait_ge(head_rstd, k + 1)
                link(dve.tensor_tensor(view, view, hrstd[:, 0:heads].unsqueeze(2).to_broadcast([P, heads, d]), ALU.mult))
                return dve.tensor_tensor(view, view, gain_, ALU.mult)

            def residual(total, following=None, post=None):
                last = START[total] + dict(PHASES)[total] - 1
                split_through(last + 2)
                if post:
                    i = NORM_AT[post]
                    dve.wait_ge(gain_landed[i % 2], 16 * (i // 2 + 1))
                if following:
                    i_next = NORM_AT[following]
                    dve.wait_ge(gain_landed[i_next % 2], 16 * (i_next // 2 + 1))
                    dve.wait_ge(turned, TURN_BASE[following])
                for t in range(NT):
                    if post:
                        dve.wait_ge(rstd_ready, NT * i + t + 1)
                    elif t == 0:
                        dve.wait_ge(sum_t0, SUM_AT[total] + 1)
                    else:
                        dve.wait_ge(weights_used, last + 1)
                    for half in range(2):
                        c = slice(512 * half, 512 * half + 512)
                        bank = psum[:, 4 + 2 * t + half, :]
                        if post:
                            link(dve.scalar_tensor_tensor(y[:, t, c], bank, rstd[:, i, t:t + 1], gain[:, i % 2, c],
                                                          ALU.mult, ALU.mult))
                            bank = y[:, t, c]
                        added = dve.tensor_tensor(x[:, t, c], x[:, t, c], bank, ALU.add)
                        if half == 0:
                            link(added)
                        else:
                            resid[0] += 1
                            added.then_inc(resid_done, 1)
                            dve.wait_ge(resid_done, resid[0])
                        if following:
                            dve.tensor_tensor(y[:, t, c], x[:, t, c], gain[:, i_next % 2, c], ALU.mult).then_inc(turn_src, 1)
                            if t == 1 and half == 0:
                                take_turns(following, 0)
                if following:
                    dve.wait_ge(turn_src, TURN_BASE[following] + 4)
                    dve.sem_inc(gain_used, 2 if post else 1)
                    take_turns(following, 1)

            def swiglu(name):
                base, groups, gu0 = START[name], FFN[name], GU0[name]

                def hidden(g, it=None):
                    par = (gu0 + g) % 2
                    for t in range(NT):
                        if name == "moe":
                            e = bass.ds(it + g // 2, 1) if it is not None else slice(g // 2, g // 2 + 1)
                            scale = gates[:, t, e]
                        else:
                            scale = rstd[:, NORM_AT[name], t:t + 1]
                        dve.wait_ge(silu_done, shifted(NT * (gu0 + g) + t + 1, it, 2 * NT))
                        dve.scalar_tensor_tensor(hid[:, par, t, :], psum[:, 2 * par + t, GROUP:2 * GROUP], scale,
                                                 silu[:, par, t, :], ALU.mult, ALU.mult).then_inc(hid_done, 1)

                def take_hidden(g, it=None):
                    par = (gu0 + g) % 2
                    dve.wait_ge(hid_hi, shifted(gu0 + g + 1, it, 2))
                    dve.tensor_tensor(h_lo[:, par, :, :], psum[:, 2 * par, :].rearrange("p (f s) -> p f s", f=2),
                                      h_hi[:, par, :, :].bitcast(F32), ALU.subtract).then_inc(hid_lo, 1)

                def split(n, it):
                    if n < CHUNKS:
                        lo(n, it)

                def step(n, g, it=None):
                    split(n + 2, it)
                    take_hidden(g, it)
                    split(n + 3, it)
                    hidden(g + 1, it)
                    split(n + 4, it)

                split_through(base + 3)
                hidden(0)
                peel = name == "ffn2_1"
                with dve.Fori(0, (groups - 1) // 2 - peel) as it:
                    step(base + 2, 0, it)
                    step(base + 5, 1, it)
                for g in range((groups - 1) // 2 * 2 - 2 * peel, groups - 1):
                    step(base + 2 + 3 * g, g)
                ahead[0] = base + 3 * groups + 1
                take_hidden(groups - 1)

            def take_gather(w):
                for kk in range(2):
                    dve.wait_ge(gathered_hi, 2 * w + kk + 1)
                    part = (slice(None), w % 2, slice(4 * kk, 4 * kk + 4), slice(None))
                    dve.tensor_tensor(x_lo[part], psum[:, 2 + kk, :].rearrange("p (k c) -> p k c", k=4),
                                      x_hi[part].bitcast(F32), ALU.subtract).then_inc(gathered_lo, 1)

            def experts():
                base = START["moe"]

                def hidden(w, g, it=None):
                    e = bass.ds(it + (g % 8) // 2, 1) if it is not None else slice((g % 8) // 2, (g % 8) // 2 + 1)
                    by_group = slotv[:, w, 4 * w:4 * w + 4]
                    dve.wait_ge(silu_done, shifted(NT * (g + 1), it, 2 * NT))
                    dve.scalar_tensor_tensor(hid[:, g % 2, 0, :], psum[:, g % 2, GROUP:2 * GROUP], by_group[:, e],
                                             silu[:, g % 2, 0, :], ALU.mult, ALU.mult).then_inc(hid_done, NT)

                def take_hidden(g, it=None):
                    dve.wait_ge(hid_hi, shifted(g + 1, it, 2))
                    dve.tensor_tensor(h_lo[:, g % 2, :, 0:P], psum[:, g % 2, 0:2 * P].rearrange("p (f s) -> p f s", f=2),
                                      h_hi[:, g % 2, :, 0:P].bitcast(F32), ALU.subtract).then_inc(hid_lo, 1)

                def step(g, it=None, between=None):
                    n = base + 2 + 3 * g
                    lo(n + 2, it)
                    if between is not None:
                        between()
                    take_hidden(g, it)
                    lo(n + 3, it)
                    hidden((g + 1) // 8, g + 1, it)
                    lo(n + 4, it)

                def take_scatter(w):
                    if w:
                        dve.wait_ge(scatter_taken, NT * w)
                    for t in range(NT):
                        dve.wait_ge(scattered, NT * w + t + 1)
                        banks = psum[:, 2:4, :] if t == 0 else psum[:, 4 + 2 * (w % 2):6 + 2 * (w % 2), :]
                        x_ = x[:, t, :].rearrange("p (b c) -> p b c", b=2)
                        dve.tensor_tensor(x_, x_, banks, ALU.add).then_inc(scatter_taken, 1)

                split_through(base + 3)
                dve.wait_ge(slotv_done, 1)
                dve.tensor_copy(slotv, psum[:, 5, 32:160].rearrange("p (w c) -> p w c", w=WINDOWS)[:, :, 0:17]).then_inc(slotv_out, 1)
                dve.wait_ge(slotv_out, 1)
                hidden(0, 0)
                for t in range(NT):
                    link(dve.tensor_scalar(rt[:, t, 105:106], rt[:, t, 104:105], -128.0, None, ALU.add))
                    dve.tensor_scalar(over_pick[:, t, :], slots, rt[:, t, 105:106], None, ALU.is_equal)
                v = rt[:, 0, :]
                link(dve.max(v[:, 120:128], v[:, 112:120]))
                link(dve.max_index(v[:, 128:136].bitcast(U32), v[:, 120:128], v[:, 112:120]))
                link(dve.tensor_scalar(v[:, 138:139], v[:, 120:121], P + 0.5, None, ALU.is_gt))
                dve.tensor_copy(v[:, 139:140].bitcast(I32), v[:, 138:139]).then_inc(over_known, 1)
                for w in range(WINDOWS):
                    with dve.Fori(0, 3) as it:
                        step(8 * w, it)
                        step(8 * w + 1, it)
                    if w:
                        take_scatter(w - 1)
                    step(8 * w + 6, None, (lambda: take_gather(w + 1)) if w < WINDOWS - 1 else None)
                    if w < WINDOWS - 1:
                        step(8 * w + 7)
                ahead[0] = base + 24 * WINDOWS + 1
                take_hidden(8 * WINDOWS - 1)
                split_through(base + 24 * WINDOWS + 1)
                take_scatter(WINDOWS - 1)
                dve.wait_ge(over_known, 1)
                with dve.If(dve.value_load(is_over, min_val=0, max_val=1) > 0):
                    group = dve.value_load(over_group, min_val=0, max_val=WINDOWS - 1)
                    dve.wait_ge(scatter_taken, NT * WINDOWS)
                    dve.wait_ge(over_in, 1)
                    dve.tensor_copy(over_x.rearrange("p k s -> p (k s)"), psum[:, 0:2, :].rearrange("p b c -> p (b c)"))
                    dve.tensor_copy(over_pickT.rearrange("p t s -> p (t s)"), psum[:, 2, 0:256])
                    dve.tensor_copy(over_slotv, psum[:, 3, 0:17]).then_inc(over_taken, 1)
                    dve.wait_ge(over_taken, 1)
                    with dve.Fori(0, 4) as it:
                        dve.wait_ge(over_silued, it + 1)
                        dve.wait_ge(over_up, it + 1)
                        dve.scalar_tensor_tensor(over_hid, psum[:, 1, :], over_slotv[:, bass.ds(group * 4 + it, 1)],
                                                 over_silu, ALU.mult, ALU.mult).then_inc(over_hidden, 1)
                        dve.wait_ge(over_turned, it + 1)
                        dve.tensor_copy(over_hidT, psum[:, 2, :]).then_inc(over_hidT_out, 1)
                    dve.wait_ge(over_down, 5)
                    dve.tensor_copy(slot_y, psum[:, 4:6, :].rearrange("p b c -> p (b c)")).then_inc(over_y_out, 1)
                    dve.wait_ge(over_scattered, 1)
                    for t in range(NT):
                        dve.tensor_tensor(x[:, t, :], x[:, t, :], psum[:, 2 * t:2 * t + 2, :].rearrange("p b c -> p (b c)"),
                                          ALU.add).then_inc(over_added, 1)
                    dve.wait_ge(over_added, NT)
                dve.wait_ge(scatter_taken, NT * WINDOWS)
                dve.sem_inc(resid_done, NT)
                resid[0] += NT

            scaled("mix", x)
            dve.wait_ge(const_landed, 16)
            take_turns("mix")
            split_through(PROJ_CHUNK["gqk"] + 2)
            dve.wait_ge(logits_done, 1)
            dve.wait_ge(mixw_landed, 16 * MIX_LOADS)
            dve.wait_ge(rstd_ready, NT)
            for t in range(NT):
                link(dve.tensor_scalar(lg[:, t, 0:24], psum[:, 4, t * 64:t * 64 + 24], rstd[:, 0, t:t + 1], None, ALU.mult))
            link(dve.tensor_tensor(lg[:, :, 0:8], lg[:, :, 0:8], bias_g[:, 0:8].unsqueeze(1).to_broadcast([P, NT, 8]), ALU.add))
            dve.sem_inc(logits_out, 1)
            dve.wait_ge(ga_turned, 1)
            dve.tensor_copy(gaT[0:16, :], psum[0:16, 5, 0:S]).then_inc(ga_out, 1)
            take_projection("gqk")
            dve.wait_ge(alpha_done, 1)
            dve.tensor_tensor(lg[:, :, 8:264], psum[:, 6, :].rearrange("p (t c) -> p t c", t=NT),
                              bias_g[:, 8:264].unsqueeze(1).to_broadcast([P, NT, 256]), ALU.add).then_inc(logits_in, 1)
            take_k("gla", gkT)
            dve.wait_ge(logsig_ln, 1)
            dve.scalar_tensor_tensor(lg, lg, 0.0, lsg, ALU.min, ALU.subtract).then_inc(logsig_done, 1)
            take_projection("gv")
            dve.wait_ge(decay_done, 1)
            dve.tensor_copy(gb, psum[:, 4, :]).then_inc(gb_out, 1)
            dve.wait_ge(decay_done, 3)
            dve.tensor_scalar(ct[0:8, :], psum[0:8, 7, 0:S], -1.0, None, ALU.mult).then_inc(ct_out, 1)
            dve.wait_ge(suffix_out, 1)
            dve.wait_ge(proj_out0, 2)
            dve.wait_ge(k_out, 1)
            dve.tensor_tensor(gks, gqk[:, :, 256:512], gs.rearrange("p (t c) -> p t c", t=NT), ALU.mult).then_inc(ks_ready, 1)
            take_projection("fq")
            dve.wait_ge(expb_ready, 1)
            dve.wait_ge(q_out, 1)
            dve.wait_ge(ks_ready, 1)
            dve.tensor_tensor(gs, gqT, gexp, ALU.mult).then_inc(qb_ready, 1)
            dve.wait_ge(u_done, 1)
            u_ = [psum[:, 6, 0:256], psum[:, 7, 0:256], psum[:, 6, 256:512]]
            link(dve.tensor_copy(st[:, 0, :, :], u_[0].rearrange("p (f v) -> p f v", f=2)))
            for c in (1, 2):
                for f in range(2):
                    last = dve.scalar_tensor_tensor(st[:, c, f, :], st[:, c - 1, f, :],
                                                    gexp[:, f * S + c * 64 + 63:f * S + c * 64 + 64],
                                                    u_[c][:, f * P:f * P + P], ALU.mult, ALU.add)
                link(last)
            dve.sem_inc(state_ready, 1)

            def level_start(l):
                h = 1 << l
                if l:
                    dve.wait_ge(z_ready, l)
                v = gb.rearrange("p (n c) -> p n c", c=2 * h)
                dve.tensor_tensor(ge.rearrange("p (n c) -> p n c", c=2 * h), v,
                                  v[:, :, h - 1:h].to_broadcast([P, 512 // (2 * h), 2 * h]), ALU.subtract).then_inc(diff_ready, 1)

            def level_operand(l):
                h = 1 << l
                dve.wait_ge(decay_exp, l + 1)
                if l >= 2:
                    dve.wait_ge(level_done, l - 1)
                v = [z.rearrange("p (n c) -> p n c", c=2 * h) for z in (gz[:, l % 2, :], gkT, gqT, ge)]
                dve.tensor_tensor(v[0][:, :, 0:h], v[1][:, :, 0:h], v[3][:, :, 0:h], ALU.mult)
                dve.tensor_tensor(v[0][:, :, h:2 * h], v[2][:, :, h:2 * h], v[3][:, :, h:2 * h], ALU.mult).then_inc(z_ready, 1)

            def level_take(l):
                dve.wait_ge(level_done, l + 1)
                dve.wait_ge(level_out if l else at_zero, max(l, 1))
                mask = masks[:, l * P:l * P + P].unsqueeze(1).unsqueeze(1).to_broadcast([P, NT, 2, P])
                for h in range(2):
                    last = dve.copy_predicated(at_.rearrange("p t (g h) q -> p t g h q", h=2)[:, :, :, h, :], mask,
                                               psum[:, 4 + 2 * (l % 2) + h, :].rearrange("p (t g q) -> p t g q", t=NT, g=2))
                last.then_inc(level_out, 1)

            dve.wait_ge(gb_out, 1)
            for l in range(LEVELS):
                if l >= 2 and l % 2 == 0:
                    take_projection("fk" if l == 2 else "fv")
                level_start(l)
                if l >= 1:
                    level_take(l - 1)
                level_operand(l)
            level_take(LEVELS - 1)
            level_take(LEVELS)
            dve.wait_ge(gla_o_done, 1)
            for h in range(2):
                dst = y[:, :, 512:1024].rearrange("p t (g h v) -> p t g h v", g=2, h=2)[:, :, :, h, :]
                last = dve.tensor_copy(dst, psum[:, 6 + h, :].rearrange("p (t g v) -> p t g v", t=NT, g=2))
            last.then_inc(gla_o_out, 1)
            take_k("fox", region(6144, 1024))
            attention("fox", probs_1, probsT_1, weighted("fox", lambda g: y[:, g, 0:512]))
            dve.wait_ge(squared, NT * NORM_AT["mem"] + NT)
            head_norm("fox", y[:, 1, 0:512].rearrange("p (h d) -> p h d", h=8), fb[:, 1536:2048].rearrange("p (h d) -> p h d", h=8),
                      fox_gain.rearrange("p (h d) -> p h d", h=8)).then_inc(dve_chain, 1)
            chained[0] += 1
            take_turns("mem")
            dve.wait_ge(dve_chain, chained[0])
            dve.wait_ge(heads_normed, 2)
            dve.sem_inc(turn_src, 4)
            take_projection("xk")
            take_projection("xv")
            take_turns("mix_y")
            split_through(START["mix_out"] + 5)
            residual("mix_out", "cross")
            take_projection("xq")
            take_k("cross", region(4096, 1024))
            attention("cross", probs_1, probsT_1, weighted("cross", lambda g: y[:, g, 0:512]))
            dve.sem_inc(turn_src, 2)
            take_turns("cross_y")
            residual("cross_out", "moe")
            split_through(START["moe"] + 2)
            dve.wait_ge(logits_done, 2)
            dve.wait_ge(router_landed, 16 * 5)
            dve.wait_ge(rstd_ready, NT * (NORM_AT["moe"] + 1))
            dve.memset(rt[:, 0, 112:120], NEG)
            link(dve.memset(rt[:, :, 24:40], NEG))
            for t in range(NT):
                link(dve.scalar_tensor_tensor(rt[:, t, 0:20], psum[:, 4, t * 64:t * 64 + 20], rstd[:, NORM_AT["moe"], t:t + 1],
                                              b_router, ALU.mult, ALU.add))
            dve.sem_inc(logits_out, 1)
            for t in range(NT):
                v = rt[:, t, :]
                g8, top, idx, sc = v[:, 24:32], v[:, 40:48], v[:, 48:56].bitcast(U32), v[:, 64:80]
                link(dve.tensor_copy(g8[:, 0:4], v[:, 0:4]))
                link(dve.max(top, g8))
                link(dve.max_index(idx, top, g8))
                dve.tensor_scalar(sc[:, 0:1], top[:, 0:1], -1.0, None, ALU.mult).then_inc(route_in, 1)
                link(dve.tensor_copy(sc[:, 4:5], idx[:, 0:1]))
                link(dve.tensor_scalar(v[:, 56:60], iota4, sc[:, 4:5], None, ALU.is_equal))
            dve.sem_inc(hot_ready, 1)
            dve.wait_ge(ranked, 1)
            for t in range(NT):
                v = rt[:, t, :]
                link(dve.tensor_tensor(v[:, 96:100], psum[:, 5, 8 * t:8 * t + 4], v[:, 56:60], ALU.mult))
                link(dve.tensor_reduce(v[:, 104:105], v[:, 96:100], AX.X, ALU.add))
            dve.tensor_copy(rt[:, 0, 112:116], psum[:, 5, 16:20])
            for w in range(WINDOWS):
                for t in range(NT):
                    dve.tensor_scalar(pick[:, w, t, :], slots, rt[:, t, 104:105], rt[:, t, 56 + w:57 + w],
                                      ALU.is_equal, ALU.mult).then_inc(pick_ready, 1)
            take_gather(0)
            for t in range(NT):
                v = rt[:, t, :]
                e8, top, idx, sc = v[:, 32:40], v[:, 40:48], v[:, 48:56].bitcast(U32), v[:, 64:80]
                hot, two = v[:, 56:60], v[:, 84:92]
                link(dve.tensor_scalar(e8[:, 0:4], v[:, 4:8], hot[:, 0:1], None, ALU.mult))
                for g in range(1, 4):
                    link(dve.scalar_tensor_tensor(e8[:, 0:4], v[:, 4 + 4 * g:8 + 4 * g], hot[:, g:g + 1], e8[:, 0:4], ALU.mult, ALU.add))
                link(dve.max(top, e8))
                link(dve.max_index(idx, top, e8))
                dve.tensor_tensor(sc[:, 2:3], top[:, 1:2], top[:, 0:1], ALU.subtract).then_inc(route_in, 1)
                link(dve.tensor_copy(sc[:, 4:6], idx[:, 0:2]))
                dve.wait_ge(route_exp, NT + t + 1)
                link(dve.tensor_scalar(sc[:, 6:7], sc[:, 3:4], 1.0, None, ALU.add))
                link(dve.tensor_tensor(sc[:, 6:7], sc[:, 6:7], sc[:, 1:2], ALU.mult))
                link(dve.reciprocal(sc[:, 7:8], sc[:, 6:7]))
                link(dve.tensor_tensor(sc[:, 7:8], sc[:, 7:8], rstd[:, NORM_AT["moe"], t:t + 1], ALU.mult))
                link(dve.tensor_tensor(sc[:, 8:9], sc[:, 7:8], sc[:, 3:4], ALU.mult))
                dve.tensor_scalar(two[:, 0:4], iota4, sc[:, 4:5], sc[:, 7:8], ALU.is_equal, ALU.mult)
                link(dve.tensor_scalar(two[:, 4:8], iota4, sc[:, 5:6], sc[:, 8:9], ALU.is_equal, ALU.mult))
                link(dve.tensor_tensor(two[:, 0:4], two[:, 0:4], two[:, 4:8], ALU.add))
                for g in range(4):
                    dve.tensor_scalar(gates[:, t, 4 * g:4 * g + 4], two[:, 0:4], hot[:, g:g + 1], None, ALU.mult)
                link(dve.tensor_copy(gates[:, t, 16:17], rstd[:, NORM_AT["moe"], t:t + 1]))
            dve.sem_inc(gates_ready, 1)
            experts()
            i = NORM_AT["final"]
            dve.wait_ge(rstd_ready, NT * (i + 1))
            dve.wait_ge(gain_landed[i % 2], 16 * (i // 2 + 1))
            for t in range(NT):
                dve.scalar_tensor_tensor(x[:, t, :], x[:, t, :], rstd[:, i, t:t + 1], gain[:, i % 2, :], ALU.mult,
                                         ALU.mult).then_inc(resid_done, 1)
                resid[0] += 1
            dve.wait_ge(resid_done, resid[0])
            dve.sem_inc(gain_used, 1)
            scaled("ffn1_0", x)
            take_turns("ffn1_0")
            dve.wait_ge(diffw_landed, 32)
            for k in range(2):
                last = dve.tensor_tensor_reduce(ropet[:, 64 * k:64 * k + 64], lamv[:, 128 * k:128 * k + 64], lamv[:, 128 * k + 64:128 * k + 128],
                                                1.0, 0.0, ALU.mult, ALU.add, lams[:, k:k + 1])
            last.then_inc(lam_sum, 1)
            dve.wait_ge(lam_exp, 1)
            link(dve.tensor_tensor(lams[:, 4:5], lams[:, 2:3], lams[:, 3:4], ALU.subtract))
            link(dve.tensor_scalar(lams[:, 5:6], lams[:, 4:5], 0.2, -1.0, ALU.add, ALU.mult))
            swiglu("ffn1_0")
            residual("ffn1_0", "diff", "ffn1_0_p")
            for name in PROJ[9:15]:
                take_projection(name)
            dve.wait_ge(proj_out0, 15)
            dve.wait_ge(proj_out1, 15)
            for turn_, z in enumerate((q2, y)):
                if turn_:
                    dve.wait_ge(rope_done, 1)
                z4 = z.rearrange("p t (m c) -> p t m c", m=16)
                x1, x2 = z4[:, :, :, 0:8], z4[:, :, :, 8:16]
                cos, sin = (rope[:, :, k, :].unsqueeze(2).to_broadcast([P, NT, 16, 8]) for k in range(2))
                tt = [ropet[:, 256 * k:256 * k + 256].rearrange("p (t m c) -> p t m c", t=NT, m=16) for k in range(4)]
                dve.tensor_tensor(tt[0], x1, cos, ALU.mult)
                dve.tensor_tensor(tt[1], x2, sin, ALU.mult)
                dve.tensor_tensor(tt[2], x2, cos, ALU.mult)
                link(dve.tensor_tensor(tt[3], x1, sin, ALU.mult))
                link(dve.tensor_tensor(x1, tt[0], tt[1], ALU.subtract))
                dve.tensor_tensor(x2, tt[2], tt[3], ALU.add).then_inc(rope_done, 1)
            take_k("diff", region(4608, 2048))
            attention("diff", probs_2, probsT_2, take_diff)
            dve.wait_ge(heads_normed, 3)
            dve.sem_inc(turn_src, 2)
            head_norm("diff", y[:, 1, 512:1024].rearrange("p (h d) -> p h d", h=4), region(10240, 512).rearrange("p (h d) -> p h d", h=4),
                      subln.unsqueeze(1).to_broadcast([P, 4, P])).then_inc(dve_chain, 1)
            chained[0] += 1
            dve.wait_ge(dve_chain, chained[0])
            dve.wait_ge(heads_normed, 4)
            dve.sem_inc(turn_src, 2)
            take_turns("diff_y")
            residual("diff_out", "ffn2_0", "diff_p")
            swiglu("ffn2_0")
            residual("ffn2_0", "ffn1_1", "ffn2_0_p")
            swiglu("ffn1_1")
            residual("ffn1_1", "na", "ffn1_1_p")
            dve.wait_ge(nab_landed, 16)
            dve.wait_ge(namask_landed, 16)
            for name in PROJ[15:21]:
                take_projection(name)
                if name in PROJ[15:19]:
                    k = PROJ[15:19].index(name)
                    v = nab[:, 4 * k:4 * k + 4, :, :]
                    dve.tensor_tensor(v, v, namask.unsqueeze(1).unsqueeze(1).to_broadcast([P, 4, 6, 64]), ALU.add).then_inc(nab_ready, 1)
            dve.wait_ge(nab_ready, 4)
            take_k("na", region(4608, 2048))
            attention("na", probs_2, probsT_2, weighted("na", lambda g: y[:, g // 2, (g % 2) * 512:(g % 2) * 512 + 512]))
            dve.sem_inc(turn_src, 4)
            take_turns("na_y")
            residual("na_out", "ffn2_1", "na_p")
            swiglu("ffn2_1")
            residual("ffn2_1", None, "ffn2_1_p")

        @block.gpsimd
        def _(pool):
            ahead, chained = [0], [0]

            def lo(n, it=None):
                pool.wait_ge(hi_done, shifted(n + 1, it, 6))
                pool.tensor_tensor(w_lo[:, n % SPLIT, LO_V:CHUNK], raw[:, n % RAW, LO_V:CHUNK],
                                   w_hi[:, n % SPLIT, LO_V:CHUNK].bitcast(F32), ALU.subtract).then_inc(lo_p_done, 1)

            def split_through(n):
                while ahead[0] <= min(n, CHUNKS - 1):
                    lo(ahead[0])
                    ahead[0] += 1

            def link(ins):
                chained[0] += 1
                ins.then_inc(pool_chain, 1)
                pool.wait_ge(pool_chain, chained[0])

            def inverse_rms(name):
                i, f = NORM_AT[name], NORM_FACTOR.get(name, 1.0) ** -2
                for t in range(NT):
                    if NT * i + t:
                        pool.wait_ge(rstd_ready, NT * i + t)
                    pool.wait_ge(squared, NT * i + t + 1)
                    link(pool.tensor_scalar(vtmp[:, 0:1], sums[:, i, t:t + 1], f / D, f * EPS, ALU.mult, ALU.add))
                    pool.tensor_tensor(rstd[:, i, t:t + 1], vtmp[:, 0:1], neghalf[:, 0:1], ALU.pow).then_inc(rstd_ready, 1)
                if name in SCALED:
                    pool.wait_ge(rstd_ready, NT * (i + 1))
                    pool.tensor_scalar(rstd_q[:, SCALED.index(name), :], rstd[:, i, :], SCORE_SCALE[name], None,
                                       ALU.mult).then_inc(rstdq_ready, 1)

            def inverse_head_rms(name, heads, d, factor=1.0):
                k, f = HEADNORMS.index(name), factor ** -2
                pool.wait_ge(head_sums, k + 1)
                link(pool.tensor_scalar(htmp[:, 0:heads], hsum[:, 0:heads], f / d, f * EPS, ALU.mult, ALU.add))
                pool.tensor_tensor(hrstd[:, 0:heads], htmp[:, 0:heads], neghalf[:, 0:heads], ALU.pow).then_inc(head_rstd, 1)

            def head_norm(view, tmp, gain_, more=None, factor=1.0):
                (heads, d), f = view.shape[1:], factor ** -2
                sums_, r_ = pool_heads[:, 0:heads], pool_heads[:, 8:8 + heads]
                link(pool.tensor_tensor(tmp, view, view, ALU.mult))
                n = d
                while n > 1:
                    n //= 2
                    link(pool.tensor_tensor(tmp[:, :, 0:n], tmp[:, :, 0:n], tmp[:, :, n:2 * n], ALU.add))
                link(pool.tensor_scalar(sums_.unsqueeze(2), tmp[:, :, 0:1], f / d, f * EPS, ALU.mult, ALU.add))
                link(pool.tensor_tensor(r_, sums_, neghalf[:, 0:heads], ALU.pow))
                link(pool.tensor_tensor(view, view, r_.unsqueeze(2).to_broadcast([P, heads, d]), ALU.mult))
                if more is not None:
                    link(pool.tensor_tensor(view, view, more, ALU.mult))
                link(pool.tensor_tensor(view, view, gain_, ALU.mult))

            def swiglu(name):
                base, groups = START[name], FFN[name]
                peel = name == "ffn2_1"

                def splits(n, it=None):
                    for k in range(2, 8 if it is not None else 5):
                        if n + k < CHUNKS:
                            lo(n + k, it)

                split_through(base + 3)
                with pool.Fori(0, (groups - 1) // 2 - peel) as it:
                    splits(base + 2, it)
                for g in range((groups - 1) // 2 * 2 - 2 * peel, groups - 1):
                    splits(base + 2 + 3 * g)
                ahead[0] = base + 3 * groups + 1

            pool.memset(zeros[:, :], 0.0).then_inc(zeros_ready, 1)
            pool.wait_ge(const_landed, 16)
            split_through(2)
            inverse_rms("mix")
            pool.memset(fb[:, 1024:2048], 0.0).then_inc(at_zero, 1)
            split_through(START["mix_in"] + 13)
            pool.wait_ge(gla_o_out, 1)
            for t in range(NT):
                head_norm(y[:, t, 512:1024].rearrange("p (h d) -> p h d", h=4), fb[:, 0:512].rearrange("p (h d) -> p h d", h=4),
                          gla_gain.rearrange("p (h d) -> p h d", h=4), gg[:, t, :].rearrange("p (h d) -> p h d", h=4))
            pool.sem_inc(heads_normed, 1)
            i = NORM_AT["mem"]
            inverse_rms("mem")
            pool.wait_ge(mem_landed, 16)
            pool.wait_ge(gain_landed[i % 2], 16 * (i // 2 + 1))
            for t in range(NT):
                for half in range(2):
                    c = slice(512 * half, 512 * half + 512)
                    pool.tensor_tensor(mem[:, t, c], mem[:, t, c], gain[:, i % 2, c], ALU.mult).then_inc(turn_src, 1)
            pool.wait_ge(turn_src, TURN_BASE["mem"] + 4)
            pool.sem_inc(gain_used, 1)
            pool.wait_ge(pv_taken, GROUP0["fox"] + 1)
            head_norm(y[:, 0, 0:512].rearrange("p (h d) -> p h d", h=8), fb[:, 1024:1536].rearrange("p (h d) -> p h d", h=8),
                      fox_gain.rearrange("p (h d) -> p h d", h=8))
            pool.sem_inc(heads_normed, 1)
            inverse_head_rms("fox", 8, 64)
            split_through(START["mix_out"] + 5)
            inverse_rms("cross")
            split_through(START["cross_out"] + 3)
            inverse_rms("moe")
            swiglu("moe")
            split_through(START["moe"] + 3 * MOE_GROUPS + 1)
            inverse_rms("final")
            inverse_rms("ffn1_0")
            swiglu("ffn1_0")
            split_through(START["ffn1_0"] + 3 * FF_GROUPS + 1)
            inverse_rms("ffn1_0_p")
            inverse_rms("diff")
            split_through(START["diff_in"] + 13)
            for groups, t, c0, c1 in ((4, 0, 0, 1024), (6, 1, 0, 512)):
                pool.wait_ge(pv_taken, GROUP0["diff"] + groups)
                heads = (c1 - c0) // P
                head_norm(y[:, t, c0:c1].rearrange("p (h d) -> p h d", h=heads),
                          region(9216, c1 - c0).rearrange("p (h d) -> p h d", h=heads),
                          subln.unsqueeze(1).to_broadcast([P, heads, P]), None, 1.0 - (0.8 - 0.6))
                pool.sem_inc(heads_normed, 1)
            inverse_head_rms("diff", 4, P, 1.0 - (0.8 - 0.6))
            split_through(START["diff_out"] + 5)
            inverse_rms("diff_p")
            inverse_rms("ffn2_0")
            swiglu("ffn2_0")
            split_through(START["ffn2_0"] + 3 * FF_GROUPS + 1)
            inverse_rms("ffn2_0_p")
            inverse_rms("ffn1_1")
            swiglu("ffn1_1")
            split_through(START["ffn1_1"] + 3 * FF_GROUPS + 1)
            inverse_rms("ffn1_1_p")
            inverse_rms("na")
            split_through(START["na_out"] + 5)
            inverse_rms("na_p")
            inverse_rms("ffn2_1")
            swiglu("ffn2_1")
            inverse_rms("ffn2_1_p")


def toeplitz(rpb):
    j, c, s, k = np.ix_(range(2), range(64), range(6), range(64))
    laid = rpb[0][:, 5 - j + s, np.clip(k - c + 15, 0, 30)]
    return np.ascontiguousarray(laid.transpose(1, 2, 0, 3, 4)).reshape(P, 16 * 6 * 64)


_INS = ["x", "mem", "mem_norm", "mix_norm", "w_in", "b_forget", "w_alpha_up", "b_alpha", "fox_out_gain",
        "gla_out_gain", "w_out", "cross_norm", "w_xq", "w_xk", "w_xv", "w_xo", "moe_norm", "w_router_group",
        "b_router_group", "w_router_expert", "b_router_expert", "w_expert_gate", "w_expert_up",
        "w_expert_down", "final_norm", "norm_g_2", "ffn1_wg_2", "ffn1_wu_2", "ffn1_wd_2", "ffn2_wg_2",
        "ffn2_wu_2", "ffn2_wd_2", "diff_w_in_2", "diff_w_out_2", "diff_lambda_2", "diff_subln_2",
        "na_w_in_2", "na_w_out_2"]


def kernel(**inputs):
    import numpy as _np
    import concourse.bacc as _bacc
    from concourse import mybir as _mybir
    from concourse.bass_utils import run_bass_kernel_spmd as _run

    nc = _bacc.Bacc("TRN2", target_bir_lowering=False, num_devices=1)
    consts, masks = shape_constants()
    arrays = {name: _np.ascontiguousarray(inputs[name]) for name in _INS}
    arrays["consts"], arrays["masks"] = consts, masks
    arrays["na_biases"] = toeplitz(_np.asarray(inputs["na_rpb_2"]))
    aps = {}
    for name, v in arrays.items():
        aps[name] = nc.dram_tensor(name, v.shape, _mybir.dt.from_np(v.dtype), kind="ExternalInput").ap()
    out = nc.dram_tensor("out", (1, S, D), _mybir.dt.float32, kind="ExternalOutput").ap()
    two_blocks(nc, aps, out)
    r = _run(nc, [arrays], core_ids=[0])
    return r.results[0]["out"]
```

```python
from contextlib import ExitStack

import numpy as np
import concourse.bass as bass
from concourse import mybir

F32 = mybir.dt.float32
F32R = mybir.dt.float32r
U8 = mybir.dt.uint8
I32 = mybir.dt.int32
U32 = mybir.dt.uint32
ALU = mybir.AluOpType
ACT = mybir.ActivationFunctionType
AX = mybir.AxisListType

P = 128
S = 256
NT = S // P
D = 1024
KD = D // P
EPS = 1e-6
NEG = -1e30
LOWEST = -3e38
CHUNK = 2048
RAW = 6
SPLIT = 3
LO_V = 1280
GROUP = 256
FF_GROUPS = 2816 // GROUP
MOE_GROUPS = 16 * 512 // GROUP
WINDOWS = 4
GLA_C = 64
LEVELS = 6

PHASES = [("mix_in", 12), ("mem_kv", 4), ("mix_out", 4), ("cross_q", 2), ("cross_out", 2),
          ("moe", 3 * MOE_GROUPS), ("ffn1_0", 3 * FF_GROUPS), ("diff_in", 12), ("diff_out", 4),
          ("ffn2_0", 3 * FF_GROUPS), ("ffn1_1", 3 * FF_GROUPS), ("na_in", 12), ("na_out", 4),
          ("ffn2_1", 3 * FF_GROUPS)]
START, _n = {}, 0
for _name, _count in PHASES:
    START[_name] = _n
    _n += _count
CHUNKS = _n

TURNS = ["mix", "mem", "mix_y", "cross", "cross_y", "moe", "ffn1_0", "diff", "diff_y", "ffn2_0",
         "ffn1_1", "na", "na_y", "ffn2_1"]
TURN_BANKS = {name: 2 if name == "cross_y" else 4 for name in TURNS}
TURN_BASE = {name: sum(TURN_BANKS[x] for x in TURNS[:i]) for i, name in enumerate(TURNS)}

TURN_FIRST = {name: 2 if name in ("diff", "na", "ffn2_0", "ffn2_1") else 0 for name in TURNS}


def turn_bank(name, i):
    return (TURN_FIRST[name] + i) % 4


NORMS = ["mix", "mem", "cross", "moe", "final", "ffn1_0", "ffn1_0_p", "diff", "diff_p", "ffn2_0",
         "ffn2_0_p", "ffn1_1", "ffn1_1_p", "na", "na_p", "ffn2_1", "ffn2_1_p"]
NORM_AT = {name: i for i, name in enumerate(NORMS)}
NORM_FACTOR = {"ffn1_0_p": 0.5, "ffn2_0_p": 0.5, "ffn1_1_p": 0.5, "ffn2_1_p": 0.5}
SCORE_SCALE = {"mix": 64 ** -0.5, "cross": 128 ** -0.5, "diff": 64 ** -0.5, "na": 64 ** -0.5}
SCALED = list(SCORE_SCALE)
MIX_LOADS = 9

SUMS = ["mix_out", "cross_out", "ffn1_0", "diff_out", "ffn2_0", "ffn1_1", "na_out", "ffn2_1"]
SUM_AT = {name: i for i, name in enumerate(SUMS)}

PROJ = ["gg", "gqk", "gv", "fq", "fk", "fv", "xk", "xv", "xq", "dq0", "dq1", "dk0", "dk1", "dv0",
        "dv1", "nq0", "nq1", "nk0", "nk1", "nv0", "nv1"]
PROJ_AT = {name: i for i, name in enumerate(PROJ)}
PROJ_CHUNK = {}
for _i, _name in enumerate(PROJ):
    _ph, _first = (("mix_in", 0) if _i < 6 else ("mem_kv", 6) if _i < 8 else ("cross_q", 8) if _i < 9
                   else ("diff_in", 9) if _i < 15 else ("na_in", 15))
    PROJ_CHUNK[_name] = START[_ph] + 2 * (_i - _first)

PAIRS = {"fox": 4, "cross": 2, "diff": 8, "na": 8}
GSIZE = {"fox": 4, "cross": 2, "diff": 2, "na": 4}
UNIT0 = {"fox": 0, "cross": 8, "diff": 12, "na": 28}
GROUP0 = {"fox": 0, "cross": 2, "diff": 4, "na": 12}


def score_map(name, p, j):
    return 2 * p + j if name == "cross" else 4 * (p // 2) + 2 * j + p % 2


QKT_BANKS = {"gla": 1, "fox": 2, "cross": 2, "diff": 4, "na": 4}
QKT0 = {"gla": 0, "fox": 1, "cross": 3, "diff": 5, "na": 9}
HEADNORMS = ["fox", "diff"]

C_IDENT, C_IOTA, C_NEGHALF, C_ROPE = 0, 128, 132, 148
C_TRI, C_ONES, C_CUM, C_SUF, C_CAUSAL = 180, 308, 436, 564, 692
C_NAMASK, C_SLOT, C_END = 948, 1012, 1140


def shape_constants():
    c = np.zeros((P, C_END), np.float32)
    s, t = np.arange(P)[:, None], np.arange(P)[None, :]
    c[:, C_IDENT:C_IDENT + P] = s == t
    c[:, C_IOTA:C_IOTA + 4] = np.arange(4)
    c[:, C_NEGHALF:C_NEGHALF + 16] = -0.5
    inv = np.float32(500000.0) ** (-np.arange(0, 16, 2, dtype=np.float32) / np.float32(16))
    ang = np.arange(S, dtype=np.float32)[:, None] * inv[None, :]
    rope = np.stack([np.cos(ang), np.sin(ang)], 1).astype(np.float32)
    c[:, C_ROPE:C_ROPE + 32] = rope.reshape(NT, P, 16).transpose(1, 0, 2).reshape(P, 32)
    c[:, C_TRI:C_TRI + P] = s <= t
    c[:, C_ONES:C_ONES + P] = 1.0
    same = s // GLA_C == t // GLA_C
    c[:, C_CUM:C_CUM + P] = (same & (s <= t)) / 16.0
    c[:, C_SUF:C_SUF + P] = (same & (s > t)) / 16.0
    c[:, C_CAUSAL + P:C_CAUSAL + 2 * P] = np.where(t > s, NEG, 0.0)
    q, k = np.arange(64)[:, None], np.arange(64)[None, :]
    left = np.clip(q - 8, 0, 48)
    c[:, C_NAMASK:C_NAMASK + 64] = np.tile(np.where((k >= left) & (k < left + 16), 0.0, NEG), (2, 1))
    c[:, C_SLOT:C_SLOT + P] = 1 + np.arange(P)
    m = np.zeros((P, LEVELS + 1, P), np.uint8)
    for l in range(LEVELS):
        h = 1 << l
        m[:, l] = (s // (2 * h) == t // (2 * h)) & (s % (2 * h) < h) & (t % (2 * h) >= h)
    m[:, LEVELS] = s == t
    return c, m.reshape(P, (LEVELS + 1) * P).view(np.int32)


def two_blocks(nc, a, out):
    with ExitStack() as ctx:
        def sb(name, shape, dt=F32):
            return ctx.enter_context(nc.sbuf_tensor("sb_" + name, shape, dt))

        def sem(name):
            return ctx.enter_context(nc.semaphore(name))

        raw = sb("raw", [P, RAW, CHUNK])
        w_hi = sb("w_hi", [P, SPLIT, CHUNK], F32R)
        w_lo = sb("w_lo", [P, SPLIT, CHUNK], F32R)
        x = sb("x", [P, NT, D])
        x_hi = sb("x_hi", [P, NT, KD, P], F32R)
        x_lo = sb("x_lo", [P, NT, KD, P], F32R)
        y = sb("y", [P, NT, D])
        h_hi = sb("h_hi", [P, 2, 2, S], F32R)
        h_lo = sb("h_lo", [P, 2, 2, S], F32R)
        fb = sb("fb", [P, 2048])
        gain = sb("gain", [P, 2, D])
        with nc.sbuf_tensor("sb_arena", [P, 12800], F32) as arena:
            pass
        arena_r = sb("arena_r", [P, 12800], F32R)
        const = sb("const", [P, C_TRI])
        sums = sb("sums", [P, len(NORMS), NT])
        rstd = sb("rstd", [P, len(NORMS), NT])
        rstd_q = sb("rstd_q", [P, 4, NT])
        vtmp, htmp = sb("vtmp", [P, 2]), sb("htmp", [P, 16])
        hsum = sb("hsum", [P, 16])
        hrstd = sb("hrstd", [P, 16])
        pool_heads = sb("pool_heads", [P, 16])
        negmax = sb("negmax", [P, 3, 2])
        rows = sb("rows", [P, 44, 2])
        rrow = sb("rrow", [P, 8])
        rheads = sb("rheads", [P, 8])
        gates = sb("gates", [P, NT, 17])
        psum = ctx.enter_context(nc.psum_tensor("psum", [P, 8, 512], F32))

        ident = const[:, C_IDENT:C_IDENT + P]
        iota4 = const[:, C_IOTA:C_IOTA + 4]
        neghalf = const[:, C_NEGHALF:C_NEGHALF + 16]
        rope = const[:, C_ROPE:C_ROPE + 32].rearrange("p (t c j) -> p t c j", t=NT, c=2)
        silu = fb[:, 0:1024].rearrange("p (r t f) -> p r t f", r=2, t=NT)
        hid = fb[:, 1024:2048].rearrange("p (r t f) -> p r t f", r=2, t=NT)
        junk = fb[:, 0:D]

        def region(at, n):
            return arena[:, at:at + n]

        def region_r(at, n):
            return arena_r[:, at:at + n]

        fq = region(0, 1024).rearrange("p (t c) -> p t c", t=NT)
        fk = region(1024, 1024).rearrange("p (t c) -> p t c", t=NT)
        fv = region(2048, 1024).rearrange("p (t c) -> p t c", t=NT)
        gg = region(3072, 1024).rearrange("p (t c) -> p t c", t=NT)
        gqk = region(4096, 1024).rearrange("p (t c) -> p t c", t=NT)
        gv = region(5120, 1024).rearrange("p (t c) -> p t c", t=NT)
        gb = region(6144, 512)
        lg = region(6656, 528).rearrange("p (t c) -> p t c", t=NT)
        ge = region(7184, 512)
        gz = region(7696, 1024).rearrange("p (r c) -> p r c", r=2)
        gs = region(8720, 512)
        st = region(9232, 768).rearrange("p (c f v) -> p c f v", c=3, f=2)
        fox_gain = region(10000, 512)
        gla_gain = region(10512, 512)
        bias_g = region(11024, 264)
        w_small = region(11288, 192).rearrange("p (k c) -> p k c", k=KD)
        w_small_parts = [region_r(9232 + 192 * i, 192).rearrange("p (k c) -> p k c", k=KD) for i in range(2)]
        smallT = region(9616, S)[0:24, :]
        w_alpha = region(11480, 256)
        mixc = region(11736, C_CAUSAL + 2 * P - C_TRI)
        tri, ones = mixc[:, 0:P], mixc[:, P:2 * P]
        cum, suf, causal = mixc[:, 2 * P:3 * P], mixc[:, 3 * P:4 * P], mixc[:, 4 * P:6 * P]
        mask_words = sb("masks", [P, (LEVELS + 1) * P // 4], I32)
        masks = mask_words[:, :].bitcast(U8)
        zeros = sb("zeros", [P, 512], mybir.dt.bfloat16)
        gaT = region(12504, 256)
        gqT, gkT = fb[:, 0:512], fb[:, 512:1024]
        at_ = fb[:, 1024:2048].rearrange("p (t h q) -> p t h q", t=NT, h=4)
        lsg = region(7696, 528).rearrange("p (t c) -> p t c", t=NT)
        gks = gqk[:, :, 256:512]
        gexp = region(6656, 512)
        fqT = region(4096, 1024).rearrange("p (f s) -> p f s", f=4)
        fkT = region(6144, 1024).rearrange("p (f s) -> p f s", f=4)
        probs_1 = region(7168, 1536).rearrange("p (r m k) -> p r m k", r=3, m=2)
        probsT_1 = region(8704, 1024).rearrange("p (r c) -> p r c", r=2)
        ct = region(12504, 256)
        mem = region(0, 2048).rearrange("p (t c) -> p t c", t=NT)
        xk = region(2048, 1024).rearrange("p (t c) -> p t c", t=NT)
        xv = region(5120, 1024).rearrange("p (t c) -> p t c", t=NT)
        xkT = region(4096, 1024).rearrange("p (f s) -> p f s", f=4)
        xq = region(3072, 1024).rearrange("p (t c) -> p t c", t=NT)
        xqT = region(6144, 1024).rearrange("p (f s) -> p f s", f=4)
        w_router = region(10000, 160).rearrange("p (k c) -> p k c", k=KD)
        w_router_parts = [region_r(10832 + 160 * i, 160).rearrange("p (k c) -> p k c", k=KD) for i in range(2)]
        routerT = region(11152, S)[0:20, :]
        b_router = region(10160, 20)
        rt = region(10192, 512).rearrange("p (t c) -> p t c", t=NT)
        slots = region(10704, P)
        y_hi, y_lo = (region_r(4736 + 2048 * i, 2048).rearrange("p (t c) -> p t c", t=NT) for i in range(2))
        pick = region_r(0, 1024).rearrange("p (w t s) -> p w t s", w=WINDOWS, t=NT)
        pickT = region_r(1024, 1024).rearrange("p (w t s) -> p w t s", w=WINDOWS, t=NT)
        window_x = [[z[:, w % 2, :, :] for z in (x_hi, x_lo)] for w in range(3)]
        window_x.append([z[:, 0, :].rearrange("p (k s) -> p k s", k=KD) for z in (y_hi, y_lo)])
        slot_y = [region_r(2048, 1024), region_r(8832, 1024)]
        slotv = region(3072, 17 * WINDOWS).rearrange("p (w c) -> p w c", w=WINDOWS)
        over_slotv = region(3140, 17)
        over_pick = region(3200, 256).rearrange("p (t s) -> p t s", t=NT)
        over_pickT = region(3456, 256).rearrange("p (t s) -> p t s", t=NT)
        over_x = region(3712, 1024).rearrange("p (k s) -> p k s", k=KD)
        over_w = region(4736, 4096)
        over_y = region(2048, 1024)
        over_silu, over_hidT, over_hid = fb[:, 0:512], fb[:, 512:1024], fb[:, 1024:1536]
        is_over = rt[0:1, 0, 139:140].bitcast(I32)
        over_group = rt[0:1, 0, 128:129].bitcast(I32)
        q2 = region(0, 2048).rearrange("p (t c) -> p t c", t=NT)
        probs_2 = region(0, 1536).rearrange("p (r m k) -> p r m k", r=3, m=2)
        probsT_2 = region(1536, 1024).rearrange("p (r c) -> p r c", r=2)
        q2T = region(2560, 2048).rearrange("p (f s) -> p f s", f=8)
        k2T = region(4608, 2048).rearrange("p (f s) -> p f s", f=8)
        v2 = fb[:, :].rearrange("p (t c) -> p t c", t=NT)
        subln = region(6656, 128)
        lamv = region(6784, 256)
        lams = region(7040, 32)
        ropet = region(7168, 2048)
        nab = region(6656, 6144).rearrange("p (h r c) -> p h r c", h=16, r=6)
        namask = mask_words[:, 0:64].bitcast(F32)

        raw_landed = [sem(f"raw_landed{i}") for i in range(RAW)]
        hi_done, lo_v_done, lo_p_done = sem("hi_done"), sem("lo_v_done"), sem("lo_p_done")
        weights_used = sem("weights_used")
        x_landed, const_landed, mixw_landed, mem_landed = (
            [sem("x_landed0"), sem("x_landed1")], sem("const_landed"), sem("mixw_landed"), sem("mem_landed"))
        router_landed, diffw_landed = sem("router_landed"), sem("diffw_landed")
        nab_landed, namask_landed = sem("nab_landed"), sem("namask_landed")
        gain_landed = [sem("gain_landed0"), sem("gain_landed1")]
        gain_used = sem("gain_used")
        turn_src, turned, turn_hi, turn_lo = sem("turn_src"), sem("turned"), sem("turn_hi"), sem("turn_lo")
        squared, rstd_ready, rstdq_ready = sem("squared"), sem("rstd_ready"), sem("rstdq_ready")
        proj_t0, proj_out0, proj_out1 = sem("proj_t0"), sem("proj_out0"), sem("proj_out1")
        gu_t0, silu_done, hid_done = sem("gu_t0"), sem("silu_done"), sem("hid_done")
        hid_turned, hid_hi, hid_lo = sem("hid_turned"), sem("hid_hi"), sem("hid_lo")
        sum_t0, resid_done = sem("sum_t0"), sem("resid_done")
        qk_turned, q_out, k_out = sem("qk_turned"), sem("q_out"), sem("k_out")
        scores, max_done, probs_done = sem("scores"), sem("max_done"), sem("probs_done")
        probs_turned, probsT_done = sem("probs_turned"), sem("probsT_done")
        pv_done, pv_taken = sem("pv_done"), sem("pv_taken")
        head_sums, head_rstd, heads_normed = sem("head_sums"), sem("head_rstd"), sem("heads_normed")
        logits_done, logits_out = sem("logits_done"), sem("logits_out")
        ga_turned, ga_out, alpha_done = sem("ga_turned"), sem("ga_out"), sem("alpha_done")
        logits_in, logsig_abs, logsig_ln, logsig_done = sem("logits_in"), sem("logsig_abs"), sem("logsig_ln"), sem("logsig_done")
        decay_done, gb_out, suffix_out, ct_out = (
            sem("decay_done"), sem("gb_out"), sem("suffix_out"), sem("ct_out"))
        ks_ready, u_done, state_ready, qb_ready, expb_ready = (
            sem("ks_ready"), sem("u_done"), sem("state_ready"), sem("qb_ready"), sem("expb_ready"))
        diff_ready, decay_exp, z_ready, level_done, level_out = (
            sem("level_diff"), sem("level_exp"), sem("z_ready"), sem("level_done"), sem("level_out"))
        at_zero, gla_o_done, gla_o_out = sem("at_zero"), sem("gla_o_done"), sem("gla_o_out")
        route_exp, route_in, gates_ready = sem("route_exp"), sem("route_in"), sem("gates_ready")
        small_split, small_out, gained_hi, gained_lo = sem("small_split"), sem("small_out"), sem("gained_hi"), sem("gained_lo")
        slot_y_lo = sem("slot_y_lo")
        hot_ready, ranked, pick_ready, pick_turned, pickT_out = (
            sem("hot_ready"), sem("ranked"), sem("pick_ready"), sem("pick_turned"), sem("pickT_out"))
        slotv_done, slotv_out = sem("slotv_done"), sem("slotv_out")
        gathered, gathered_hi, gathered_lo = sem("gathered"), sem("gathered_hi"), sem("gathered_lo")
        slot_y_out, scattered, scatter_taken = sem("slot_y_out"), sem("scattered"), sem("scatter_taken")
        over_known, over_in, over_taken, over_landed = (
            sem("over_known"), sem("over_in"), sem("over_taken"), sem("over_landed"))
        over_gate, over_up, over_silued, over_hidden = (
            sem("over_gate"), sem("over_up"), sem("over_silued"), sem("over_hidden"))
        over_turned, over_hidT_out, over_down = sem("over_turned"), sem("over_hidT_out"), sem("over_down")
        over_y_out, over_scattered, over_added = sem("over_y_out"), sem("over_scattered"), sem("over_added")
        rope_done, lam_sum, lam_exp = sem("rope_done"), sem("lam_sum"), sem("lam_exp")
        nab_ready, zeros_ready = sem("nab_ready"), sem("zeros_ready")
        out_landed = sem("out_landed")
        dve_chain, act_chain, pool_chain = sem("dve_chain"), sem("act_chain"), sem("pool_chain")

        def columns(w, k0, c0):
            src = w.rearrange("(k p) c -> p k c", p=P)
            return [(slice(1024 * i, 1024 * i + 1024), src[:, k0 + 2 * i:k0 + 2 * i + 2, c0:c0 + 512], 2)
                    for i in range(2)]

        def full_rows(w, k0):
            src = w.rearrange("(k p) c -> p k c", p=P)
            return [(slice(1024 * i, 1024 * i + 1024), src[:, k0 + i:k0 + i + 1, :], 1) for i in range(2)]

        w_in = a["w_in"][0]
        OFF = {"fq": 0, "fk": 512, "fv": 1024, "gqk": 1544, "gv": 2056, "gg": 2568}
        PROJ_SRC = {n: (w_in, OFF[n]) for n in OFF}
        PROJ_SRC |= {"xk": (a["w_xk"][0], 0), "xv": (a["w_xv"][0], 0), "xq": (a["w_xq"][0], 0)}
        for i, n in enumerate(PROJ[9:15]):
            PROJ_SRC[n] = (a["diff_w_in_2"][0], 512 * i)
        for i, n in enumerate(PROJ[15:21]):
            PROJ_SRC[n] = (a["na_w_in_2"][0], 512 * i)
        SUM_SRC = {"mix_out": (a["w_out"][0], 4), "cross_out": (a["w_xo"][0], 2),
                   "diff_out": (a["diff_w_out_2"][0], 4), "na_out": (a["na_w_out_2"][0], 4)}
        FFN = {"moe": MOE_GROUPS, "ffn1_0": FF_GROUPS, "ffn2_0": FF_GROUPS, "ffn1_1": FF_GROUPS,
               "ffn2_1": FF_GROUPS}
        GU0 = {}
        for name in FFN:
            GU0[name] = sum(FFN[m] for m in list(FFN)[:list(FFN).index(name)])

        def swiglu_weights(name):
            if name == "moe":
                return a["w_expert_gate"][0], a["w_expert_up"][0], a["w_expert_down"][0]
            layer, which = int(name[-1]), name[:4]
            return a[which + "_wg_2"][layer], a[which + "_wu_2"][layer], a[which + "_wd_2"][layer]

        def gate_up(name, g, k0, it):
            parts = []
            for i, w in enumerate(swiglu_weights(name)[:2]):
                if name == "moe":
                    src = w[bass.ds(it + g // 2, 1)] if it is not None else w[g // 2:g // 2 + 1]
                    src = src.rearrange("e (k p) c -> p (e k) c", p=P)[:, k0:k0 + 4, GROUP * (g % 2):GROUP * (g % 2) + GROUP]
                else:
                    src = w.rearrange("(k p) c -> p k c", p=P)[:, k0:k0 + 4, :]
                    c = bass.ds(it * (2 * GROUP) + g * GROUP, GROUP) if it is not None else slice(g * GROUP, g * GROUP + GROUP)
                    src = src[:, :, c]
                parts.append((i, src, 4))
            return parts

        def down(name, g, it):
            w = swiglu_weights(name)[2]
            parts = []
            for i in (1, 0):
                if name == "moe":
                    src = w[bass.ds(it + g // 2, 1)] if it is not None else w[g // 2:g // 2 + 1]
                    src = src.rearrange("e (k p) c -> p (e k) c", p=P)[:, 2 * (g % 2) + i:2 * (g % 2) + i + 1, :]
                else:
                    r = bass.ds(it * (2 * GROUP) + g * GROUP + P * i, P) if it is not None else slice(g * GROUP + P * i, g * GROUP + P * i + P)
                    src = w[r, :].unsqueeze(1)
                parts.append((slice(1024 * i, 1024 * i + 1024), src, 1))
            return parts

        def shifted(value, it, per):
            return value if it is None else it * per + value

        def view(slot_ap, part, k):
            if isinstance(part, slice):
                return slot_ap[:, part].rearrange("p (k c) -> p k c", k=k)
            return slot_ap.rearrange("p (k u c) -> p k u c", k=k, u=2)[:, :, part, :]

        def gather_bank(w, q):
            return q if w == 0 else 2 + q % 2

        def gathered_views(w, q):
            bank = psum[:, gather_bank(w, q), :].rearrange("p (k w s) -> p k w s", k=2, w=2)
            return [(bank[:, :, i, :], *(z[:, 2 * q:2 * q + 2, :] for z in window_x[w + i])) for i in range(2)]

        def row(vector, n):
            return vector.unsqueeze(0).to_broadcast([P, n])

        block = ctx.enter_context(nc.Block())

        @block.sync
        def _(sp):
            def load(n, parts, it=None):
                if n >= RAW:
                    sp.wait_ge(hi_done, shifted(n - RAW + 1, it, 6))
                    sp.wait_ge(lo_v_done, shifted(n - RAW + 1, it, 6))
                    sp.wait_ge(lo_p_done, shifted(n - RAW + 1, it, 6))
                for part, src, k in parts:
                    sp.dma_start(view(raw[:, n % RAW, :], part, k), src).then_inc(raw_landed[n % RAW], 16)

            def projection(name):
                w, c0 = PROJ_SRC[name]
                for half in range(2):
                    load(PROJ_CHUNK[name] + half, columns(w, 4 * half, c0))

            def out_projection(name):
                w, count = SUM_SRC[name]
                for i in range(count):
                    load(START[name] + i, full_rows(w, 2 * i))

            def swiglu(name):
                n, groups = START[name], FFN[name]

                def step(n, g, it=None):
                    load(n, gate_up(name, g + 1, 0, it), it)
                    load(n + 1, gate_up(name, g + 1, 4, it), it)
                    load(n + 2, down(name, g, it), it)

                load(n, gate_up(name, 0, 0, None))
                load(n + 1, gate_up(name, 0, 4, None))
                with sp.Fori(0, (groups - 1) // 2) as it:
                    step(n + 2, 0, it)
                    step(n + 5, 1, it)
                if groups % 2 == 0:
                    step(n + 3 * groups - 4, groups - 2)
                load(n + 3 * groups - 1, down(name, groups - 1, None))

            sp.dma_start(x[:, 0, :], a["x"][0, 0:P, :]).then_inc(x_landed[0], 16)
            load(0, columns(w_in, 0, OFF["gg"]))
            sp.dma_start(x[:, 1, :], a["x"][0, P:S, :]).then_inc(x_landed[1], 16)
            load(1, columns(w_in, 4, OFF["gg"]))
            projection("gqk")
            sp.dma_start(w_small[:, :, 0:8], w_in[:, 1536:1544].rearrange("(k p) c -> p k c", p=P)).then_inc(mixw_landed, 16)
            sp.dma_start(w_small[:, :, 8:24], w_in[:, 3080:3096].rearrange("(k p) c -> p k c", p=P)).then_inc(mixw_landed, 16)
            sp.dma_start(bias_g[:, 0:8], row(a["b_forget"][0], 8)).then_inc(mixw_landed, 16)
            sp.dma_start(bias_g[:, 8:264], row(a["b_alpha"][0], 256)).then_inc(mixw_landed, 16)
            sp.dma_start(w_alpha[0:16, :], a["w_alpha_up"][0]).then_inc(mixw_landed, 16)
            sp.dma_start(mixc, a["consts"][:, C_TRI:C_CAUSAL + 2 * P]).then_inc(mixw_landed, 16)
            sp.dma_start(mask_words[:, :], a["masks"]).then_inc(mixw_landed, 16)
            sp.dma_start(fox_gain, row(a["fox_out_gain"][0], 512)).then_inc(mixw_landed, 16)
            sp.dma_start(gla_gain, row(a["gla_out_gain"][0], 512)).then_inc(mixw_landed, 16)
            for name in PROJ[2:6]:
                projection(name)
            projection("xk")
            projection("xv")
            out_projection("mix_out")
            projection("xq")
            out_projection("cross_out")
            swiglu("moe")
            swiglu("ffn1_0")
            for name in PROJ[9:15]:
                projection(name)
            out_projection("diff_out")
            swiglu("ffn2_0")
            swiglu("ffn1_1")
            for name in PROJ[15:21]:
                projection(name)
            out_projection("na_out")
            swiglu("ffn2_1")
            for t in range(NT):
                sp.wait_ge(resid_done, 9 * NT + t + 1)
                sp.dma_start(out[0, t * P:t * P + P, :], x[:, t, :]).then_inc(out_landed, 16)
            sp.wait_ge(out_landed, 16 * NT)

        @block.tensor
        def _(pe):
            def products(bank, xh, xl, wh, wl, first, last):
                pe.matmul(bank, xh, wh, start=first, stop=False)
                pe.matmul(bank, xh, wl, start=False, stop=False)
                return pe.matmul(bank, xl, wh, start=False, stop=last)

            def weights(n, it=None):
                pe.wait_ge(lo_v_done, shifted(n + 1, it, 6))
                pe.wait_ge(lo_p_done, shifted(n + 1, it, 6))

            def turn(name, t, src=y):
                per_tile = TURN_BANKS[name] // NT
                for kk in range(per_tile):
                    i = t * per_tile + kk
                    pe.wait_ge(turn_src, TURN_BASE[name] + i + 1)
                    for k in range(4):
                        f = 4 * kk + k
                        last = pe.transpose(psum[:, turn_bank(name, i), k * P:k * P + P], src[:, t, f * P:f * P + P], ident)
                    last.then_inc(turned, 1)

            def keep_warm(bank, count):
                for _ in range(count):
                    pe.matmul(psum[:, bank, :], zeros[:, 0:P], zeros[:, :], start=True, stop=True)

            def input_of(name, src=y):
                per_tile = TURN_BANKS[name] // NT

                def ready(t, kk):
                    if kk == 0:
                        if t == 0:
                            keep_warm(turn_bank(name, 0), 7)
                        turn(name, t, src)
                        if t == 0:
                            keep_warm(turn_bank(name, 3), 6)
                    pe.wait_ge(turn_lo, TURN_BASE[name] + t * per_tile + kk + 1)
                return ready

            def projection(name, between=None, ready=None):
                j, n = PROJ_AT[name], PROJ_CHUNK[name]
                if j >= 2:
                    pe.wait_ge(proj_out0, j - 1)
                    pe.wait_ge(proj_out1, j - 1)
                for half in range(2):
                    for t in range(NT):
                        if ready is not None:
                            ready(t, half)
                        if t == 0:
                            weights(n + half)
                        bank = psum[:, 2 * (j % 2) + t, :]
                        for k in range(4):
                            c = slice(512 * k, 512 * k + 512)
                            last = products(bank, x_hi[:, t, 4 * half + k, :], x_lo[:, t, 4 * half + k, :],
                                            w_hi[:, (n + half) % SPLIT, c], w_lo[:, (n + half) % SPLIT, c],
                                            half == 0 and k == 0, half == 1 and k == 3)
                        if t == 0 and half == 1:
                            last.then_inc(proj_t0, 1)
                    last.then_inc(weights_used, 1)
                    if half == 0 and between is not None:
                        between()

            def out_projection(name, ready):
                count = SUM_SRC[name][1]
                for i in range(count):
                    n = START[name] + i
                    for t in range(NT):
                        if i % 2 == 0:
                            ready(t, i // 2)
                        if t == 0:
                            weights(n)
                        for k in range(2):
                            for half in range(2):
                                c = slice(1024 * k + 512 * half, 1024 * k + 512 * half + 512)
                                last = products(psum[:, 4 + 2 * t + half, :], x_hi[:, t, 2 * i + k, :],
                                                x_lo[:, t, 2 * i + k, :], w_hi[:, n % SPLIT, c],
                                                w_lo[:, n % SPLIT, c], i == 0 and k == 0,
                                                i == count - 1 and k == 1)
                        if t == 0 and i == count - 1:
                            last.then_inc(sum_t0, 1)
                    last.then_inc(weights_used, 1)

            def swiglu(name):
                base, groups, gu0 = START[name], FFN[name], GU0[name]

                def gate_up_half(n, g, half, it=None, ready=None):
                    par = (gu0 + g) % 2
                    for t in range(NT):
                        if ready is not None:
                            ready(t, half)
                        if t == 0:
                            weights(n, it)
                        for k in range(4):
                            c = slice(512 * k, 512 * k + 512)
                            last = products(psum[:, 2 * par + t, :], x_hi[:, t, 4 * half + k, :],
                                            x_lo[:, t, 4 * half + k, :], w_hi[:, n % SPLIT, c],
                                            w_lo[:, n % SPLIT, c], half == 0 and k == 0,
                                            half == 1 and k == 3)
                        if t == 0 and half == 1:
                            last.then_inc(gu_t0, 1)
                    last.then_inc(weights_used, 1)

                def turn_hidden(g, it=None):
                    par = (gu0 + g) % 2
                    pe.wait_ge(hid_done, shifted(NT * (gu0 + g + 1), it, 2 * NT))
                    for f in range(2):
                        for t in range(NT):
                            last = pe.transpose(psum[:, 2 * par, f * S + t * P:f * S + t * P + P],
                                                hid[:, par, t, f * P:f * P + P], ident)
                    last.then_inc(hid_turned, 1)

                def down_sum(n, g, it=None, first=False, final=False):
                    par = (gu0 + g) % 2
                    weights(n, it)
                    pe.wait_ge(hid_lo, shifted(gu0 + g + 1, it, 2))
                    for t in range(NT):
                        for f in range(2):
                            for half in range(2):
                                c = slice(1024 * f + 512 * half, 1024 * f + 512 * half + 512)
                                bank = psum[:, 4 + 2 * t + half, :]
                                hh, hl = (h[:, par, f, t * P:t * P + P] for h in (h_hi, h_lo))
                                st0 = first and f == 0
                                sp0 = final and f == 1
                                pe.matmul(bank, hh, w_hi[:, n % SPLIT, c], start=st0, stop=False, skip_group_check=True)
                                pe.matmul(bank, hh, w_lo[:, n % SPLIT, c], start=False, stop=False, skip_group_check=True)
                                last = pe.matmul(bank, hl, w_hi[:, n % SPLIT, c], start=False, stop=sp0, skip_group_check=True)
                        if t == 0 and final:
                            last.then_inc(sum_t0, 1)
                    last.then_inc(weights_used, 1)

                def step(n, g, it=None, first=False):
                    gate_up_half(n, g + 1, 0, it)
                    turn_hidden(g, it)
                    gate_up_half(n + 1, g + 1, 1, it)
                    down_sum(n + 2, g, it, first)

                ready = input_of(name)
                gate_up_half(base, 0, 0, None, ready)
                gate_up_half(base + 1, 0, 1, None, ready)
                for b in range(4, 8):
                    pe.matmul(psum[:, b, :], zeros[:, 0:P], zeros[:, :], start=True, stop=False, skip_group_check=True)
                with pe.Fori(0, (groups - 1) // 2) as it:
                    step(base + 2, 0, it)
                    step(base + 5, 1, it)
                if groups % 2 == 0:
                    step(base + 3 * groups - 4, groups - 2)
                turn_hidden(groups - 1)
                down_sum(base + 3 * groups - 1, groups - 1, final=True)

            def experts():
                base = START["moe"]

                def gather(w, quarters):
                    for q in quarters:
                        if w == 0:
                            pe.wait_ge(pick_ready, NT * 2)
                            pe.wait_ge(gained_lo, 1)
                        elif q < 2:
                            pe.wait_ge(scatter_taken, 1)
                        else:
                            pe.wait_ge(gathered_lo, 4 + q - 1)
                        bank = psum[:, gather_bank(w, q), :].rearrange("p (k w s) -> p k w s", k=2, w=2)
                        for k in range(2):
                            f = slice((2 * q + k) * P, (2 * q + k) * P + P)
                            for t in range(NT):
                                for part in (y_hi, y_lo):
                                    last = pe.matmul(bank[:, k, :, :], part[:, t, f], pick[:, w:w + 2, t, :],
                                                     start=t == 0 and part is y_hi, stop=t == NT - 1 and part is y_lo)
                        last.then_inc(gathered, 1)

                def scatter(w):
                    pe.wait_ge(slot_y_lo, w + 1)
                    for t in range(NT):
                        for half in range(2):
                            bank = 2 + half if t == 0 else 4 + 2 * (w % 2) + half
                            for part in slot_y:
                                last = pe.matmul(psum[:, bank, :], pickT[:, w, t, :], part[:, 512 * half:512 * half + 512],
                                                 start=part is slot_y[0], stop=part is slot_y[1])
                        last.then_inc(scattered, 1)

                def gate_up_half(n, w, g, half, it=None):
                    weights(n, it)
                    if half == 0 and g % 16 == 0:
                        pe.wait_ge(gathered_lo, 4 * (w // 2) + 4)
                    for k in range(4):
                        c = slice(512 * k, 512 * k + 512)
                        xh, xl = window_x[w]
                        last = products(psum[:, g % 2, :], xh[:, 4 * half + k, :], xl[:, 4 * half + k, :], w_hi[:, n % SPLIT, c],
                                        w_lo[:, n % SPLIT, c], half == 0 and k == 0, half == 1 and k == 3)
                    last.then_inc(weights_used, 1)

                def turn_hidden(g, it=None):
                    pe.wait_ge(hid_done, shifted(NT * (g + 1), it, 2 * NT))
                    for f in range(2):
                        last = pe.transpose(psum[:, g % 2, f * P:f * P + P], hid[:, g % 2, 0, f * P:f * P + P], ident)
                    last.then_inc(hid_turned, 1)

                def down_sum(n, w, g, it=None):
                    weights(n, it)
                    pe.wait_ge(hid_lo, shifted(g + 1, it, 2))
                    for f in range(2):
                        for half in range(2):
                            c = slice(1024 * f + 512 * half, 1024 * f + 512 * half + 512)
                            bank = psum[:, 4 + 2 * (w % 2) + half, :]
                            hh, hl = (h[:, g % 2, f, 0:P] for h in (h_hi, h_lo))
                            pe.matmul(bank, hh, w_hi[:, n % SPLIT, c], start=False, stop=False, skip_group_check=True)
                            pe.matmul(bank, hh, w_lo[:, n % SPLIT, c], start=False, stop=False, skip_group_check=True)
                            last = pe.matmul(bank, hl, w_hi[:, n % SPLIT, c], start=False, stop=False, skip_group_check=True)
                    last.then_inc(weights_used, 1)

                def step(w, g, it=None, gathers=False):
                    n, w_next = base + 2 + 3 * g, (g + 1) // 8
                    gate_up_half(n, w_next, g + 1, 0, it)
                    if gathers:
                        gather(2, (0, 1))
                    turn_hidden(g, it)
                    gate_up_half(n + 1, w_next, g + 1, 1, it)
                    if gathers:
                        gather(2, (2, 3))
                    down_sum(n + 2, w, g, it)

                pe.wait_ge(hot_ready, 1)
                hot0, hot1 = rt[:, 0, 56:60], rt[:, 1, 56:60]
                pe.matmul(psum[:, 5, 0:4], tri, hot0, start=True, stop=True)
                pe.matmul(psum[:, 5, 8:12], ones, hot0, start=True, stop=False)
                pe.matmul(psum[:, 5, 8:12], tri, hot1, start=False, stop=True)
                pe.matmul(psum[:, 5, 16:20], ones, hot0, start=True, stop=False)
                pe.matmul(psum[:, 5, 16:20], ones, hot1, start=False, stop=True).then_inc(ranked, 1)
                gather(0, range(4))
                pe.wait_ge(pick_ready, NT * WINDOWS)
                for w in range(WINDOWS):
                    for t in range(NT):
                        last = pe.transpose(psum[:, 6 + w // 2, (w % 2) * 256 + t * P:(w % 2) * 256 + t * P + P],
                                            pick[:, w, t, :].bitcast(F32), ident)
                last.then_inc(pick_turned, 1)
                gate_up_half(base, 0, 0, 0)
                gate_up_half(base + 1, 0, 0, 1)
                pe.wait_ge(gates_ready, 1)
                for w in range(WINDOWS):
                    for t in range(NT):
                        last = pe.matmul(psum[:, 5, 32 + 32 * w:32 + 32 * w + 17], pick[:, w, t, :].bitcast(F32), gates[:, t, :],
                                         start=t == 0, stop=t == NT - 1)
                last.then_inc(slotv_done, 1)
                pe.wait_ge(slotv_out, 1)
                pe.wait_ge(pickT_out, 1)
                for w in range(WINDOWS):
                    if w >= 2:
                        pe.wait_ge(scatter_taken, NT * (w - 1))
                    for b in range(2):
                        pe.matmul(psum[:, 4 + 2 * (w % 2) + b, :], zeros[:, 0:P], zeros[:, :], start=True, stop=False,
                                  skip_group_check=True)
                    with pe.Fori(0, 3) as it:
                        step(w, 8 * w, it)
                        step(w, 8 * w + 1, it)
                    if w:
                        scatter(w - 1)
                    step(w, 8 * w + 6, None, w == 1)
                    if w < WINDOWS - 1:
                        step(w, 8 * w + 7)
                turn_hidden(8 * WINDOWS - 1)
                down_sum(base + 24 * WINDOWS - 1, WINDOWS - 1, 8 * WINDOWS - 1)
                scatter(WINDOWS - 1)
                pe.wait_ge(over_known, 1)
                with pe.If(pe.value_load(is_over, min_val=0, max_val=1) > 0):
                    pe.wait_ge(scatter_taken, NT * WINDOWS)
                    for k in range(KD):
                        for t in range(NT):
                            pe.matmul(psum[:, k // 4, (k % 4) * P:(k % 4) * P + P], y[:, t, k * P:k * P + P],
                                      over_pick[:, t, :], start=t == 0, stop=t == NT - 1)
                    for t in range(NT):
                        pe.transpose(psum[:, 2, t * P:t * P + P], over_pick[:, t, :], ident)
                    for t in range(NT):
                        last = pe.matmul(psum[:, 3, 0:17], over_pick[:, t, :], gates[:, t, :], start=t == 0, stop=t == NT - 1)
                    last.then_inc(over_in, 1)
                    pe.wait_ge(over_taken, 1)
                    for b in (4, 5):
                        last = pe.matmul(psum[:, b, :], zeros[:, 0:P], zeros[:, :], start=True, stop=False, skip_group_check=True)
                    last.then_inc(over_down, 1)
                    with pe.Fori(0, 4) as it:
                        for which, done in enumerate((over_gate, over_up)):
                            pe.wait_ge(over_landed, it * 48 + (16 + 16 * which))
                            for k in range(KD):
                                last = pe.matmul(psum[:, which, :], over_x[:, k, :], over_w[:, 512 * k:512 * k + 512],
                                                 start=k == 0, stop=k == KD - 1)
                            last.then_inc(done, 1)
                        pe.wait_ge(over_hidden, it + 1)
                        for f in range(4):
                            last = pe.transpose(psum[:, 2, f * P:f * P + P], over_hid[:, f * P:f * P + P], ident)
                        last.then_inc(over_turned, 1)
                        pe.wait_ge(over_landed, it * 48 + 48)
                        pe.wait_ge(over_hidT_out, it + 1)
                        for f in range(4):
                            for half in range(2):
                                c = slice(1024 * f + 512 * half, 1024 * f + 512 * half + 512)
                                last = pe.matmul(psum[:, 4 + half, :], over_hidT[:, f * P:f * P + P], over_w[:, c],
                                                 start=False, stop=False, skip_group_check=True)
                        last.then_inc(over_down, 1)
                    pe.wait_ge(over_y_out, 1)
                    for t in range(NT):
                        for half in range(2):
                            last = pe.matmul(psum[:, 2 * t + half, :], over_pickT[:, t, :],
                                             over_y[:, 512 * half:512 * half + 512], start=True, stop=True)
                    last.then_inc(over_scattered, 1)
                    pe.wait_ge(over_added, NT)

            def qk_turn(name, q, k):
                for b in range(QKT_BANKS[name]):
                    for i, src in enumerate((q, k)):
                        c = 2 * (QKT0[name] + b) + i
                        if QKT0[name] + b >= 2:
                            pe.wait_ge(q_out if i == 0 else k_out, QKT0[name] + b - 1)
                        for f in range(2):
                            for t in range(NT):
                                last = pe.transpose(psum[:, 4 + c % 4, f * S + t * P:f * S + t * P + P],
                                                    src[:, t, (2 * b + f) * P:(2 * b + f) * P + P], ident)
                        last.then_inc(qk_turned, 1)

            def attention(name, qT, kT, v, probs, probsT, d, last_proj):
                pairs, gsize, u0 = PAIRS[name], GSIZE[name], UNIT0[name]
                units = [(i, p) for i in range(NT) for p in range(pairs)]
                dv = {"fox": 64, "cross": 128, "diff": 128, "na": 64}[name]

                def keys(i):
                    return (i + 1) * P if name == "fox" else S

                def rows_of(T, m, c):
                    if d == P:
                        return T[:, m, c]
                    return T[(m % 2) * 64:(m % 2) * 64 + 64, m // 2, c]

                def score(n):
                    i, p = units[n]
                    u = u0 + n
                    if n >= 4:
                        pe.wait_ge(probs_done, u - 3)
                    for j in range(2):
                        m = score_map(name, p, j)
                        bank = psum[:, u % 4, j * S:j * S + keys(i)]
                        last = pe.matmul(bank, rows_of(qT, m, slice(i * P, i * P + P)),
                                         rows_of(kT, m, slice(0, keys(i))), start=True, stop=name != "fox")
                        if name == "fox":
                            last = pe.matmul(bank, ident[0:8, m:m + 1].to_broadcast([8, P]), ct[0:8, 0:keys(i)],
                                             start=False, stop=True)
                    last.then_inc(scores, 1)

                def turn_probs(n):
                    i, p = units[n]
                    u = u0 + n
                    pe.wait_ge(probs_done, u + 1)
                    if n >= 2:
                        pe.wait_ge(probsT_done, u - 1)
                    for j in range(2):
                        for kt in range(keys(i) // P):
                            last = pe.transpose(psum[:, 4 + u % 2, (2 * j + kt) * P:(2 * j + kt) * P + P],
                                                probs[:, u % 3, j, kt * P:kt * P + P], ident)
                    last.then_inc(probs_turned, 1)

                def apply(n):
                    i, p = units[n]
                    u = u0 + n
                    grp = GROUP0[name] + n // gsize
                    pe.wait_ge(probsT_done, u + 1)
                    if n % gsize == 0 and n // gsize >= 2:
                        pe.wait_ge(pv_taken, grp - 1)
                    nk = keys(i) // P
                    for j in range(2):
                        m = score_map(name, p, j)
                        at = m % (2 * gsize) * dv
                        vc = (m // 2 if name == "diff" else m) * dv
                        for kt in range(nk):
                            last = pe.matmul(psum[:, 6 + grp % 2, at:at + dv],
                                             probsT[:, u % 2, (2 * j + kt) * P:(2 * j + kt) * P + P],
                                             v[:, kt, vc:vc + dv], start=kt == 0, stop=kt == nk - 1)
                    if n % gsize == gsize - 1:
                        last.then_inc(pv_done, 1)

                pe.wait_ge(q_out, QKT0[name] + QKT_BANKS[name])
                pe.wait_ge(k_out, QKT0[name] + QKT_BANKS[name])
                pe.wait_ge(proj_out0, PROJ_AT[last_proj] + 1)
                pe.wait_ge(proj_out1, PROJ_AT[last_proj] + 1)
                score(0)
                score(1)
                for n in range(len(units)):
                    if n + 2 < len(units):
                        score(n + 2)
                    turn_probs(n)
                    if n >= 1:
                        apply(n - 1)
                apply(len(units) - 1)

            def small(wh, wl):
                out_ = psum[0:wh.shape[2], 4, 0:S].rearrange("p (t c) -> p t c", t=NT)
                for k in range(KD):
                    pe.matmul(out_, wh[:, k, :], x_hi[:, :, k, :], start=k == 0, stop=False)
                    pe.matmul(out_, wh[:, k, :], x_lo[:, :, k, :], start=False, stop=False)
                    last = pe.matmul(out_, wl[:, k, :], x_hi[:, :, k, :], start=False, stop=k == KD - 1)
                last.then_inc(logits_done, 1)

            def small_turn(out_t, count):
                pe.wait_ge(small_out, count)
                n = out_t.shape[0]
                for t in range(NT):
                    last = pe.transpose(psum[:, 4, t * 64:t * 64 + n], out_t[:, t * P:t * P + P], ident[0:n, 0:n])
                last.then_inc(logits_done, 1)

            pe.wait_ge(zeros_ready, 1)
            pe.wait_ge(const_landed, 16)
            projection("gg", None, input_of("mix"))
            pe.wait_ge(mixw_landed, 16 * MIX_LOADS)
            pe.wait_ge(small_split, 1)
            small(*w_small_parts)
            projection("gqk", lambda: small_turn(smallT, 1))
            pe.wait_ge(logits_out, 1)
            for t in range(NT):
                last = pe.transpose(psum[0:16, 5, t * P:t * P + P], lg[:, t, 8:24], ident)
            last.then_inc(ga_turned, 1)
            pe.wait_ge(ga_out, 1)
            for t in range(NT):
                last = pe.matmul(psum[:, 6, t * S:t * S + S], gaT[0:16, t * P:t * P + P], w_alpha[0:16, :],
                                 start=True, stop=True)
            last.then_inc(alpha_done, 1)
            pe.wait_ge(proj_out0, 2)
            pe.wait_ge(proj_out1, 2)
            qk_turn("gla", gqk[:, :, 0:256], gqk[:, :, 256:512])
            projection("gv")
            pe.wait_ge(logsig_done, 1)
            pe.wait_ge(q_out, 1)
            for t in range(NT):
                for f in range(2):
                    last = pe.matmul(psum[:, 4, f * S + t * P:f * S + t * P + P],
                                     lg[:, t, 8 + f * P:8 + f * P + P], cum, start=True, stop=True)
            last.then_inc(decay_done, 1)
            pe.wait_ge(k_out, 1)
            for t in range(NT):
                last = pe.matmul(psum[:, 5, t * S:t * S + S], suf, lg[:, t, 8:264], start=True, stop=True)
            last.then_inc(decay_done, 1)
            pe.matmul(psum[0:8, 7, 0:P], lg[:, 0, 0:8], tri, start=True, stop=True)
            pe.matmul(psum[0:8, 7, P:S], lg[:, 0, 0:8], ones, start=True, stop=False)
            pe.matmul(psum[0:8, 7, P:S], lg[:, 1, 0:8], tri, start=False, stop=True).then_inc(decay_done, 1)
            projection("fq")
            pe.wait_ge(ks_ready, 1)
            pe.wait_ge(ct_out, 1)
            pe.wait_ge(proj_out0, 3)
            for c in range(3):
                r = slice((c % 2) * 64, (c % 2) * 64 + 64)
                for h in range(4):
                    at = (c // 2) * 256 + (h // 2) * P
                    last = pe.matmul(psum[(h % 2) * 64:(h % 2) * 64 + 64, 6 + c % 2, at:at + P],
                                     gks[r, c // 2, h * 64:h * 64 + 64], gv[r, c // 2, h * P:h * P + P],
                                     start=True, stop=True)
            last.then_inc(u_done, 1)

            def level(l):
                if l < LEVELS:
                    pe.wait_ge(z_ready, l + 1)
                if l == 0:
                    pe.wait_ge(gb_out, 1)
                    pe.wait_ge(suffix_out, 1)
                if l == 1:
                    pe.wait_ge(state_ready, 1)
                if l >= 2:
                    pe.wait_ge(level_out, l - 1)
                for t in range(NT):
                    for h in range(4):
                        r = slice((h % 2) * 64, (h % 2) * 64 + 64)
                        c = slice((h // 2) * S + t * P, (h // 2) * S + t * P + P)
                        lhs, rhs = (gz[r, l % 2, c], gz[r, l % 2, c]) if l < LEVELS else (gkT[r, c], gqT[r, c])
                        at = t * 256 + (h // 2) * P
                        last = pe.matmul(psum[:, 4 + 2 * (l % 2) + h % 2, at:at + P], lhs, rhs,
                                         start=True, stop=True)
                last.then_inc(level_done, 1)

            level(0)
            level(1)
            projection("fk")
            level(2)
            level(3)
            projection("fv")
            level(4)
            level(5)
            level(6)
            pe.wait_ge(level_out, LEVELS + 1)
            pe.wait_ge(qb_ready, 1)
            for h in (0, 2, 1, 3):
                r = slice((h % 2) * 64, (h % 2) * 64 + 64)
                for t in range(NT):
                    at = slice(t * 256 + (h // 2) * P, t * 256 + (h // 2) * P + P)
                    last = pe.matmul(psum[:, 6 + h % 2, at], at_[:, t, h, :], gv[:, t, h * P:h * P + P],
                                     start=True, stop=False, skip_group_check=True)
                    for c in range(2 * t, 2 * t + 2):
                        if c == 0:
                            continue
                        q = slice((h // 2) * S + c * 64, (h // 2) * S + c * 64 + 64)
                        last = pe.matmul(psum[(c % 2) * 64:(c % 2) * 64 + 64, 6 + h % 2, at],
                                         gs[r, q], st[r, c - 1, h // 2, :], start=False, stop=True,
                                         skip_group_check=True)
            last.then_inc(gla_o_done, 1)
            pe.wait_ge(gla_o_out, 1)
            pe.wait_ge(proj_out0, 6)
            pe.wait_ge(proj_out1, 6)
            qk_turn("fox", fq, fk)
            attention("fox", fqT, fkT, fv, probs_1, probsT_1, 64, "fv")
            projection("xk", None, input_of("mem", mem))
            projection("xv")
            pe.wait_ge(proj_out0, 8)
            pe.wait_ge(proj_out1, 8)
            out_projection("mix_out", input_of("mix_y"))

            projection("xq", None, input_of("cross"))
            pe.wait_ge(proj_out0, 9)
            pe.wait_ge(proj_out1, 9)
            qk_turn("cross", xq, xk)
            attention("cross", xqT, xkT, xv, probs_1, probsT_1, P, "xq")
            out_projection("cross_out", input_of("cross_y"))

            for t in range(NT):
                turn("moe", t)
            pe.wait_ge(turn_lo, TURN_BASE["moe"] + TURN_BANKS["moe"])
            pe.wait_ge(router_landed, 16 * 5)
            pe.wait_ge(zeros_ready, 1)
            pe.wait_ge(small_split, 2)
            small(*w_router_parts)
            small_turn(routerT, 2)
            pe.wait_ge(logits_out, 2)
            experts()

            swiglu("ffn1_0")
            projection(PROJ[9], None, input_of("diff"))
            for name in PROJ[10:15]:
                projection(name)
            pe.wait_ge(rope_done, 2)
            qk_turn("diff", q2, y)
            attention("diff", q2T, k2T, v2, probs_2, probsT_2, 64, "dv1")
            out_projection("diff_out", input_of("diff_y"))
            swiglu("ffn2_0")
            swiglu("ffn1_1")
            projection(PROJ[15], None, input_of("na"))
            for name in PROJ[16:21]:
                projection(name)
            pe.wait_ge(proj_out0, 21)
            pe.wait_ge(proj_out1, 21)
            qk_turn("na", q2, y)
            attention("na", q2T, k2T, v2, probs_2, probsT_2, 64, "nv1")
            out_projection("na_out", input_of("na_y"))
            swiglu("ffn2_1")

        def outlets(name, t):
            r, q = (lambda n: rstd[:, NORM_AT[n], t:t + 1]), (lambda n: rstd_q[:, SCALED.index(n), t:t + 1])
            half = int(name[-1]) * 512 if name[-1] in "01" else 0
            return {
                "gg": lambda: [(0, 512, gg[:, t, :], r("mix"))],
                "gqk": lambda: [(0, 256, gqk[:, t, 0:256], q("mix")), (256, 512, gqk[:, t, 256:512], r("mix"))],
                "gv": lambda: [(0, 512, gv[:, t, :], r("mix"))],
                "fq": lambda: [(0, 512, fq[:, t, :], q("mix"))],
                "fk": lambda: [(0, 512, fk[:, t, :], r("mix"))],
                "fv": lambda: [(0, 512, fv[:, t, :], r("mix"))],
                "xk": lambda: [(0, 512, xk[:, t, :], r("mem"))],
                "xv": lambda: [(0, 512, xv[:, t, :], r("mem"))],
                "xq": lambda: [(0, 512, xq[:, t, :], q("cross"))],
                "dq": lambda: [(0, 512, q2[:, t, half:half + 512], q("diff"))],
                "dk": lambda: [(0, 512, y[:, t, half:half + 512], r("diff"))],
                "dv": lambda: [(0, 512, v2[:, t, half:half + 512], r("diff"))],
                "nq": lambda: [(0, 512, q2[:, t, half:half + 512], q("na"))],
                "nk": lambda: [(0, 512, y[:, t, half:half + 512], r("na"))],
                "nv": lambda: [(0, 512, v2[:, t, half:half + 512], r("na"))],
            }[name.rstrip("01")]()

        def norm_of(name):
            return {"x": "mem" if name in ("xk", "xv") else "cross", "d": "diff", "n": "na"}.get(name[0], "mix")

        def gain_row(name):
            own = {"mix": "mix_norm", "cross": "cross_norm", "moe": "moe_norm"}
            if name in own:
                return a[own[name]][0]
            if name in ("mem", "final"):
                return a[name + "_norm"]
            layer = {"diff": 0, "na": 1}.get(name.split("_")[0])
            which = 2
            if layer is None:
                layer, which = int(name.split("_")[1]), 0 if name[3] == "1" else 4
            return a["norm_g_2"][layer, which + name.endswith("_p")]

        @block.scalar
        def _(act):
            ahead, gains, squares = [0], [0], [0]

            def hi(n, it=None):
                act.wait_ge(raw_landed[n % RAW], shifted(32 * (n // RAW + 1), it, 32))
                if n >= SPLIT:
                    act.wait_ge(weights_used, shifted(n - SPLIT + 1, it, 6))
                act.activation(w_hi[:, n % SPLIT, :], raw[:, n % RAW, :], ACT.Copy).then_inc(hi_done, 1)

            def split_through(n):
                while ahead[0] <= min(n, CHUNKS - 1):
                    hi(ahead[0])
                    ahead[0] += 1

            def load_gains(through):
                while gains[0] <= min(through, len(NORMS) - 1):
                    i = gains[0]
                    if i >= 2:
                        act.wait_ge(gain_used, i - 1)
                    act.dma_start(gain[:, i % 2, :], row(gain_row(NORMS[i]), D)).then_inc(gain_landed[i % 2], 16)
                    gains[0] += 1

            def square(name, t, src, junk=junk):
                if squares[0]:
                    act.wait_ge(squared, squares[0])
                squares[0] += 1
                act.activation(junk, src, ACT.Square, accum_out=sums[:, NORM_AT[name], t:t + 1]).then_inc(squared, 1)

            def take_turn(name, i):
                t, kk = divmod(i, TURN_BANKS[name] // NT)
                act.wait_ge(turned, TURN_BASE[name] + i + 1)
                act.activation(x_hi[:, t, 4 * kk:4 * kk + 4, :], psum[:, turn_bank(name, i), :].rearrange("p (k c) -> p k c", k=4),
                               ACT.Copy).then_inc(turn_hi, 1)

            def take_turns(name):
                for i in range(TURN_BANKS[name]):
                    take_turn(name, i)

            def take_projection(name):
                j, n = PROJ_AT[name], PROJ_CHUNK[name]
                split_through(n + 3)
                act.wait_ge(proj_t0, j + 1)
                act.wait_ge(rstdq_ready, SCALED.index("mix" if norm_of(name) == "mem" else norm_of(name)) + 1)
                act.wait_ge(rstd_ready, NT * (NORM_AT[norm_of(name)] + 1))
                for t in range(NT if name == "gg" else 1):
                    if t == 1:
                        act.wait_ge(weights_used, n + 2)
                    for c0, c1, dst, scale in outlets(name, t):
                        last = act.activation(dst, psum[:, 2 * (j % 2) + t, c0:c1],
                                              ACT.Silu if name == "gg" else ACT.Copy, scale=scale)
                    last.then_inc(proj_out0 if t == 0 else proj_out1, 1)

            def take_q(name, dst):
                for b in range(QKT_BANKS[name]):
                    act.wait_ge(qk_turned, 2 * (QKT0[name] + b) + 1)
                    act.activation(dst[:, 512 * b:512 * b + 512], psum[:, 4 + 2 * ((QKT0[name] + b) % 2), :],
                                   ACT.Copy).then_inc(q_out, 1)

            def attention(name, probs, midway=None):
                u0 = UNIT0[name]
                for n in range(NT * PAIRS[name]):
                    if n == PAIRS[name] and midway:
                        midway()
                    u, i = u0 + n, n // PAIRS[name]
                    keys = (i + 1) * P if name == "fox" else S
                    act.wait_ge(max_done, u + 1)
                    if n >= 3:
                        act.wait_ge(probs_turned, u - 2)
                    for j in range(2):
                        p_ = probs[:, u % 3, j, 0:keys]
                        src = p_ if name in ("fox", "na") else psum[:, u % 4, j * S:j * S + keys]
                        last = act.activation(p_, src, ACT.Exp, bias=negmax[:, u % 3, j:j + 1],
                                              accum_out=rows[:, u, j:j + 1])
                    last.then_inc(probs_done, 1)

            def square_sum(name, total):
                last = START[total] + dict(PHASES)[total] - 1
                split_through(last + 2)
                act.wait_ge(sum_t0, SUM_AT[total] + 1)
                square(name, 0, psum[:, 4:6, :].rearrange("p b c -> p (b c)"))
                act.wait_ge(weights_used, last + 1)
                square(name, 1, psum[:, 6:8, :].rearrange("p b c -> p (b c)"))

            def residual_squares(name, count):
                for t in range(NT):
                    act.wait_ge(resid_done, count + t + 1)
                    square(name, t, x[:, t, :])

            def norm_turn_resid(name, count):
                take_turns(name)
                for t in range(NT):
                    act.wait_ge(resid_done, count + t + 1)
                    square(name, t, x[:, t, :])
                load_gains(NORM_AT[name] + 2)

            def swiglu(name):
                base, groups, gu0 = START[name], FFN[name], GU0[name]

                def gated(n, g, it=None):
                    par = (gu0 + g) % 2
                    for t in range(NT):
                        if t == 0:
                            act.wait_ge(gu_t0, shifted(gu0 - MOE_GROUPS + g + 1, it, 2))
                        else:
                            act.wait_ge(weights_used, shifted(n + 2, it, 6))
                        act.activation(silu[:, par, t, :], psum[:, 2 * par + t, 0:GROUP], ACT.Silu,
                                       scale=rstd[:, NORM_AT[name], t:t + 1]).then_inc(silu_done, 1)

                def take_hidden(g, it=None):
                    par = (gu0 + g) % 2
                    act.wait_ge(hid_turned, shifted(gu0 + g + 1, it, 2))
                    act.activation(h_hi[:, par, :, :], psum[:, 2 * par, :].rearrange("p (f s) -> p f s", f=2),
                                   ACT.Copy).then_inc(hid_hi, 1)

                def split(n, it):
                    if n < CHUNKS:
                        hi(n, it)

                def step(n, g, it=None):
                    split(n + 2, it)
                    take_hidden(g, it)
                    split(n + 3, it)
                    gated(n, g + 1, it)
                    split(n + 4, it)

                split_through(base + 3)
                act.wait_ge(rstd_ready, NT * (NORM_AT[name] + 1))
                gated(base, 0)
                peel = name == "ffn2_1"
                with act.Fori(0, (groups - 1) // 2 - peel) as it:
                    step(base + 2, 0, it)
                    step(base + 5, 1, it)
                for g in range((groups - 1) // 2 * 2 - 2 * peel, groups - 1):
                    step(base + 2 + 3 * g, g)
                ahead[0] = base + 3 * groups + 1
                take_hidden(groups - 1)

            def experts():
                base = START["moe"]

                def take_gather(w, quarters):
                    for q in quarters:
                        act.wait_ge(gathered, 2 * w + q + 1)
                        for src, hi_, lo_ in gathered_views(w, q):
                            last = act.activation(hi_, src, ACT.Copy)
                        last.then_inc(gathered_hi, 1)

                def gated(n, w, g, it=None):
                    act.wait_ge(weights_used, shifted(n + 2, it, 6))
                    act.activation(silu[:, g % 2, 0, :], psum[:, g % 2, 0:GROUP], ACT.Silu,
                                   scale=slotv[:, w, 16:17]).then_inc(silu_done, NT)

                def take_hidden(g, it=None):
                    act.wait_ge(hid_turned, shifted(g + 1, it, 2))
                    act.activation(h_hi[:, g % 2, :, 0:P], psum[:, g % 2, 0:2 * P].rearrange("p (f s) -> p f s", f=2),
                                   ACT.Copy).then_inc(hid_hi, 1)

                def step(g, it=None, gathers=False):
                    n = base + 2 + 3 * g
                    hi(n + 2, it)
                    if gathers:
                        take_gather(2, (0, 1))
                    take_hidden(g, it)
                    hi(n + 3, it)
                    gated(n, (g + 1) // 8, g + 1, it)
                    if gathers:
                        take_gather(2, (2, 3))
                    hi(n + 4, it)

                def take_slot_y(w):
                    act.wait_ge(weights_used, base + 24 * (w + 1) + (2 if w < WINDOWS - 1 else 0))
                    if w:
                        act.wait_ge(scattered, NT * w)
                    act.activation(slot_y[0], psum[:, 4 + 2 * (w % 2):6 + 2 * (w % 2), :].rearrange("p b c -> p (b c)"),
                                   ACT.Copy).then_inc(slot_y_out, 1)

                act.activation(y_hi, y[:, :, :], ACT.Copy).then_inc(gained_hi, 1)
                for t in range(NT):
                    act.wait_ge(route_in, t + 1)
                    act.activation(rt[:, t, 80:84], rt[:, t, 24:28], ACT.Exp, bias=rt[:, t, 64:65],
                                   accum_out=rt[:, t, 65:66]).then_inc(route_exp, 1)
                take_gather(0, range(4))
                act.wait_ge(pick_turned, 1)
                act.activation(pickT.rearrange("p w t s -> p (w t s)"), psum[:, 6:8, :].rearrange("p b c -> p (b c)"),
                               ACT.Copy).then_inc(pickT_out, 1)
                for t in range(NT):
                    act.wait_ge(route_in, NT + t + 1)
                    act.activation(rt[:, t, 67:68], rt[:, t, 66:67], ACT.Exp).then_inc(route_exp, 1)
                split_through(base + 3)
                act.wait_ge(slotv_out, 1)
                gated(base, 0, 0)
                for w in range(WINDOWS):
                    with act.Fori(0, 3) as it:
                        step(8 * w, it)
                        step(8 * w + 1, it)
                    step(8 * w + 6, None, w == 1)
                    if w < WINDOWS - 1:
                        step(8 * w + 7)
                        take_slot_y(w)
                ahead[0] = base + 24 * WINDOWS + 1
                take_hidden(8 * WINDOWS - 1)
                split_through(base + 24 * WINDOWS + 1)
                take_slot_y(WINDOWS - 1)
                act.wait_ge(over_known, 1)
                with act.If(act.value_load(is_over, min_val=0, max_val=1) > 0):
                    group = act.value_load(over_group, min_val=0, max_val=WINDOWS - 1)
                    with act.Fori(0, 4) as it:
                        e = bass.ds(group * 4 + it, 1)
                        act.wait_ge(over_down, it + 1)
                        act.dma_start(over_w.rearrange("p (k c) -> p k c", k=KD),
                                      a["w_expert_gate"][0][e].rearrange("e (k p) c -> p (e k) c", p=P)).then_inc(over_landed, 16)
                        act.wait_ge(over_gate, it + 1)
                        act.dma_start(over_w.rearrange("p (k c) -> p k c", k=KD),
                                      a["w_expert_up"][0][e].rearrange("e (k p) c -> p (e k) c", p=P)).then_inc(over_landed, 16)
                        act.activation(over_silu, psum[:, 0, :], ACT.Silu, scale=over_slotv[:, 16:17]).then_inc(over_silued, 1)
                        act.wait_ge(over_up, it + 1)
                        act.dma_start(over_w.rearrange("p (k c) -> p k c", k=4),
                                      a["w_expert_down"][0][e].rearrange("e (k p) c -> p (e k) c", p=P)).then_inc(over_landed, 16)

            load_gains(0)
            act.dma_start(const[:, :], a["consts"][:, 0:C_TRI]).then_inc(const_landed, 16)
            split_through(0)
            take_turns("mix")
            split_through(2)
            for t in range(NT):
                act.wait_ge(x_landed[t], 16)
                square("mix", t, x[:, t, :])
            load_gains(NORM_AT["mix"] + 2)
            take_projection("gg")
            take_projection("gqk")
            take_q("gla", gqT)
            act.wait_ge(logits_in, 1)
            act.activation(lsg, lg, ACT.Abs).then_inc(logsig_abs, 1)
            act.wait_ge(logsig_abs, 1)
            act.activation(lsg, lsg, ACT.Exp, scale=-1.0).then_inc(act_chain, 1)
            act.wait_ge(act_chain, 1)
            act.activation(lsg, lsg, ACT.Ln, bias=1.0).then_inc(logsig_ln, 1)
            take_projection("gv")
            act.wait_ge(decay_done, 2)
            act.activation(gs, psum[:, 5, :], ACT.Exp).then_inc(suffix_out, 1)
            act.wait_ge(decay_done, 3)
            act.wait_ge(gb_out, 1)
            act.activation(gexp, gb, ACT.Exp).then_inc(expb_ready, 1)

            def decay(l):
                act.wait_ge(diff_ready, l + 1)
                act.activation(ge, ge, ACT.Abs).then_inc(act_chain, 1)
                act.wait_ge(act_chain, l + 2)
                act.activation(ge, ge, ACT.Exp, scale=-1.0).then_inc(decay_exp, 1)

            split_through(PROJ_CHUNK["fq"] + 3)
            decay(0)
            decay(1)
            take_projection("fq")
            decay(2)
            decay(3)
            take_projection("fk")
            decay(4)
            take_projection("fv")
            decay(5)

            act.wait_ge(gla_o_out, 1)
            take_q("fox", region(4096, 1024))
            act.wait_ge(qk_turned, 2 * (QKT0["fox"] + QKT_BANKS["fox"]))
            act.dma_start(mem[:, :, :], a["mem"][0].rearrange("(t p) c -> p t c", p=P)).then_inc(mem_landed, 16)

            def mem_squares():
                act.wait_ge(mem_landed, 16)
                for t in range(NT):
                    square("mem", t, mem[:, t, :], fb[:, 1024:2048])

            attention("fox", probs_1, mem_squares)
            take_turns("mem")
            load_gains(NORM_AT["mem"] + 2)
            take_projection("xk")
            take_projection("xv")
            take_turns("mix_y")
            split_through(START["mix_out"] + 5)
            act.dma_start(w_router[:, :, 0:4], a["w_router_group"][0].rearrange("(k p) c -> p k c", p=P)).then_inc(router_landed, 16)
            act.dma_start(w_router[:, :, 4:20], a["w_router_expert"][0].rearrange("(k p) c -> p k c", p=P)).then_inc(router_landed, 16)
            act.dma_start(slots, a["consts"][:, C_SLOT:C_END]).then_inc(router_landed, 16)
            act.dma_start(b_router[:, 0:4], row(a["b_router_group"][0], 4)).then_inc(router_landed, 16)
            act.dma_start(b_router[:, 4:20], row(a["b_router_expert"][0], 16)).then_inc(router_landed, 16)
            norm_turn_resid("cross", 0)
            take_projection("xq")
            take_q("cross", region(6144, 1024))
            attention("cross", probs_1)
            take_turns("cross_y")
            split_through(START["cross_out"] + 3)
            norm_turn_resid("moe", NT)
            split_through(START["moe"] + 2)
            experts()
            split_through(START["moe"] + 3 * MOE_GROUPS + 1)
            residual_squares("final", 2 * NT)
            norm_turn_resid("ffn1_0", 3 * NT)
            act.dma_start(subln, row(a["diff_subln_2"][0], P)).then_inc(diffw_landed, 16)
            act.dma_start(lamv, row(a["diff_lambda_2"][0].rearrange("a b -> (a b)"), 256)).then_inc(diffw_landed, 16)
            act.dma_start(namask, a["consts"][:, C_NAMASK:C_SLOT]).then_inc(namask_landed, 16)
            swiglu("ffn1_0")
            square_sum("ffn1_0_p", "ffn1_0")
            norm_turn_resid("diff", 4 * NT)
            for name in PROJ[9:13]:
                take_projection(name)
            act.wait_ge(lam_sum, 1)
            act.activation(lams[:, 2:4], lams[:, 0:2], ACT.Exp).then_inc(lam_exp, 1)
            for name in PROJ[13:15]:
                take_projection(name)
            take_q("diff", region(2560, 2048))
            attention("diff", probs_2)
            take_turns("diff_y")
            square_sum("diff_p", "diff_out")
            norm_turn_resid("ffn2_0", 5 * NT)
            act.dma_start(region(6656, 6144), a["na_biases"]).then_inc(nab_landed, 16)
            swiglu("ffn2_0")
            square_sum("ffn2_0_p", "ffn2_0")
            norm_turn_resid("ffn1_1", 6 * NT)
            swiglu("ffn1_1")
            square_sum("ffn1_1_p", "ffn1_1")
            norm_turn_resid("na", 7 * NT)
            for name in PROJ[15:21]:
                take_projection(name)
            take_q("na", region(2560, 2048))
            attention("na", probs_2)
            take_turns("na_y")
            square_sum("na_p", "na_out")
            norm_turn_resid("ffn2_1", 8 * NT)
            swiglu("ffn2_1")
            square_sum("ffn2_1_p", "ffn2_1")

        @block.vector
        def _(dve):
            ahead, chained, resid = [0], [0], [0]

            def lo(n, it=None):
                dve.wait_ge(hi_done, shifted(n + 1, it, 6))
                dve.tensor_tensor(w_lo[:, n % SPLIT, 0:LO_V], raw[:, n % RAW, 0:LO_V],
                                  w_hi[:, n % SPLIT, 0:LO_V].bitcast(F32), ALU.subtract).then_inc(lo_v_done, 1)

            def split_through(n):
                while ahead[0] <= min(n, CHUNKS - 1):
                    lo(ahead[0])
                    ahead[0] += 1

            def link(ins):
                chained[0] += 1
                ins.then_inc(dve_chain, 1)
                dve.wait_ge(dve_chain, chained[0])

            def split_small(w, parts):
                link(dve.tensor_copy(parts[0], w))
                dve.tensor_tensor(parts[1], w, parts[0].bitcast(F32), ALU.subtract).then_inc(small_split, 1)

            def take_turn(name, i):
                t, kk = divmod(i, TURN_BANKS[name] // NT)
                dve.wait_ge(turn_hi, TURN_BASE[name] + i + 1)
                xh = x_hi[:, t, 4 * kk:4 * kk + 4, :].bitcast(F32)
                dve.tensor_tensor(x_lo[:, t, 4 * kk:4 * kk + 4, :], psum[:, turn_bank(name, i), :].rearrange("p (k c) -> p k c", k=4),
                                  xh, ALU.subtract).then_inc(turn_lo, 1)

            def take_turns(name):
                for i in range(TURN_BANKS[name]):
                    take_turn(name, i)

            def take_projection(name):
                j, n = PROJ_AT[name], PROJ_CHUNK[name]
                split_through(n + 3)
                if name == "gg":
                    return
                dve.wait_ge(weights_used, n + 2)
                dve.wait_ge(rstdq_ready, SCALED.index("mix" if norm_of(name) == "mem" else norm_of(name)) + 1)
                dve.wait_ge(rstd_ready, NT * (NORM_AT[norm_of(name)] + 1))
                if j == 1:
                    dve.wait_ge(proj_out1, 1)
                for c0, c1, dst, scale in outlets(name, 1):
                    last = dve.tensor_scalar(dst, psum[:, 2 * (j % 2) + 1, c0:c1], scale, None, ALU.mult)
                last.then_inc(proj_out1, 1)

            def take_k(name, dst):
                for b in range(QKT_BANKS[name]):
                    dve.wait_ge(qk_turned, 2 * (QKT0[name] + b) + 2)
                    dve.tensor_copy(dst[:, 512 * b:512 * b + 512],
                                    psum[:, 5 + 2 * ((QKT0[name] + b) % 2), :]).then_inc(k_out, 1)

            def attention(name, probs, probsT, take_group):
                pairs, gsize, u0 = PAIRS[name], GSIZE[name], UNIT0[name]
                units = NT * pairs
                masked = name in ("fox", "na")

                def keys(n):
                    return (n // pairs + 1) * P if name == "fox" else S

                def maxima(n):
                    u, i = u0 + n, n // pairs
                    dve.wait_ge(scores, u + 1)
                    nm = negmax[:, u % 3, :]
                    if not masked:
                        dve.tensor_reduce(nm, psum[:, u % 4, :].rearrange("p (m k) -> p m k", m=2), AX.X,
                                          ALU.max, negate=True).then_inc(max_done, 1)
                        return
                    if n >= 3:
                        dve.wait_ge(probs_turned, u - 2)
                    if u:
                        dve.wait_ge(max_done, u)
                    for j in range(2):
                        m = score_map(name, n % pairs, j)
                        if name == "fox":
                            mask = causal[:, P - i * P:2 * P]
                        else:
                            mask = nab[:, m, 2 - 2 * i:6 - 2 * i, :].rearrange("p r c -> p (r c)")
                        last = dve.tensor_tensor_reduce(probs[:, u % 3, j, 0:keys(n)], psum[:, u % 4, j * S:j * S + keys(n)],
                                                        mask, 1.0, LOWEST, ALU.add, ALU.max, rrow[:, 6 + j:7 + j])
                    link(last)
                    dve.tensor_scalar(nm, rrow[:, 6:8], -1.0, None, ALU.mult).then_inc(max_done, 1)

                def copy_turned(n):
                    u = u0 + n
                    dve.wait_ge(probs_turned, u + 1)
                    src, dst = psum[:, 4 + u % 2, :], probsT[:, u % 2, :]
                    if keys(n) < S:
                        src, dst = (z.rearrange("p (m k) -> p m k", m=2)[:, :, 0:P] for z in (src, dst))
                    dve.tensor_copy(dst, src).then_inc(probsT_done, 1)

                maxima(0)
                maxima(1)
                for n in range(units):
                    if n + 2 < units:
                        maxima(n + 2)
                    copy_turned(n)
                    if n >= 1 and n % gsize == 0:
                        take_group(n // gsize - 1)
                take_group(units // gsize - 1)

            def weighted(name, dst):
                def take(g):
                    gsize, grp = GSIZE[name], GROUP0[name] + g
                    heads = 2 * gsize
                    dve.wait_ge(pv_done, grp + 1)
                    u = UNIT0[name] + g * gsize
                    r_ = rheads[:, 0:heads]
                    if name == "cross":
                        link(dve.reciprocal(r_, rows[:, u:u + gsize, :].rearrange("p u m -> p (u m)")))
                    else:
                        link(dve.reciprocal(r_.rearrange("p (r j h) -> p r j h", r=2, j=2),
                                            rows[:, u:u + gsize, :].rearrange("p (r h) j -> p r j h", r=2)))
                    last = dve.tensor_tensor(dst(g).rearrange("p (h d) -> p h d", h=heads),
                                             psum[:, 6 + grp % 2, :].rearrange("p (h d) -> p h d", h=heads),
                                             r_.unsqueeze(2).to_broadcast([P, heads, 512 // heads]), ALU.mult)
                    link(last)
                    dve.sem_inc(pv_taken, 1)
                return take

            def take_diff(g):
                grp = GROUP0["diff"] + g
                i, h = divmod(2 * g, 8)
                dve.wait_ge(pv_done, grp + 1)
                u = UNIT0["diff"] + 2 * g
                link(dve.reciprocal(rrow[:, 0:4].rearrange("p (j h) -> p j h", j=2), rows[:, u:u + 2, :].rearrange("p h j -> p j h")))
                link(dve.tensor_scalar(rrow[:, 4:6], rrow[:, 0:4].rearrange("p (h m) -> p h m", m=2)[:, :, 1],
                                       lams[:, 5:6], None, ALU.mult))
                for k in range(2):
                    pv = psum[:, 6 + grp % 2, :]
                    link(dve.tensor_scalar(ropet[:, 0:P], pv[:, 256 * k:256 * k + P], rrow[:, 2 * k:2 * k + 1], None, ALU.mult))
                    link(dve.scalar_tensor_tensor(y[:, i, (h + k) * P:(h + k) * P + P], pv[:, 256 * k + P:256 * k + 2 * P],
                                                  rrow[:, 4 + k:5 + k], ropet[:, 0:P], ALU.mult, ALU.add))
                dve.sem_inc(pv_taken, 1)

            def head_norm(name, view, tmp, gain_, turns):
                k, (heads, d) = HEADNORMS.index(name), view.shape[1:]
                link(dve.tensor_tensor(tmp, view, view, ALU.mult))
                dve.tensor_reduce(hsum[:, 0:heads], tmp, AX.X, ALU.add).then_inc(head_sums, 1)
                take_turn(turns, 0)
                take_turn(turns, 1)
                dve.wait_ge(head_rstd, k + 1)
                link(dve.tensor_tensor(view, view, hrstd[:, 0:heads].unsqueeze(2).to_broadcast([P, heads, d]), ALU.mult))
                return dve.tensor_tensor(view, view, gain_, ALU.mult)

            def residual(total, following=None, post=None):
                last = START[total] + dict(PHASES)[total] - 1
                split_through(last + 2)
                if post:
                    i = NORM_AT[post]
                    dve.wait_ge(gain_landed[i % 2], 16 * (i // 2 + 1))
                if following:
                    i_next = NORM_AT[following]
                    dve.wait_ge(gain_landed[i_next % 2], 16 * (i_next // 2 + 1))
                    dve.wait_ge(turned, TURN_BASE[following])
                for t in range(NT):
                    if post:
                        dve.wait_ge(rstd_ready, NT * i + t + 1)
                    elif t == 0:
                        dve.wait_ge(sum_t0, SUM_AT[total] + 1)
                    else:
                        dve.wait_ge(weights_used, last + 1)
                    for half in range(2):
                        c = slice(512 * half, 512 * half + 512)
                        bank = psum[:, 4 + 2 * t + half, :]
                        if post:
                            link(dve.scalar_tensor_tensor(y[:, t, c], bank, rstd[:, i, t:t + 1], gain[:, i % 2, c],
                                                          ALU.mult, ALU.mult))
                            bank = y[:, t, c]
                        added = dve.tensor_tensor(x[:, t, c], x[:, t, c], bank, ALU.add)
                        if half == 0:
                            link(added)
                        else:
                            resid[0] += 1
                            added.then_inc(resid_done, 1)
                            dve.wait_ge(resid_done, resid[0])
                        if following:
                            dve.tensor_tensor(y[:, t, c], x[:, t, c], gain[:, i_next % 2, c], ALU.mult).then_inc(turn_src, 1)
                            if t * 2 + half in (1, 2):
                                take_turn(following, t * 2 + half - 1)
                if following:
                    dve.wait_ge(turn_src, TURN_BASE[following] + 4)
                    dve.sem_inc(gain_used, 2 if post else 1)
                    take_turn(following, 2)
                    take_turn(following, 3)

            def swiglu(name):
                base, groups, gu0 = START[name], FFN[name], GU0[name]

                def hidden(g, it=None):
                    par = (gu0 + g) % 2
                    for t in range(NT):
                        scale = rstd[:, NORM_AT[name], t:t + 1]
                        dve.wait_ge(silu_done, shifted(NT * (gu0 + g) + t + 1, it, 2 * NT))
                        dve.scalar_tensor_tensor(hid[:, par, t, :], psum[:, 2 * par + t, GROUP:2 * GROUP], scale,
                                                 silu[:, par, t, :], ALU.mult, ALU.mult).then_inc(hid_done, 1)

                def take_hidden(g, it=None):
                    par = (gu0 + g) % 2
                    dve.wait_ge(hid_hi, shifted(gu0 + g + 1, it, 2))
                    dve.tensor_tensor(h_lo[:, par, :, :], psum[:, 2 * par, :].rearrange("p (f s) -> p f s", f=2),
                                      h_hi[:, par, :, :].bitcast(F32), ALU.subtract).then_inc(hid_lo, 1)

                def split(n, it):
                    if n < CHUNKS:
                        lo(n, it)

                def step(n, g, it=None):
                    split(n + 2, it)
                    take_hidden(g, it)
                    split(n + 3, it)
                    hidden(g + 1, it)
                    split(n + 4, it)

                split_through(base + 3)
                hidden(0)
                peel = name == "ffn2_1"
                with dve.Fori(0, (groups - 1) // 2 - peel) as it:
                    step(base + 2, 0, it)
                    step(base + 5, 1, it)
                for g in range((groups - 1) // 2 * 2 - 2 * peel, groups - 1):
                    step(base + 2 + 3 * g, g)
                ahead[0] = base + 3 * groups + 1
                take_hidden(groups - 1)

            def take_gather(w, quarters):
                for q in quarters:
                    dve.wait_ge(gathered_hi, 2 * w + q + 1)
                    for src, hi_, lo_ in gathered_views(w, q):
                        last = dve.tensor_tensor(lo_, src, hi_.bitcast(F32), ALU.subtract)
                    last.then_inc(gathered_lo, 1)

            def experts():
                base = START["moe"]

                def hidden(w, g, it=None):
                    e = bass.ds(it + (g % 8) // 2, 1) if it is not None else slice((g % 8) // 2, (g % 8) // 2 + 1)
                    by_group = slotv[:, w, 4 * w:4 * w + 4]
                    dve.wait_ge(silu_done, shifted(NT * (g + 1), it, 2 * NT))
                    dve.scalar_tensor_tensor(hid[:, g % 2, 0, :], psum[:, g % 2, GROUP:2 * GROUP], by_group[:, e],
                                             silu[:, g % 2, 0, :], ALU.mult, ALU.mult).then_inc(hid_done, NT)

                def take_hidden(g, it=None):
                    dve.wait_ge(hid_hi, shifted(g + 1, it, 2))
                    dve.tensor_tensor(h_lo[:, g % 2, :, 0:P], psum[:, g % 2, 0:2 * P].rearrange("p (f s) -> p f s", f=2),
                                      h_hi[:, g % 2, :, 0:P].bitcast(F32), ALU.subtract).then_inc(hid_lo, 1)

                def step(g, it=None, gathers=False):
                    n = base + 2 + 3 * g
                    lo(n + 2, it)
                    if gathers:
                        take_gather(2, (0, 1))
                    take_hidden(g, it)
                    lo(n + 3, it)
                    hidden((g + 1) // 8, g + 1, it)
                    if gathers:
                        take_gather(2, (2, 3))
                    lo(n + 4, it)

                def take_slot_y(w):
                    dve.wait_ge(slot_y_out, w + 1)
                    dve.tensor_tensor(slot_y[1], psum[:, 4 + 2 * (w % 2):6 + 2 * (w % 2), :].rearrange("p b c -> p (b c)"),
                                      slot_y[0].bitcast(F32), ALU.subtract).then_inc(slot_y_lo, 1)

                def take_scatter(w):
                    if w:
                        dve.wait_ge(scatter_taken, NT * w)
                    for t in range(NT):
                        dve.wait_ge(scattered, NT * w + t + 1)
                        banks = psum[:, 2:4, :] if t == 0 else psum[:, 4 + 2 * (w % 2):6 + 2 * (w % 2), :]
                        x_ = x[:, t, :].rearrange("p (b c) -> p b c", b=2)
                        dve.tensor_tensor(x_, x_, banks, ALU.add).then_inc(scatter_taken, 1)

                split_through(base + 3)
                dve.wait_ge(slotv_done, 1)
                dve.tensor_copy(slotv, psum[:, 5, 32:160].rearrange("p (w c) -> p w c", w=WINDOWS)[:, :, 0:17]).then_inc(slotv_out, 1)
                dve.wait_ge(slotv_out, 1)
                hidden(0, 0)
                for t in range(NT):
                    link(dve.tensor_scalar(rt[:, t, 105:106], rt[:, t, 104:105], -128.0, None, ALU.add))
                    dve.tensor_scalar(over_pick[:, t, :], slots, rt[:, t, 105:106], None, ALU.is_equal)
                v = rt[:, 0, :]
                link(dve.max(v[:, 120:128], v[:, 112:120]))
                link(dve.max_index(v[:, 128:136].bitcast(U32), v[:, 120:128], v[:, 112:120]))
                link(dve.tensor_scalar(v[:, 138:139], v[:, 120:121], P + 0.5, None, ALU.is_gt))
                dve.tensor_copy(v[:, 139:140].bitcast(I32), v[:, 138:139]).then_inc(over_known, 1)
                for w in range(WINDOWS):
                    with dve.Fori(0, 3) as it:
                        step(8 * w, it)
                        step(8 * w + 1, it)
                    if w:
                        take_scatter(w - 1)
                    step(8 * w + 6, None, w == 1)
                    if w < WINDOWS - 1:
                        step(8 * w + 7)
                        take_slot_y(w)
                ahead[0] = base + 24 * WINDOWS + 1
                take_hidden(8 * WINDOWS - 1)
                split_through(base + 24 * WINDOWS + 1)
                take_slot_y(WINDOWS - 1)
                take_scatter(WINDOWS - 1)
                dve.wait_ge(over_known, 1)
                with dve.If(dve.value_load(is_over, min_val=0, max_val=1) > 0):
                    group = dve.value_load(over_group, min_val=0, max_val=WINDOWS - 1)
                    dve.wait_ge(scatter_taken, NT * WINDOWS)
                    dve.wait_ge(over_in, 1)
                    dve.tensor_copy(over_x.rearrange("p k s -> p (k s)"), psum[:, 0:2, :].rearrange("p b c -> p (b c)"))
                    dve.tensor_copy(over_pickT.rearrange("p t s -> p (t s)"), psum[:, 2, 0:256])
                    dve.tensor_copy(over_slotv, psum[:, 3, 0:17]).then_inc(over_taken, 1)
                    dve.wait_ge(over_taken, 1)
                    with dve.Fori(0, 4) as it:
                        dve.wait_ge(over_silued, it + 1)
                        dve.wait_ge(over_up, it + 1)
                        dve.scalar_tensor_tensor(over_hid, psum[:, 1, :], over_slotv[:, bass.ds(group * 4 + it, 1)],
                                                 over_silu, ALU.mult, ALU.mult).then_inc(over_hidden, 1)
                        dve.wait_ge(over_turned, it + 1)
                        dve.tensor_copy(over_hidT, psum[:, 2, :]).then_inc(over_hidT_out, 1)
                    dve.wait_ge(over_down, 5)
                    dve.tensor_copy(over_y, psum[:, 4:6, :].rearrange("p b c -> p (b c)")).then_inc(over_y_out, 1)
                    dve.wait_ge(over_scattered, 1)
                    for t in range(NT):
                        dve.tensor_tensor(x[:, t, :], x[:, t, :], psum[:, 2 * t:2 * t + 2, :].rearrange("p b c -> p (b c)"),
                                          ALU.add).then_inc(over_added, 1)
                    dve.wait_ge(over_added, NT)
                dve.wait_ge(scatter_taken, NT * WINDOWS)
                dve.sem_inc(resid_done, NT)
                resid[0] += NT

            dve.wait_ge(gain_landed[0], 16)
            for t in range(NT):
                dve.wait_ge(x_landed[t], 16)
                for half in range(2):
                    c = slice(512 * half, 512 * half + 512)
                    dve.tensor_tensor(y[:, t, c], x[:, t, c], gain[:, 0, c], ALU.mult).then_inc(turn_src, 1)
                if t == 1:
                    dve.wait_ge(turn_src, 4)
                    dve.sem_inc(gain_used, 1)
                take_turn("mix", 2 * t)
                take_turn("mix", 2 * t + 1)
                if t == 0:
                    split_through(0)
            dve.wait_ge(const_landed, 16)
            split_through(PROJ_CHUNK["gqk"] + 1)
            dve.wait_ge(mixw_landed, 16 * MIX_LOADS)
            split_small(w_small, w_small_parts)
            split_through(PROJ_CHUNK["gqk"] + 2)
            dve.wait_ge(logits_done, 1)
            dve.tensor_copy(smallT, psum[0:24, 4, 0:S]).then_inc(small_out, 1)
            dve.wait_ge(logits_done, 2)
            dve.wait_ge(rstd_ready, NT)
            for t in range(NT):
                link(dve.tensor_scalar(lg[:, t, 0:24], psum[:, 4, t * 64:t * 64 + 24], rstd[:, 0, t:t + 1], None, ALU.mult))
            link(dve.tensor_tensor(lg[:, :, 0:8], lg[:, :, 0:8], bias_g[:, 0:8].unsqueeze(1).to_broadcast([P, NT, 8]), ALU.add))
            dve.sem_inc(logits_out, 1)
            take_projection("gqk")
            dve.wait_ge(ga_turned, 1)
            dve.tensor_copy(gaT[0:16, :], psum[0:16, 5, 0:S]).then_inc(ga_out, 1)
            dve.wait_ge(alpha_done, 1)
            dve.tensor_tensor(lg[:, :, 8:264], psum[:, 6, :].rearrange("p (t c) -> p t c", t=NT),
                              bias_g[:, 8:264].unsqueeze(1).to_broadcast([P, NT, 256]), ALU.add).then_inc(logits_in, 1)
            take_k("gla", gkT)
            dve.wait_ge(logsig_ln, 1)
            dve.scalar_tensor_tensor(lg, lg, 0.0, lsg, ALU.min, ALU.subtract).then_inc(logsig_done, 1)
            take_projection("gv")
            dve.wait_ge(decay_done, 1)
            dve.tensor_copy(gb, psum[:, 4, :]).then_inc(gb_out, 1)
            dve.wait_ge(decay_done, 3)
            dve.tensor_scalar(ct[0:8, :], psum[0:8, 7, 0:S], -1.0, None, ALU.mult).then_inc(ct_out, 1)
            dve.wait_ge(suffix_out, 1)
            dve.wait_ge(proj_out0, 2)
            dve.wait_ge(k_out, 1)
            dve.tensor_tensor(gks, gqk[:, :, 256:512], gs.rearrange("p (t c) -> p t c", t=NT), ALU.mult).then_inc(ks_ready, 1)
            def level_start(l):
                h = 1 << l
                if l:
                    dve.wait_ge(z_ready, l)
                v = gb.rearrange("p (n c) -> p n c", c=2 * h)
                dve.tensor_tensor(ge.rearrange("p (n c) -> p n c", c=2 * h), v,
                                  v[:, :, h - 1:h].to_broadcast([P, 512 // (2 * h), 2 * h]), ALU.subtract).then_inc(diff_ready, 1)

            def level_operand(l):
                h = 1 << l
                dve.wait_ge(decay_exp, l + 1)
                if l >= 2:
                    dve.wait_ge(level_done, l - 1)
                v = [z.rearrange("p (n c) -> p n c", c=2 * h) for z in (gz[:, l % 2, :], gkT, gqT, ge)]
                dve.tensor_tensor(v[0][:, :, 0:h], v[1][:, :, 0:h], v[3][:, :, 0:h], ALU.mult)
                dve.tensor_tensor(v[0][:, :, h:2 * h], v[2][:, :, h:2 * h], v[3][:, :, h:2 * h], ALU.mult).then_inc(z_ready, 1)

            def level_take(l):
                dve.wait_ge(level_done, l + 1)
                dve.wait_ge(level_out if l else at_zero, max(l, 1))
                mask = masks[:, l * P:l * P + P].unsqueeze(1).unsqueeze(1).to_broadcast([P, NT, 2, P])
                for h in range(2):
                    last = dve.copy_predicated(at_.rearrange("p t (g h) q -> p t g h q", h=2)[:, :, :, h, :], mask,
                                               psum[:, 4 + 2 * (l % 2) + h, :].rearrange("p (t g q) -> p t g q", t=NT, g=2))
                last.then_inc(level_out, 1)

            split_through(PROJ_CHUNK["fq"] + 3)
            dve.wait_ge(gb_out, 1)
            dve.wait_ge(q_out, 1)
            level_start(0)
            level_operand(0)
            level_start(1)
            level_operand(1)
            take_projection("fq")
            dve.wait_ge(expb_ready, 1)
            dve.wait_ge(q_out, 1)
            dve.wait_ge(ks_ready, 1)
            dve.tensor_tensor(gs, gqT, gexp, ALU.mult).then_inc(qb_ready, 1)
            dve.wait_ge(u_done, 1)
            u_ = [psum[:, 6, 0:256], psum[:, 7, 0:256], psum[:, 6, 256:512]]
            link(dve.tensor_copy(st[:, 0, :, :], u_[0].rearrange("p (f v) -> p f v", f=2)))
            for c in (1, 2):
                for f in range(2):
                    last = dve.scalar_tensor_tensor(st[:, c, f, :], st[:, c - 1, f, :],
                                                    gexp[:, f * S + c * 64 + 63:f * S + c * 64 + 64],
                                                    u_[c][:, f * P:f * P + P], ALU.mult, ALU.add)
                link(last)
            dve.sem_inc(state_ready, 1)

            level_start(2)
            level_take(0)
            level_operand(2)
            level_start(3)
            level_take(1)
            level_operand(3)
            take_projection("fk")
            level_start(4)
            level_take(2)
            level_operand(4)
            level_start(5)
            level_take(3)
            take_projection("fv")
            level_operand(5)
            level_take(4)
            level_take(5)
            level_take(6)
            dve.wait_ge(gla_o_done, 1)
            for h in range(2):
                dst = y[:, :, 512:1024].rearrange("p t (g h v) -> p t g h v", g=2, h=2)[:, :, :, h, :]
                last = dve.tensor_copy(dst, psum[:, 6 + h, :].rearrange("p (t g v) -> p t g v", t=NT, g=2))
            last.then_inc(gla_o_out, 1)
            take_k("fox", region(6144, 1024))
            attention("fox", probs_1, probsT_1, weighted("fox", lambda g: y[:, g, 0:512]))
            dve.wait_ge(squared, NT * NORM_AT["mem"] + NT)
            head_norm("fox", y[:, 1, 0:512].rearrange("p (h d) -> p h d", h=8), fb[:, 1536:2048].rearrange("p (h d) -> p h d", h=8),
                      fox_gain.rearrange("p (h d) -> p h d", h=8), "mem").then_inc(dve_chain, 1)
            chained[0] += 1
            take_turn("mem", 2)
            take_turn("mem", 3)
            dve.wait_ge(dve_chain, chained[0])
            dve.wait_ge(heads_normed, 2)
            dve.sem_inc(turn_src, 4)
            take_projection("xk")
            take_projection("xv")
            take_turns("mix_y")
            split_through(START["mix_out"] + 5)
            residual("mix_out", "cross")
            take_projection("xq")
            take_k("cross", region(4096, 1024))
            attention("cross", probs_1, probsT_1, weighted("cross", lambda g: y[:, g, 0:512]))
            dve.sem_inc(turn_src, 2)
            take_turns("cross_y")
            dve.wait_ge(router_landed, 16 * 5)
            split_small(w_router, w_router_parts)
            residual("cross_out", "moe")
            split_through(START["moe"] + 2)
            dve.wait_ge(logits_done, 3)
            dve.tensor_copy(routerT, psum[0:20, 4, 0:S]).then_inc(small_out, 1)
            dve.wait_ge(logits_done, 4)
            dve.wait_ge(rstd_ready, NT * (NORM_AT["moe"] + 1))
            dve.memset(rt[:, 0, 112:120], NEG)
            link(dve.memset(rt[:, :, 24:40], NEG))
            for t in range(NT):
                link(dve.scalar_tensor_tensor(rt[:, t, 0:20], psum[:, 4, t * 64:t * 64 + 20], rstd[:, NORM_AT["moe"], t:t + 1],
                                              b_router, ALU.mult, ALU.add))
            dve.sem_inc(logits_out, 1)
            for t in range(NT):
                v = rt[:, t, :]
                g8, top, idx, sc = v[:, 24:32], v[:, 40:48], v[:, 48:56].bitcast(U32), v[:, 64:80]
                link(dve.tensor_copy(g8[:, 0:4], v[:, 0:4]))
                link(dve.max(top, g8))
                link(dve.max_index(idx, top, g8))
                dve.tensor_scalar(sc[:, 0:1], top[:, 0:1], -1.0, None, ALU.mult).then_inc(route_in, 1)
                link(dve.tensor_copy(sc[:, 4:5], idx[:, 0:1]))
                link(dve.tensor_scalar(v[:, 56:60], iota4, sc[:, 4:5], None, ALU.is_equal))
            dve.sem_inc(hot_ready, 1)
            dve.wait_ge(gained_hi, 1)
            dve.tensor_tensor(y_lo, y[:, :, :], y_hi.bitcast(F32), ALU.subtract).then_inc(gained_lo, 1)
            dve.wait_ge(ranked, 1)
            for t in range(NT):
                v = rt[:, t, :]
                link(dve.tensor_tensor(v[:, 96:100], psum[:, 5, 8 * t:8 * t + 4], v[:, 56:60], ALU.mult))
                link(dve.tensor_reduce(v[:, 104:105], v[:, 96:100], AX.X, ALU.add))
            dve.tensor_copy(rt[:, 0, 112:116], psum[:, 5, 16:20])
            for w in range(WINDOWS):
                for t in range(NT):
                    dve.tensor_scalar(pick[:, w, t, :], slots, rt[:, t, 104:105], rt[:, t, 56 + w:57 + w],
                                      ALU.is_equal, ALU.mult).then_inc(pick_ready, 1)
            take_gather(0, range(4))
            for t in range(NT):
                v = rt[:, t, :]
                e8, top, idx, sc = v[:, 32:40], v[:, 40:48], v[:, 48:56].bitcast(U32), v[:, 64:80]
                hot, two = v[:, 56:60], v[:, 84:92]
                link(dve.tensor_scalar(e8[:, 0:4], v[:, 4:8], hot[:, 0:1], None, ALU.mult))
                for g in range(1, 4):
                    link(dve.scalar_tensor_tensor(e8[:, 0:4], v[:, 4 + 4 * g:8 + 4 * g], hot[:, g:g + 1], e8[:, 0:4], ALU.mult, ALU.add))
                link(dve.max(top, e8))
                link(dve.max_index(idx, top, e8))
                dve.tensor_tensor(sc[:, 2:3], top[:, 1:2], top[:, 0:1], ALU.subtract).then_inc(route_in, 1)
                link(dve.tensor_copy(sc[:, 4:6], idx[:, 0:2]))
                dve.wait_ge(route_exp, NT + t + 1)
                link(dve.tensor_scalar(sc[:, 6:7], sc[:, 3:4], 1.0, None, ALU.add))
                link(dve.tensor_tensor(sc[:, 6:7], sc[:, 6:7], sc[:, 1:2], ALU.mult))
                link(dve.reciprocal(sc[:, 7:8], sc[:, 6:7]))
                link(dve.tensor_tensor(sc[:, 7:8], sc[:, 7:8], rstd[:, NORM_AT["moe"], t:t + 1], ALU.mult))
                link(dve.tensor_tensor(sc[:, 8:9], sc[:, 7:8], sc[:, 3:4], ALU.mult))
                dve.tensor_scalar(two[:, 0:4], iota4, sc[:, 4:5], sc[:, 7:8], ALU.is_equal, ALU.mult)
                link(dve.tensor_scalar(two[:, 4:8], iota4, sc[:, 5:6], sc[:, 8:9], ALU.is_equal, ALU.mult))
                link(dve.tensor_tensor(two[:, 0:4], two[:, 0:4], two[:, 4:8], ALU.add))
                for g in range(4):
                    dve.tensor_scalar(gates[:, t, 4 * g:4 * g + 4], two[:, 0:4], hot[:, g:g + 1], None, ALU.mult)
                link(dve.tensor_copy(gates[:, t, 16:17], rstd[:, NORM_AT["moe"], t:t + 1]))
            dve.sem_inc(gates_ready, 1)
            experts()
            i, i_next = NORM_AT["final"], NORM_AT["ffn1_0"]
            dve.wait_ge(gain_landed[i % 2], 16 * (i // 2 + 1))
            dve.wait_ge(gain_landed[i_next % 2], 16 * (i_next // 2 + 1))
            for t in range(NT):
                dve.wait_ge(rstd_ready, NT * i + t + 1)
                for half in range(2):
                    c = slice(512 * half, 512 * half + 512)
                    ins = dve.scalar_tensor_tensor(x[:, t, c], x[:, t, c], rstd[:, i, t:t + 1], gain[:, i % 2, c], ALU.mult, ALU.mult)
                    if half == 0:
                        link(ins)
                    else:
                        resid[0] += 1
                        ins.then_inc(resid_done, 1)
                        dve.wait_ge(resid_done, resid[0])
                    dve.tensor_tensor(y[:, t, c], x[:, t, c], gain[:, i_next % 2, c], ALU.mult).then_inc(turn_src, 1)
                    if t * 2 + half in (1, 2):
                        take_turn("ffn1_0", t * 2 + half - 1)
            dve.wait_ge(turn_src, TURN_BASE["ffn1_0"] + 4)
            dve.sem_inc(gain_used, 2)
            take_turn("ffn1_0", 2)
            take_turn("ffn1_0", 3)
            swiglu("ffn1_0")
            residual("ffn1_0", "diff", "ffn1_0_p")
            for name in PROJ[9:13]:
                take_projection(name)
            dve.wait_ge(diffw_landed, 32)
            for k in range(2):
                last = dve.tensor_tensor_reduce(ropet[:, 64 * k:64 * k + 64], lamv[:, 128 * k:128 * k + 64], lamv[:, 128 * k + 64:128 * k + 128],
                                                1.0, 0.0, ALU.mult, ALU.add, lams[:, k:k + 1])
            last.then_inc(lam_sum, 1)
            dve.wait_ge(lam_exp, 1)
            link(dve.tensor_tensor(lams[:, 4:5], lams[:, 2:3], lams[:, 3:4], ALU.subtract))
            link(dve.tensor_scalar(lams[:, 5:6], lams[:, 4:5], 0.2, -1.0, ALU.add, ALU.mult))
            dve.wait_ge(proj_out0, PROJ_AT["dk1"] + 1)
            dve.wait_ge(proj_out1, PROJ_AT["dk1"] + 1)
            for turn_, z in enumerate((q2, y)):
                if turn_:
                    dve.wait_ge(rope_done, 1)
                z4 = z.rearrange("p t (m c) -> p t m c", m=16)
                x1, x2 = z4[:, :, :, 0:8], z4[:, :, :, 8:16]
                cos, sin = (rope[:, :, k, :].unsqueeze(2).to_broadcast([P, NT, 16, 8]) for k in range(2))
                tt = [ropet[:, 256 * k:256 * k + 256].rearrange("p (t m c) -> p t m c", t=NT, m=16) for k in range(4)]
                dve.tensor_tensor(tt[0], x1, cos, ALU.mult)
                dve.tensor_tensor(tt[1], x2, sin, ALU.mult)
                dve.tensor_tensor(tt[2], x2, cos, ALU.mult)
                link(dve.tensor_tensor(tt[3], x1, sin, ALU.mult))
                link(dve.tensor_tensor(x1, tt[0], tt[1], ALU.subtract))
                dve.tensor_tensor(x2, tt[2], tt[3], ALU.add).then_inc(rope_done, 1)
            for name in PROJ[13:15]:
                take_projection(name)
            take_k("diff", region(4608, 2048))
            attention("diff", probs_2, probsT_2, take_diff)
            dve.wait_ge(heads_normed, 3)
            dve.sem_inc(turn_src, 2)
            head_norm("diff", y[:, 1, 256:1024].rearrange("p (h d) -> p h d", h=6), region(10240, 768).rearrange("p (h d) -> p h d", h=6),
                      subln.unsqueeze(1).to_broadcast([P, 6, P]), "diff_y").then_inc(dve_chain, 1)
            chained[0] += 1
            dve.wait_ge(dve_chain, chained[0])
            dve.wait_ge(heads_normed, 4)
            dve.sem_inc(turn_src, 2)
            take_turn("diff_y", 2)
            take_turn("diff_y", 3)
            residual("diff_out", "ffn2_0", "diff_p")
            swiglu("ffn2_0")
            residual("ffn2_0", "ffn1_1", "ffn2_0_p")
            swiglu("ffn1_1")
            residual("ffn1_1", "na", "ffn1_1_p")
            dve.wait_ge(nab_landed, 16)
            dve.wait_ge(namask_landed, 16)
            for name in PROJ[15:21]:
                take_projection(name)
                if name in PROJ[15:19]:
                    k = PROJ[15:19].index(name)
                    v = nab[:, 4 * k:4 * k + 4, :, :]
                    dve.tensor_tensor(v, v, namask.unsqueeze(1).unsqueeze(1).to_broadcast([P, 4, 6, 64]), ALU.add).then_inc(nab_ready, 1)
            dve.wait_ge(nab_ready, 4)
            take_k("na", region(4608, 2048))
            attention("na", probs_2, probsT_2, weighted("na", lambda g: y[:, g // 2, (g % 2) * 512:(g % 2) * 512 + 512]))
            dve.sem_inc(turn_src, 4)
            take_turns("na_y")
            residual("na_out", "ffn2_1", "na_p")
            swiglu("ffn2_1")
            residual("ffn2_1", None, "ffn2_1_p")

        @block.gpsimd
        def _(pool):
            ahead, chained = [0], [0]

            def lo(n, it=None):
                pool.wait_ge(hi_done, shifted(n + 1, it, 6))
                pool.tensor_tensor(w_lo[:, n % SPLIT, LO_V:CHUNK], raw[:, n % RAW, LO_V:CHUNK],
                                   w_hi[:, n % SPLIT, LO_V:CHUNK].bitcast(F32), ALU.subtract).then_inc(lo_p_done, 1)

            def split_through(n):
                while ahead[0] <= min(n, CHUNKS - 1):
                    lo(ahead[0])
                    ahead[0] += 1

            def link(ins):
                chained[0] += 1
                ins.then_inc(pool_chain, 1)
                pool.wait_ge(pool_chain, chained[0])

            def inverse_rms(name):
                i, f = NORM_AT[name], NORM_FACTOR.get(name, 1.0) ** -2
                for t in range(NT):
                    if NT * i + t:
                        pool.wait_ge(rstd_ready, NT * i + t)
                    pool.wait_ge(squared, NT * i + t + 1)
                    link(pool.tensor_scalar(vtmp[:, 0:1], sums[:, i, t:t + 1], f / D, f * EPS, ALU.mult, ALU.add))
                    pool.tensor_tensor(rstd[:, i, t:t + 1], vtmp[:, 0:1], neghalf[:, 0:1], ALU.pow).then_inc(rstd_ready, 1)
                if name in SCALED:
                    pool.wait_ge(rstd_ready, NT * (i + 1))
                    pool.tensor_scalar(rstd_q[:, SCALED.index(name), :], rstd[:, i, :], SCORE_SCALE[name], None,
                                       ALU.mult).then_inc(rstdq_ready, 1)

            def inverse_head_rms(name, heads, d, factor=1.0):
                k, f = HEADNORMS.index(name), factor ** -2
                pool.wait_ge(head_sums, k + 1)
                link(pool.tensor_scalar(htmp[:, 0:heads], hsum[:, 0:heads], f / d, f * EPS, ALU.mult, ALU.add))
                pool.tensor_tensor(hrstd[:, 0:heads], htmp[:, 0:heads], neghalf[:, 0:heads], ALU.pow).then_inc(head_rstd, 1)

            def head_norm(view, tmp, gain_, more=None, factor=1.0):
                (heads, d), f = view.shape[1:], factor ** -2
                sums_, r_ = pool_heads[:, 0:heads], pool_heads[:, 8:8 + heads]
                link(pool.tensor_tensor(tmp, view, view, ALU.mult))
                n = d
                while n > 1:
                    n //= 2
                    link(pool.tensor_tensor(tmp[:, :, 0:n], tmp[:, :, 0:n], tmp[:, :, n:2 * n], ALU.add))
                link(pool.tensor_scalar(sums_.unsqueeze(2), tmp[:, :, 0:1], f / d, f * EPS, ALU.mult, ALU.add))
                link(pool.tensor_tensor(r_, sums_, neghalf[:, 0:heads], ALU.pow))
                link(pool.tensor_tensor(view, view, r_.unsqueeze(2).to_broadcast([P, heads, d]), ALU.mult))
                if more is not None:
                    link(pool.tensor_tensor(view, view, more, ALU.mult))
                link(pool.tensor_tensor(view, view, gain_, ALU.mult))

            def swiglu(name):
                base, groups = START[name], FFN[name]
                peel = name == "ffn2_1"

                def splits(n, it=None):
                    for k in range(2, 8 if it is not None else 5):
                        if n + k < CHUNKS:
                            lo(n + k, it)

                split_through(base + 3)
                with pool.Fori(0, (groups - 1) // 2 - peel) as it:
                    splits(base + 2, it)
                for g in range((groups - 1) // 2 * 2 - 2 * peel, groups - 1):
                    splits(base + 2 + 3 * g)
                ahead[0] = base + 3 * groups + 1

            pool.memset(zeros[:, :], 0.0).then_inc(zeros_ready, 1)
            pool.wait_ge(const_landed, 16)
            split_through(2)
            inverse_rms("mix")
            pool.memset(fb[:, 1024:2048], 0.0).then_inc(at_zero, 1)
            split_through(START["mix_in"] + 13)
            pool.wait_ge(gla_o_out, 1)
            for t in range(NT):
                head_norm(y[:, t, 512:1024].rearrange("p (h d) -> p h d", h=4), fb[:, 0:512].rearrange("p (h d) -> p h d", h=4),
                          gla_gain.rearrange("p (h d) -> p h d", h=4), gg[:, t, :].rearrange("p (h d) -> p h d", h=4))
            pool.sem_inc(heads_normed, 1)
            i = NORM_AT["mem"]
            inverse_rms("mem")
            pool.wait_ge(mem_landed, 16)
            pool.wait_ge(gain_landed[i % 2], 16 * (i // 2 + 1))
            for t in range(NT):
                for half in range(2):
                    c = slice(512 * half, 512 * half + 512)
                    pool.tensor_tensor(mem[:, t, c], mem[:, t, c], gain[:, i % 2, c], ALU.mult).then_inc(turn_src, 1)
            pool.wait_ge(turn_src, TURN_BASE["mem"] + 4)
            pool.sem_inc(gain_used, 1)
            pool.wait_ge(pv_taken, GROUP0["fox"] + 1)
            head_norm(y[:, 0, 0:512].rearrange("p (h d) -> p h d", h=8), fb[:, 1024:1536].rearrange("p (h d) -> p h d", h=8),
                      fox_gain.rearrange("p (h d) -> p h d", h=8))
            pool.sem_inc(heads_normed, 1)
            inverse_head_rms("fox", 8, 64)
            split_through(START["mix_out"] + 5)
            inverse_rms("cross")
            split_through(START["cross_out"] + 3)
            inverse_rms("moe")
            swiglu("moe")
            split_through(START["moe"] + 3 * MOE_GROUPS + 1)
            inverse_rms("final")
            inverse_rms("ffn1_0")
            swiglu("ffn1_0")
            split_through(START["ffn1_0"] + 3 * FF_GROUPS + 1)
            inverse_rms("ffn1_0_p")
            inverse_rms("diff")
            split_through(START["diff_in"] + 13)
            for groups, t, c0, c1 in ((4, 0, 0, 1024), (5, 1, 0, 256)):
                pool.wait_ge(pv_taken, GROUP0["diff"] + groups)
                heads = (c1 - c0) // P
                head_norm(y[:, t, c0:c1].rearrange("p (h d) -> p h d", h=heads),
                          region(9216, c1 - c0).rearrange("p (h d) -> p h d", h=heads),
                          subln.unsqueeze(1).to_broadcast([P, heads, P]), None, 1.0 - (0.8 - 0.6))
                pool.sem_inc(heads_normed, 1)
            inverse_head_rms("diff", 6, P, 1.0 - (0.8 - 0.6))
            split_through(START["diff_out"] + 5)
            inverse_rms("diff_p")
            inverse_rms("ffn2_0")
            swiglu("ffn2_0")
            split_through(START["ffn2_0"] + 3 * FF_GROUPS + 1)
            inverse_rms("ffn2_0_p")
            inverse_rms("ffn1_1")
            swiglu("ffn1_1")
            split_through(START["ffn1_1"] + 3 * FF_GROUPS + 1)
            inverse_rms("ffn1_1_p")
            inverse_rms("na")
            split_through(START["na_out"] + 5)
            inverse_rms("na_p")
            inverse_rms("ffn2_1")
            swiglu("ffn2_1")
            inverse_rms("ffn2_1_p")


def toeplitz(rpb):
    j, c, s, k = np.ix_(range(2), range(64), range(6), range(64))
    laid = rpb[0][:, 5 - j + s, np.clip(k - c + 15, 0, 30)]
    return np.ascontiguousarray(laid.transpose(1, 2, 0, 3, 4)).reshape(P, 16 * 6 * 64)


_INS = ["x", "mem", "mem_norm", "mix_norm", "w_in", "b_forget", "w_alpha_up", "b_alpha", "fox_out_gain",
        "gla_out_gain", "w_out", "cross_norm", "w_xq", "w_xk", "w_xv", "w_xo", "moe_norm", "w_router_group",
        "b_router_group", "w_router_expert", "b_router_expert", "w_expert_gate", "w_expert_up",
        "w_expert_down", "final_norm", "norm_g_2", "ffn1_wg_2", "ffn1_wu_2", "ffn1_wd_2", "ffn2_wg_2",
        "ffn2_wu_2", "ffn2_wd_2", "diff_w_in_2", "diff_w_out_2", "diff_lambda_2", "diff_subln_2",
        "na_w_in_2", "na_w_out_2"]


def kernel(**inputs):
    import numpy as _np
    import concourse.bacc as _bacc
    from concourse import mybir as _mybir
    from concourse.bass_utils import run_bass_kernel_spmd as _run

    nc = _bacc.Bacc("TRN2", target_bir_lowering=False, num_devices=1)
    consts, masks = shape_constants()
    arrays = {name: _np.ascontiguousarray(inputs[name]) for name in _INS}
    arrays["consts"], arrays["masks"] = consts, masks
    arrays["na_biases"] = toeplitz(_np.asarray(inputs["na_rpb_2"]))
    aps = {}
    for name, v in arrays.items():
        aps[name] = nc.dram_tensor(name, v.shape, _mybir.dt.from_np(v.dtype), kind="ExternalInput").ap()
    out = nc.dram_tensor("out", (1, S, D), _mybir.dt.float32, kind="ExternalOutput").ap()
    two_blocks(nc, aps, out)
    r = _run(nc, [arrays], core_ids=[0])
    return r.results[0]["out"]
```
